# Optimizing a Trainium2 kernel written in Bass

```python
import jax, jax.numpy as jnp
from jax import lax
import numpy as np

D_MODEL = 1024
BATCH = 1
SEQ = 1024
DEPTH = 1

N_MIXERS = 2
N_META = 16
CHUNK = 64
FRONT_PAD = CHUNK - N_META
MLSTM_HEADS = 4
MLSTM_DQK = 128
MLSTM_DV = 256
GLA_HEADS = 4
GLA_DK = 128
GLA_DV = 256
GLA_GATE_RANK = 16
GLA_TAU = 16.0
N_GROUPS = 4
EXPERTS_PER_GROUP = 8
N_EXPERTS = N_GROUPS * EXPERTS_PER_GROUP
TOP_K = 2
D_EXPERT = 512
MOE_BLOCK = 128
DEEPNORM_ALPHA = (2.0 * DEPTH) ** 0.25
DEEPNORM_BETA = (8.0 * DEPTH) ** -0.25
LN_EPS = 1e-5
NEG = -1e30

kernel_name = "hybrid_mlstm_gla_hier_moe_deepnorm"

def layer_norm(x, g, b):
    xf = x.astype(jnp.float32)
    mu = xf.mean(-1, keepdims=True)
    var = jnp.mean(jnp.square(xf - mu), -1, keepdims=True)
    return ((xf - mu) * lax.rsqrt(var + LN_EPS) * g.astype(jnp.float32) + b.astype(jnp.float32)).astype(x.dtype)

def to_chunks(t, pad_value):
    t = jnp.pad(t, ((0, 0), (FRONT_PAD, 0), (0, 0), (0, 0)), constant_values=pad_value)
    b, lp, h, d = t.shape
    return t.reshape(b, lp // CHUNK, CHUNK, h, d).transpose(1, 0, 3, 2, 4)

def from_chunks(y):
    n, b, h, c, d = y.shape
    return y.transpose(1, 0, 3, 2, 4).reshape(b, n * c, h, d)[:, FRONT_PAD:]

def mlstm_mixer(x, w_in, b_gates, head_norm_w, w_out):
    bsz, length, _ = x.shape
    H, dqk, dv = MLSTM_HEADS, MLSTM_DQK, MLSTM_DV
    qk_w, v_w = H * dqk, H * dv
    proj = x @ w_in
    q = proj[..., :qk_w].reshape(bsz, length, H, dqk).astype(jnp.float32) * (dqk ** -0.5)
    k = proj[..., qk_w:2 * qk_w].reshape(bsz, length, H, dqk).astype(jnp.float32)
    v = proj[..., 2 * qk_w:2 * qk_w + v_w].reshape(bsz, length, H, dv).astype(jnp.float32)
    o_pre = proj[..., 2 * qk_w + v_w:2 * qk_w + 2 * v_w].astype(jnp.float32)
    gates = proj[..., 2 * qk_w + 2 * v_w:].astype(jnp.float32) + b_gates.astype(jnp.float32)
    log_i = gates[..., :H]
    log_f = jax.nn.log_sigmoid(gates[..., H:])
    xs = (to_chunks(q, 0.0), to_chunks(k, 0.0), to_chunks(v, 0.0),
          to_chunks(log_i[..., None], NEG)[..., 0], to_chunks(log_f[..., None], 0.0)[..., 0])
    causal = jnp.tril(jnp.ones((CHUNK, CHUNK), bool))

    def step(carry, inp):
        C, n, m = carry
        qc, kc, vc, li, lf = inp
        b = jnp.cumsum(lf, axis=-1)
        d_mat = jnp.where(causal, b[..., :, None] - b[..., None, :] + li[..., None, :], NEG)
        g = b + m[..., None]
        m_t = jnp.maximum(g, d_mat.max(-1))
        w_intra = jnp.exp(d_mat - m_t[..., None])
        w_inter = jnp.exp(g - m_t)
        s = jnp.einsum('bhtd,bhsd->bhts', qc, kc) * w_intra
        num = jnp.einsum('bhts,bhsv->bhtv', s, vc) + w_inter[..., None] * jnp.einsum('bhtd,bhdv->bhtv', qc, C)
        den = s.sum(-1) + w_inter * jnp.einsum('bhtd,bhd->bht', qc, n)
        h = num / jnp.maximum(jnp.abs(den), jnp.exp(-m_t))[..., None]
        b_last = b[..., -1]
        decay_s = b_last[..., None] - b + li
        m_new = jnp.maximum(b_last + m, decay_s.max(-1))
        w_s = jnp.exp(decay_s - m_new[..., None])
        w_prev = jnp.exp(b_last + m - m_new)
        C_new = w_prev[..., None, None] * C + jnp.einsum('bhs,bhsd,bhsv->bhdv', w_s, kc, vc)
        n_new = w_prev[..., None] * n + jnp.einsum('bhs,bhsd->bhd', w_s, kc)
        return (C_new, n_new, m_new), h

    init = (jnp.zeros((bsz, H, dqk, dv), jnp.float32), jnp.zeros((bsz, H, dqk), jnp.float32),
            jnp.zeros((bsz, H), jnp.float32))
    _, hc = lax.scan(step, init, xs)
    hs = from_chunks(hc)
    mu = hs.mean(-1, keepdims=True)
    var = jnp.mean(jnp.square(hs - mu), -1, keepdims=True)
    hs = ((hs - mu) * lax.rsqrt(var + LN_EPS)).reshape(bsz, length, v_w) * head_norm_w.astype(jnp.float32)
    out = (hs * jax.nn.sigmoid(o_pre)).astype(x.dtype)
    return out @ w_out

def gla_mixer(x, w_in, w_gate_up, b_gate, head_norm_w, w_out):
    bsz, length, _ = x.shape
    H, dk, dv = GLA_HEADS, GLA_DK, GLA_DV
    k_w, v_w = H * dk, H * dv
    proj = x @ w_in
    q = proj[..., :k_w].reshape(bsz, length, H, dk).astype(jnp.float32) * (dk ** -0.5)
    k = proj[..., k_w:2 * k_w].reshape(bsz, length, H, dk).astype(jnp.float32)
    v = proj[..., 2 * k_w:2 * k_w + v_w].reshape(bsz, length, H, dv).astype(jnp.float32)
    r = proj[..., 2 * k_w + v_w:2 * k_w + 2 * v_w].astype(jnp.float32)
    glr = proj[..., 2 * k_w + 2 * v_w:].astype(jnp.float32)
    log_a = jax.nn.log_sigmoid(glr @ w_gate_up.astype(jnp.float32) + b_gate.astype(jnp.float32)) / GLA_TAU
    log_a = log_a.reshape(bsz, length, H, dk)
    xs = (to_chunks(q, 0.0), to_chunks(k, 0.0), to_chunks(v, 0.0), to_chunks(log_a, 0.0))
    causal = jnp.tril(jnp.ones((CHUNK, CHUNK), bool))

    def step(S, inp):
        qc, kc, vc, la = inp
        bc = jnp.cumsum(la, axis=2)
        diff = bc[:, :, :, None, :] - bc[:, :, None, :, :]
        decay = jnp.exp(jnp.where(causal[:, :, None], diff, NEG))
        attn = jnp.einsum('bhtd,bhsd,bhtsd->bhts', qc, kc, decay)
        o = jnp.einsum('bhts,bhsv->bhtv', attn, vc) + jnp.einsum('bhtd,bhdv->bhtv', qc * jnp.exp(bc), S)
        b_last = bc[:, :, -1]
        k_dec = kc * jnp.exp(b_last[:, :, None] - bc)
        S_new = jnp.exp(b_last)[..., None] * S + jnp.einsum('bhsd,bhsv->bhdv', k_dec, vc)
        return S_new, o

    _, oc = lax.scan(step, jnp.zeros((bsz, H, dk, dv), jnp.float32), xs)
    o = from_chunks(oc)
    o = o * lax.rsqrt(jnp.mean(jnp.square(o), -1, keepdims=True) + LN_EPS)
    o = o.reshape(bsz, length, v_w) * head_norm_w.astype(jnp.float32)
    out = (o * jax.nn.silu(r)).astype(x.dtype)
    return out @ w_out

def hier_moe(x, w_group, b_group, w_router, b_router, w_gate, w_up, w_down):
    bsz, length, D = x.shape
    T = bsz * length
    xf = x.reshape(T, D)
    grp_logits = (xf @ w_group).astype(jnp.float32) + b_group.astype(jnp.float32)
    grp_prob = jax.nn.softmax(grp_logits, axis=-1)
    g_top = jnp.argmax(grp_logits, axis=-1).astype(jnp.int32)
    p_g = jnp.take_along_axis(grp_prob, g_top[:, None], axis=1)[:, 0]
    exp_logits = ((xf @ w_router).astype(jnp.float32) + b_router.astype(jnp.float32)).reshape(T, N_GROUPS, EXPERTS_PER_GROUP)
    idx = jnp.broadcast_to(g_top[:, None, None], (T, 1, EXPERTS_PER_GROUP))
    within = jnp.take_along_axis(exp_logits, idx, axis=1)[:, 0]
    top_vals, top_idx = lax.top_k(within, TOP_K)
    weights = p_g[:, None] * jax.nn.softmax(top_vals, axis=-1)
    expert_ids = g_top[:, None] * EXPERTS_PER_GROUP + top_idx.astype(jnp.int32)
    A = T * TOP_K
    flat_e = expert_ids.reshape(A)
    flat_tok = jnp.repeat(jnp.arange(T, dtype=jnp.int32), TOP_K)
    flat_w = weights.reshape(A)
    order = jnp.argsort(flat_e)
    se, stok, sw = flat_e[order], flat_tok[order], flat_w[order]
    counts = jnp.bincount(flat_e, length=N_EXPERTS).astype(jnp.int32)
    starts = jnp.cumsum(counts) - counts
    pcounts = ((counts + MOE_BLOCK - 1) // MOE_BLOCK) * MOE_BLOCK
    pends = jnp.cumsum(pcounts)
    pstarts = pends - pcounts
    dest = pstarts[se] + jnp.arange(A, dtype=jnp.int32) - starts[se]
    n_blocks = (A + MOE_BLOCK - 1) // MOE_BLOCK + N_EXPERTS
    P = n_blocks * MOE_BLOCK
    row_tok = jnp.full((P,), T, jnp.int32).at[dest].set(stok)
    row_w = jnp.zeros((P,), jnp.float32).at[dest].set(sw)
    block_e = jnp.minimum(jnp.searchsorted(pends, jnp.arange(n_blocks, dtype=jnp.int32) * MOE_BLOCK, side='right'),
                          N_EXPERTS - 1).astype(jnp.int32)
    x_pad = jnp.concatenate([xf, jnp.zeros((1, D), xf.dtype)], axis=0)
    xb = x_pad[row_tok].reshape(n_blocks, MOE_BLOCK, D)

    def expert_block(args):
        xblk, e = args
        hdn = jax.nn.silu(xblk @ w_gate[e]) * (xblk @ w_up[e])
        return hdn @ w_down[e]

    yb = lax.map(expert_block, (xb, block_e)).reshape(P, D)
    out = jnp.zeros((T + 1, D), yb.dtype).at[row_tok].add(yb * row_w[:, None].astype(yb.dtype))
    return out[:T].reshape(bsz, length, D)

def _normal(key, shape, scale):
    return jax.random.normal(key, shape, jnp.float32) * scale

def _moe_params(keys):
    D, F = D_MODEL, D_EXPERT
    return (_normal(next(keys), (D, N_GROUPS), D ** -0.5),
            _normal(next(keys), (N_GROUPS,), 0.01),
            _normal(next(keys), (D, N_EXPERTS), D ** -0.5),
            _normal(next(keys), (N_EXPERTS,), 0.01),
            _normal(next(keys), (N_EXPERTS, D, F), D ** -0.5),
            _normal(next(keys), (N_EXPERTS, D, F), D ** -0.5),
            _normal(next(keys), (N_EXPERTS, F, D), DEEPNORM_BETA * F ** -0.5))

def _ln_params(keys):
    return (1.0 + _normal(next(keys), (D_MODEL,), 0.02), _normal(next(keys), (D_MODEL,), 0.02))

def setup_inputs(seed: int = 0) -> dict:
    key = jax.random.key(seed)
    keys = iter(jax.random.split(key, 64))
    D = D_MODEL
    x = _normal(next(keys), (BATCH, SEQ, D), 1.0)
    meta_tokens = _normal(next(keys), (N_META, D), 1.0)
    H = MLSTM_HEADS
    qk_w, v_w = H * MLSTM_DQK, H * MLSTM_DV
    l0_w_in = jnp.concatenate([
        _normal(next(keys), (D, 2 * qk_w), D ** -0.5),
        _normal(next(keys), (D, v_w), DEEPNORM_BETA * D ** -0.5),
        _normal(next(keys), (D, v_w), D ** -0.5),
        _normal(next(keys), (D, 2 * H), D ** -0.5)], axis=1)
    l0_b_gates = jnp.concatenate([
        _normal(next(keys), (H,), 0.1),
        jnp.linspace(3.0, 6.0, H, dtype=jnp.float32) + _normal(next(keys), (H,), 0.1)])
    l0_head_norm_w = 1.0 + _normal(next(keys), (v_w,), 0.02)
    l0_w_out = _normal(next(keys), (v_w, D), DEEPNORM_BETA * v_w ** -0.5)
    l0_ln1_g, l0_ln1_b = _ln_params(keys)
    l0_w_group, l0_b_group, l0_w_router, l0_b_router, l0_w_gate, l0_w_up, l0_w_down = _moe_params(keys)
    l0_ln2_g, l0_ln2_b = _ln_params(keys)
    k_w, gv_w = GLA_HEADS * GLA_DK, GLA_HEADS * GLA_DV
    l1_w_in = jnp.concatenate([
        _normal(next(keys), (D, 2 * k_w), D ** -0.5),
        _normal(next(keys), (D, gv_w), DEEPNORM_BETA * D ** -0.5),
        _normal(next(keys), (D, gv_w), D ** -0.5),
        _normal(next(keys), (D, GLA_GATE_RANK), D ** -0.5)], axis=1)
    l1_w_gate_up = _normal(next(keys), (GLA_GATE_RANK, k_w), GLA_GATE_RANK ** -0.5)
    l1_b_gate = _normal(next(keys), (k_w,), 0.1)
    l1_head_norm_w = 1.0 + _normal(next(keys), (gv_w,), 0.02)
    l1_w_out = _normal(next(keys), (gv_w, D), DEEPNORM_BETA * gv_w ** -0.5)
    l1_ln1_g, l1_ln1_b = _ln_params(keys)
    l1_w_group, l1_b_group, l1_w_router, l1_b_router, l1_w_gate, l1_w_up, l1_w_down = _moe_params(keys)
    l1_ln2_g, l1_ln2_b = _ln_params(keys)
    return {"x": x, "meta_tokens": meta_tokens,
            "l0_w_in": l0_w_in, "l0_b_gates": l0_b_gates, "l0_head_norm_w": l0_head_norm_w, "l0_w_out": l0_w_out,
            "l0_ln1_g": l0_ln1_g, "l0_ln1_b": l0_ln1_b,
            "l0_w_group": l0_w_group, "l0_b_group": l0_b_group, "l0_w_router": l0_w_router, "l0_b_router": l0_b_router,
            "l0_w_gate": l0_w_gate, "l0_w_up": l0_w_up, "l0_w_down": l0_w_down,
            "l0_ln2_g": l0_ln2_g, "l0_ln2_b": l0_ln2_b,
            "l1_w_in": l1_w_in, "l1_w_gate_up": l1_w_gate_up, "l1_b_gate": l1_b_gate, "l1_head_norm_w": l1_head_norm_w,
            "l1_w_out": l1_w_out, "l1_ln1_g": l1_ln1_g, "l1_ln1_b": l1_ln1_b,
            "l1_w_group": l1_w_group, "l1_b_group": l1_b_group, "l1_w_router": l1_w_router, "l1_b_router": l1_b_router,
            "l1_w_gate": l1_w_gate, "l1_w_up": l1_w_up, "l1_w_down": l1_w_down,
            "l1_ln2_g": l1_ln2_g, "l1_ln2_b": l1_ln2_b}

def reference(x, meta_tokens,
              l0_w_in, l0_b_gates, l0_head_norm_w, l0_w_out, l0_ln1_g, l0_ln1_b,
              l0_w_group, l0_b_group, l0_w_router, l0_b_router, l0_w_gate, l0_w_up, l0_w_down,
              l0_ln2_g, l0_ln2_b,
              l1_w_in, l1_w_gate_up, l1_b_gate, l1_head_norm_w, l1_w_out, l1_ln1_g, l1_ln1_b,
              l1_w_group, l1_b_group, l1_w_router, l1_b_router, l1_w_gate, l1_w_up, l1_w_down,
              l1_ln2_g, l1_ln2_b):
    bsz = x.shape[0]
    meta = jnp.broadcast_to(meta_tokens.astype(x.dtype)[None], (bsz, N_META, D_MODEL))
    h = jnp.concatenate([meta, x], axis=1)
    mixers = (mlstm_mixer, gla_mixer)
    mixer_params = ((l0_w_in, l0_b_gates, l0_head_norm_w, l0_w_out),
                    (l1_w_in, l1_w_gate_up, l1_b_gate, l1_head_norm_w, l1_w_out))
    ln1 = ((l0_ln1_g, l0_ln1_b), (l1_ln1_g, l1_ln1_b))
    moe_params = ((l0_w_group, l0_b_group, l0_w_router, l0_b_router, l0_w_gate, l0_w_up, l0_w_down),
                  (l1_w_group, l1_b_group, l1_w_router, l1_b_router, l1_w_gate, l1_w_up, l1_w_down))
    ln2 = ((l0_ln2_g, l0_ln2_b), (l1_ln2_g, l1_ln2_b))
    for i in range(DEPTH):
        y = mixers[i % N_MIXERS](h, *mixer_params[i])
        h = layer_norm(DEEPNORM_ALPHA * h + y, *ln1[i])
        y = hier_moe(h, *moe_params[i])
        h = layer_norm(DEEPNORM_ALPHA * h + y, *ln2[i])
    return h[:, N_META:]


_drawn_inputs = setup_inputs


def setup_inputs(seed=0):
    import zlib

    import numpy as np

    out = dict(_drawn_inputs(seed))
    spreads = {}
    factors = {'l0_head_norm_w': 6.249,
     'l0_b_group': 26.765,
     'l0_b_router': 21.588,
     'l0_ln2_g': 8.06,
     'l0_ln2_b': 8.367}
    for name, (base, spread) in spreads.items():
        noise = np.random.default_rng([zlib.crc32(name.encode()), seed]).standard_normal(out[name].shape)
        drawn = base * np.exp(spread * noise) if base else spread * noise
        out[name] = __import__('jax').numpy.asarray(drawn.astype(out[name].dtype))
    for name, factor in factors.items():
        out[name] = (out[name] * factor).astype(out[name].dtype)
    return out
```

```python
import concourse.bass as bass
from concourse import mybir

F32 = mybir.dt.float32
F32R = mybir.dt.float32r
BF16 = mybir.dt.bfloat16
I32 = mybir.dt.int32
U32 = mybir.dt.uint32
ALU = mybir.AluOpType
ACT = mybir.ActivationFunctionType
AX = mybir.AxisListType.X

P = 128
D = 1024
KC = D // P
NMETA = 16
T = 1040
L = 116
NT = 9
TP = L * NT
H = 4
DQ = 128
DV = 256
QSCALE = DQ ** -0.5
ALPHA = 2.0 ** 0.25
EPS = 1e-5
NEG = -1e30
GROUPS = 4
PER_GROUP = 8
NE = 32
FE = 512
FC = FE // P
PIECE = 4096
EXTRA = 16
ITEMS = NE + EXTRA
OUT_ROWS = T - NMETA
NF = OUT_ROWS // P


def wait(eng, sem, value):
    if isinstance(value, int) and value <= 0:
        return
    eng.wait_ge(sem, value)


def rows_of(eng, c):
    if isinstance(c, int):
        return slice(c * L, c * L + L)
    return bass.ds(eng.snap(c * L), L)


def build(nc, hcat, w_in, b_gates, head_norm_w, w_out, ln1_g, ln1_b, w_group, b_group, w_router,
          b_router, w_gate, w_up, w_down, ln2_g, ln2_b, out):
    dma_ok = nc.allow_non_contiguous_dma(reason="small parameter vectors and gate columns")
    dma_ok.__enter__()

    proj = nc.dram_tensor("proj", (TP, 3072), F32).ap()
    h1_dram = nc.dram_tensor("h1_rows", (TP, D), F32).ap()
    ys = nc.dram_tensor("expert_rows", (2 * T, D), F32).ap()
    wts_dram = nc.dram_tensor("pair_weights", (TP, 2), F32).ap()

    base = (nc.sbuf_base + 63) // 64 * 64
    cursor = [base]

    def at(name, shape, dt=F32):
        n = 1
        for s in shape[1:]:
            n *= s
        t = nc.alloc_sbuf_tensor_at(name, list(shape), dt, offset=cursor[0])
        cursor[0] += (n * (2 if dt == BF16 else 4) + 31) // 32 * 32
        assert cursor[0] <= nc.sbuf_usable_end, (name, cursor[0])
        return t

    stream_base = cursor[0]
    raw = [at(f"raw{s}", [P, PIECE]) for s in range(3)]
    whi = [at(f"whi{s}", [P, PIECE], F32R) for s in range(2)]
    wlo = [at(f"wlo{s}", [P, PIECE], F32R) for s in range(2)]
    stream_end = cursor[0]
    ident = at("ident", [P, P])
    identb = at("identb", [P, L], BF16)
    maskb = at("maskb", [P, L], BF16)
    upto = at("upto", [P, L])
    beforeb = at("beforeb", [P, L], BF16)
    onesb = at("onesb", [P, P], BF16)
    ones = at("ones", [P, 2])
    selneg = at("selneg", [H, H, P])
    selpos = at("selpos", [H, H, P])
    hnw = at("hnw", [P, KC])
    wg_raw = at("wg_raw", [P, KC, 2 * H])
    wg_hi = at("wg_hi", [P, KC, 2 * H], F32R)
    wg_lo = at("wg_lo", [P, KC, 2 * H], F32R)
    bg = at("bg", [P, 2 * H])
    gts = at("gts", [P, NT, 2 * H])
    ga = at("ga", [P, NT, H])
    gb = at("gb", [P, NT, H])
    glf = at("glf", [P, NT, H])
    gtmp = at("gtmp", [P, NT, H])
    gcm = at("gcm", [P, NT, H])
    gmc = at("gmc", [P, H, 2 * NT])
    garg = at("garg", [P, 3, NT, H])
    gexp = at("gexp", [P, 3, NT, H])
    warg = at("warg", [P, NT, H])
    wprev = at("wprev", [P, NT, H])
    bl = at("bl", [H, NT])
    mcar = at("mcar", [H, NT + 1])
    mcl = at("mcl", [H, 2 * NT])
    cm = at("cm", [H, NT, L])
    lg = at("lg", [P, NT, GROUPS + NE])
    tokrow = at("tokrow", [P, ITEMS], I32)
    dstrow = at("dstrow", [P, ITEMS], I32)
    eidx = at("eidx", [1, ITEMS], I32)
    npm1 = at("npm1", [1, 2], I32)
    wts = at("wts", [P, NT, 2])
    wts2 = at("wts2", [P, NF, 2])
    region = cursor[0]

    xhi = at("xhi", [P, KC, TP], F32R)
    xlo = at("xlo", [P, KC, TP], F32R)
    xt_at = cursor[0]
    xt = [at(f"xt{i}", [P, D]) for i in range(2)]
    stage = [at(f"stage{i}", [P, 512]) for i in range(3)]
    cursor[0] = xt_at
    at_ = at("aT", [H, NT, L])

    cursor[0] = region
    qk = at("qk", [P, 2, H, DQ])
    vext = at("vext", [P, H, DV + 1])
    osig = at("osig", [P, H, DV])
    hres = at("hres", [P, D])
    qs = at("qs", [P, H, DQ])
    ks = at("ks", [P, H, DQ])
    qT = at("qT", [P, H * L])
    qsT = at("qsT", [P, H * L])
    kT = at("kT", [P, H * L])
    ew = at("ew", [P, H * L])
    sw = at("sw", [P, H * L])
    num = at("num", [P, H, DV + 1])
    cst = at("cst", [P, H, DV + 1])
    gt = at("gt", [P, H, DV])
    gated = at("gated", [P, H, DV])
    ohi = at("ohi", [P, KC, L], F32R)
    olo = at("olo", [P, KC, L], F32R)
    z1 = at("z1", [P, D])
    h1t = at("h1t", [P, D])
    h1T = at("h1T", [P, KC, L])
    g1 = at("g1", [P, D])
    b1 = at("b1", [P, D])
    wgr = at("wgr", [P, KC, GROUPS + NE])
    bgr = at("bgr", [P, GROUPS + NE])
    bst = at("bst", [P, H, 6])
    bmv = at("bmv", [P, H, 2])
    ep = at("ep", [P, 8, H])
    lst = at("lst", [P, 2, 6])
    lmv = at("lmv", [P, 4])

    cursor[0] = region
    route_base = cursor[0]
    whi.append(at("whi2", [P, PIECE], F32R))
    wlo.append(at("wlo2", [P, PIECE], F32R))
    xg = [at(f"xg{i}", [P, D]) for i in range(2)]
    xghi = [at(f"xghi{i}", [P, KC, P], F32R) for i in range(2)]
    xglo = [at(f"xglo{i}", [P, KC, P], F32R) for i in range(2)]
    sg = at("sg", [P, FE])
    gu = at("gu", [P, FE])
    ghi = at("ghi", [P, FC, P], F32R)
    glo = at("glo", [P, FC, P], F32R)
    yt = [at(f"yt{i}", [P, D]) for i in range(2)]
    tix = [at(f"tix{i}", [P, 1], I32) for i in range(2)]
    dix = [at(f"dix{i}", [P, 1], I32) for i in range(2)]

    cursor[0] = route_base
    KN = 2 * NT
    r_iota = at("r_iota", [P, P])
    r_eq4 = at("r_eq4", [P, NT, GROUPS])
    r_oh4 = at("r_oh4", [P, NT, GROUPS])
    r_g4 = at("r_g4", [P, NT, GROUPS])
    r_prod = at("r_prod", [P, NT, GROUPS, PER_GROUP])
    r_in = at("r_in", [P, NT, PER_GROUP])
    r_t8 = at("r_t8", [P, NT, PER_GROUP])
    r_oh8 = at("r_oh8", [P, 2, NT, PER_GROUP])
    r_s = at("r_s", [P, 16, NT])
    r_kn = at("r_kn", [P, 10, KN])
    r_oh = at("r_oh", [P, KN, NE])
    r_pr = at("r_pr", [P, KN, NE])
    r_rk = at("r_rk", [P, NT, NE])
    r_cnt = at("r_cnt", [P, NE])
    r_ex8 = at("r_ex8", [P, NE, 8])
    r_ex = at("r_ex", [P, 4, NE])
    r_c8 = at("r_c8", [P, KN, 8])
    r_thr = at("r_thr", [P, 8])
    r_a = at("r_a", [P, NT + 1, NE], BF16)
    r_acum = at("r_acum", [P, NT + 1, NE], BF16)
    r_ohr = at("r_ohr", [P, KN, P])
    r_rhs = at("r_rhs", [P, KN, ITEMS])
    r_v = at("r_v", [P, 2, ITEMS])
    r_e = at("r_e", [1, 3, ITEMS])
    r_cmp = at("r_cmp", [1, EXTRA, NE])
    assert cursor[0] <= route_base + 2 * PIECE * 4 + 2 * D * 4

    cursor[0] = stream_base
    yy = [at(f"yy{i}", [P, 2, D]) for i in range(2)]
    hh = [at(f"hh{i}", [P, D]) for i in range(2)]
    zz = [at(f"zz{i}", [P, D]) for i in range(2)]
    zn = [at(f"zn{i}", [P, D]) for i in range(2)]
    g2 = at("g2", [P, D])
    b2 = at("b2", [P, D])
    fst = at("fst", [P, 2, 6])
    fmv = at("fmv", [P, 4])
    assert cursor[0] <= stream_end

    ps = [nc.alloc_psum_tensor(f"bank{i}", [P, 512], F32) for i in range(8)]

    S = {}

    def sem(name):
        if name not in S:
            S[name] = nc.alloc_semaphore(name)
        return S[name]

    raw_landed = [sem(f"raw_landed{s}") for s in range(3)]
    xt_landed = [sem(f"xt_landed{s}") for s in range(2)]
    gathered = [sem(f"gathered{s}") for s in range(2)]
    scattered = [sem(f"scattered{s}") for s in range(2)]
    y_landed = [sem(f"y_landed{s}") for s in range(2)]
    out_stored = [sem(f"out_stored{s}") for s in range(2)]

    names = """params consts xT_mm x_hi x_lo gate_mm gate_l b_mm a_rows aT_mm m_rows mb_mm
        gate_exp hi_done lo_done blk_mm bank_free stored stage_free ones_ready sp_passed pool_passed
        qk_in v_in o_in h_in qs_done t_mm t_cp e_mm s_mm ew_done sw_done n_mm num_done u_mm
        c_done gt_done gated_done ot_mm o_hi o_lo y_mm z_done ln_done h1_done h1_stored ht_mm
        ht_cp lg_mm lg_done
        r_exp r_arg r_hot rk_mm r_rhs_done v_mm routed wts_stored wts_in
        index_ready xgT_mm xg_hi xg_lo g_mm silu_done u2_mm gu_done guT_mm g_hi g_lo y2_mm y_cp
        ln2_in y0_done fsum_done fnorm_done f_out_done""".split()
    N = {n: sem(n) for n in names}

    def piece_src(g):
        w, c = (w_in, g) if g < 6 else (w_out, g - 6)
        return w[:, c * 512:(c + 1) * 512].rearrange("(p k) n -> p k n", k=KC)

    def landed_count(g):
        return 16 * (g // 3 + 1)

    gate_w = w_gate.rearrange("e (p k) n -> e p (k n)", k=KC)
    up_w = w_up.rearrange("e (p k) n -> e p (k n)", k=KC)
    down_w = w_down.rearrange("e (p k) n -> e p (k n)", k=FC)
    G0 = 8

    def rows_load(eng, dst, src, s):
        eng.dma_start(dst[0:112], src[0:112]).then_inc(s, 16)
        eng.dma_start(dst[112:L], src[112:L]).then_inc(s, 16)

    block = nc.Block()
    block.__enter__()

    @block.sync
    def _(sp):
        def load_piece(g):
            wait(sp, N["lo_done"], g - 2)
            sp.dma_start(raw[g % 3][:].rearrange("p (k n) -> p k n", k=KC), piece_src(g)).then_inc(raw_landed[g % 3], 16)

        def load_expert(j, e, k):
            g_slot = (G0 + k) % 3
            wait(sp, N["lo_done"], j * 3 + (G0 + k - 2))
            src = (gate_w, up_w, down_w)[k]
            sp.dma_start(raw[g_slot][:], src[e, :, :] if isinstance(e, int) else src[bass.ds(e, 1), :, :].rearrange("e p n -> p (e n)")).then_inc(raw_landed[g_slot], 16)

        def load_x(n):
            wait(sp, N["xT_mm"], 2 * (n - 1))
            sp.dma_start(xt[n % 2][0:112, :], hcat[n * L:n * L + 112, :]).then_inc(xt_landed[n % 2], 16)
            sp.dma_start(xt[n % 2][112:L, :], hcat[n * L + 112:(n + 1) * L, :]).then_inc(xt_landed[n % 2], 16)

        load_x(0)
        load_x(1)
        load_piece(0)
        vec = lambda v, n: v.rearrange("(a n) -> a n", a=1).to_broadcast([n, v.shape[0]])
        sp.dma_start(wg_raw[:], w_in[:, 3072:3072 + 2 * H].rearrange("(p k) n -> p k n", k=KC)).then_inc(N["params"], 16)
        sp.dma_start(bg[:], vec(b_gates, P)).then_inc(N["params"], 16)
        sp.dma_start(hnw[:], head_norm_w.rearrange("(p k) -> p k", k=KC)).then_inc(N["params"], 16)
        for n in range(2, NT):
            load_x(n)
            if n < 4:
                load_piece(n - 1)
        for g in range(3, 8):
            load_piece(g)
        for k in range(3):
            load_expert(0, 0, k)

        sp.wait_ge(N["stored"], 16 * 6 * NT)
        sp.wait_ge(N["gate_exp"], 1)
        sp.dma_start(g1[:], vec(ln1_g, P)).then_inc(N["params"], 16)
        sp.dma_start(b1[:], vec(ln1_b, P)).then_inc(N["params"], 16)
        sp.dma_start(wgr[:, :, 0:GROUPS], w_group.rearrange("(p k) n -> p k n", k=KC)).then_inc(N["params"], 16)
        sp.dma_start(wgr[:, :, GROUPS:], w_router.rearrange("(p k) n -> p k n", k=KC)).then_inc(N["params"], 16)
        sp.dma_start(bgr[:, 0:GROUPS], vec(b_group, P)).then_inc(N["params"], 16)
        sp.dma_start(bgr[:, GROUPS:], vec(b_router, P)).then_inc(N["params"], 16)

        def load_residual(c):
            rows = rows_of(sp, c)
            wait(sp, N["z_done"], c * 2)
            rows_load(sp, hres[0:L, :], hcat[rows, :], N["h_in"])

        def load_tile(c):
            rows = rows_of(sp, c)
            src = proj[rows, :]
            wait(sp, N["t_mm"], c * 3)
            sp.sem_inc(N["sp_passed"], 1)
            wait(sp, N["qs_done"], c * 2)
            rows_load(sp, qk[0:L].rearrange("p a h d -> p (a h d)"), src[:, 0:1024], N["qk_in"])
            wait(sp, N["u_mm"], c * 4)
            for r0, r1 in ((0, 112), (112, L)):
                sp.dma_start(vext[r0:r1, :, 0:DV], src[r0:r1, 1024:2048].rearrange("p (h d) -> p h d", h=H)).then_inc(N["v_in"], 16)
            if not (isinstance(c, int) and c == 0):
                load_residual(c - 1)
            wait(sp, N["gt_done"], c)
            rows_load(sp, osig[0:L].rearrange("p h d -> p (h d)"), src[:, 2048:3072], N["o_in"])

        load_tile(0)
        with sp.Fori(1, NT) as c:
            load_tile(c)
        load_residual(NT - 1)

        sp.wait_ge(N["routed"], 1)
        pairs_m1 = sp.value_load(npm1[0:1, 0:1], min_val=NE // 2 - 1, max_val=ITEMS // 2 - 1)
        with sp.Fori(0, pairs_m1) as i:
            for par in range(2):
                j = i * 2 + (1 + par)
                e = sp.value_load(eidx[0:1, bass.ds(j, 1)], min_val=0, max_val=NE - 1)
                for k in range(3):
                    load_expert(j, e, k)
        j = pairs_m1 * 2 + 1
        e = sp.value_load(eidx[0:1, bass.ds(j, 1)], min_val=0, max_val=NE - 1)
        for k in range(3):
            load_expert(j, e, k)

        sp.wait_ge(N["y2_mm"], pairs_m1 * 4 + 4)
        sp.dma_start(g2[:], vec(ln2_g, P)).then_inc(N["ln2_in"], 16)
        sp.dma_start(b2[:], vec(ln2_b, P)).then_inc(N["ln2_in"], 16)
        for s in range(2):
            sp.wait_ge(scattered[s], pairs_m1 * 16 + 16)
        for n in range(NF):
            b = n % 2
            t0 = NMETA + n * P
            wait(sp, N["fsum_done"], n - 1)
            sp.dma_start(yy[b][:].rearrange("p a d -> p (a d)"), ys[2 * t0:2 * (t0 + P), :].rearrange("(p a) d -> p (a d)", a=2)).then_inc(y_landed[b], 16)
            sp.dma_start(hh[b][:], h1_dram[t0:t0 + P, :]).then_inc(y_landed[b], 16)

    @block.gpsimd
    def _(pool):
        g = nc.gpsimd
        g.memset(ident[:], 0.0)
        g.memset(upto[:], 1.0)
        g.memset(selpos[:], 0.0)
        g.memset(selneg[:], 0.0)
        g.memset(onesb[:], 1.0)
        g.memset(identb[:], 0.0)
        g.memset(beforeb[:], 1.0)
        g.memset(maskb[:], 0.0)
        pool.drain()
        g.affine_select(out=ident[:], in_=ident[:], compare_op=ALU.not_equal, fill=1.0, base=0, pattern=[[-1, P]], channel_multiplier=1)
        g.affine_select(out=identb[:], in_=identb[:], compare_op=ALU.not_equal, fill=1.0, base=0, pattern=[[-1, L]], channel_multiplier=1)
        g.affine_select(out=upto[:], in_=upto[:], compare_op=ALU.is_ge, fill=0.0, base=0, pattern=[[1, L]], channel_multiplier=-1)
        g.affine_select(out=beforeb[:], in_=beforeb[:], compare_op=ALU.is_gt, fill=0.0, base=0, pattern=[[1, L]], channel_multiplier=-1)
        g.affine_select(out=maskb[:], in_=maskb[:], compare_op=ALU.is_ge, fill=NEG, base=0, pattern=[[1, L]], channel_multiplier=-1)
        g.affine_select(out=selpos[:], in_=selpos[:], compare_op=ALU.not_equal, fill=1.0, base=0, pattern=[[-1, H], [0, P]], channel_multiplier=1)
        g.affine_select(out=selneg[:], in_=selneg[:], compare_op=ALU.not_equal, fill=-1.0, base=0, pattern=[[-1, H], [0, P]], channel_multiplier=1)
        pool.drain()
        g.memset(ones[:], 1.0).then_inc(N["consts"], 1)

        def store_pair(i):
            for pos in range(2 * NT):
                sub, n = divmod(pos, NT)
                s = pos % 3
                wait(pool, N["bank_free"], i * 18 + (6 + pos + 1))
                piece = i * 2 + sub
                cols = slice(piece * 512, piece * 512 + 512) if isinstance(i, int) else bass.ds(piece * 512, 512)
                pool.dma_start(proj[n * L:(n + 1) * L, cols], stage[s][0:L, :]).then_inc(N["stored"], 16)
                wait(pool, N["stored"], i * 288 + 16 * (pos + 1))
                pool.sem_inc(N["stage_free"], 1)

        with pool.Fori(0, 2) as i:
            store_pair(i)
        store_pair(2)

        pool.wait_ge(N["gate_exp"], 1)
        g.memset(vext[:, :, DV:DV + 1], 1.0).then_inc(N["ones_ready"], 1)

        def front(c):
            wait(pool, N["qk_in"], c * 32 + 32)
            wait(pool, N["t_mm"], c * 3)
            wait(pool, N["u_mm"], c * 4)
            cc = bass.ds(c, 1) if not isinstance(c, int) else slice(c, c + 1)
            wint = gexp[0:L, 0, cc, :].rearrange("p n h -> p (n h)").unsqueeze(2).to_broadcast([L, H, DQ])
            wsc = gexp[0:L, 2, cc, :].rearrange("p n h -> p (n h)").unsqueeze(2).to_broadcast([L, H, DQ])
            g.tensor_tensor(qs[0:L], qk[0:L, 0], wint, ALU.mult).then_inc(N["qs_done"], 1)
            g.tensor_tensor(ks[0:L], qk[0:L, 1], wsc, ALU.mult).then_inc(N["qs_done"], 1)

        def back(c):
            rows = rows_of(pool, c)
            wait(pool, N["ln_done"], c + 1)
            wait(pool, N["h1_stored"], c * 16)
            wait(pool, N["ht_mm"], c * 2)
            g.tensor_tensor(h1t[0:L, :], z1[0:L, :], g1[0:L, :], ALU.mult)
            pool.drain()
            g.tensor_tensor(h1t[0:L, :], h1t[0:L, :], b1[0:L, :], ALU.add).then_inc(N["h1_done"], 1)
            wait(pool, N["h1_done"], c + 1)
            pool.dma_start(h1_dram[rows, :], h1t[0:L, :]).then_inc(N["h1_stored"], 16)

        pool.wait_ge(N["params"], 16 * 9)
        front(0)
        front(1)
        back(0)
        with pool.Fori(2, NT) as i:
            front(i)
            back(i - 1)
        back(NT - 1)

        pool.wait_ge(N["lg_done"], NT)
        pool.wait_ge(N["h1_stored"], 16 * NT)
        g.iota(r_iota[:].bitcast(I32), [[1, P]], base=0, channel_multiplier=0)
        g.iota(r_thr[:].bitcast(I32), [[P, 8]], base=P, channel_multiplier=0)
        g.iota(r_kn[0:L, 0, :].rearrange("p (k n) -> p k n", k=2).bitcast(I32), [[1, 2], [2 * L, NT]], base=1, channel_multiplier=2)
        pool.drain()
        g.tensor_copy(r_iota[:], r_iota[:].bitcast(I32))
        g.tensor_copy(r_thr[:], r_thr[:].bitcast(I32))
        g.tensor_copy(r_kn[0:L, 1, :], r_kn[0:L, 0, :].bitcast(I32))
        g.memset(r_kn[0:L, 2, :], 1.0)
        pool.drain()
        g.affine_select(out=r_kn[0:L, 2, :].rearrange("p (k n) -> p k n", k=2), in_=r_kn[0:L, 2, :].rearrange("p (k n) -> p k n", k=2),
                        compare_op=ALU.is_gt, fill=0.0, base=T, pattern=[[0, 2], [-L, NT]], channel_multiplier=-1).then_inc(N["r_arg"], 1)

        pool.wait_ge(N["routed"], 1)
        pool.dma_start(wts_dram.rearrange("(n p) k -> p n k", p=L), wts[0:L, :, :]).then_inc(N["wts_stored"], 16)
        pool.wait_ge(N["wts_stored"], 16)
        pool.dma_start(wts2[:], wts_dram[NMETA:T, :].rearrange("(n p) k -> p n k", p=P)).then_inc(N["wts_in"], 16)

        for b in range(2):
            g.memset(xg[b][:], 0.0)
        pool.drain()

        last_token, last_row = pool.to_reg(T - 1), pool.to_reg(2 * T - 1)

        def gather(j, b):
            jj = slice(j, j + 1) if isinstance(j, int) else bass.ds(j, 1)
            wait(pool, gathered[b], (j - b) * 8)
            g.tensor_copy(tix[b][:], tokrow[:, jj])
            pool.drain()
            wait(pool, N["xgT_mm"], (j - 1) * 2 if not isinstance(j, int) or j > 1 else 0)
            pool.sem_inc(N["pool_passed"], 1)
            g.indirect_dma_start(xg[b][:], None, h1_dram[0:T, :], bass.IndirectOffsetOnAxis(tix[b][:].bitcast(U32), 0),
                                 bounds_check=last_token, oob_is_err=False).then_inc(gathered[b], 16)

        def scatter(j, b):
            jj = slice(j, j + 1) if isinstance(j, int) else bass.ds(j, 1)
            wait(pool, scattered[b], (j - b) * 8)
            g.tensor_copy(dix[b][:], dstrow[:, jj])
            pool.drain()
            wait(pool, N["y_cp"], j * 2 + 2)
            pool.sem_inc(N["pool_passed"], 1)
            g.indirect_dma_start(ys[0:2 * T, :], bass.IndirectOffsetOnAxis(dix[b][:].bitcast(U32), 0), yt[b][:], None,
                                 bounds_check=last_row, oob_is_err=False).then_inc(scattered[b], 16)

        pairs_m1 = pool.value_load(npm1[0:1, 0:1], min_val=NE // 2 - 1, max_val=ITEMS // 2 - 1)
        gather(0, 0)
        gather(1, 1)
        gather(2, 0)
        scatter(0, 0)
        gather(3, 1)
        scatter(1, 1)
        with pool.Fori(1, pairs_m1) as i:
            gather(i * 2 + 2, 0)
            scatter(i * 2, 0)
            gather(i * 2 + 3, 1)
            scatter(i * 2 + 1, 1)
        scatter(pairs_m1 * 2, 0)
        scatter(pairs_m1 * 2 + 1, 1)

        pool.wait_ge(N["ln2_in"], 32)
        for n in range(NF):
            b = n % 2
            pool.wait_ge(N["fnorm_done"], n + 1)
            wait(pool, out_stored[b], 16 * (n // 2))
            g.tensor_tensor(zn[b][:], zz[b][:], g2[:], ALU.mult)
            pool.drain()
            g.tensor_tensor(zn[b][:], zn[b][:], b2[:], ALU.add).then_inc(N["f_out_done"], 1)
            pool.wait_ge(N["f_out_done"], n + 1)
            pool.dma_start(out[n * P:(n + 1) * P, :], zn[b][:]).then_inc(out_stored[b], 16)
        for b in range(2):
            pool.wait_ge(out_stored[b], 16 * (NF // 2))

    @block.scalar
    def _(act):
        a = nc.scalar
        act.sem_inc(N["bank_free"], 6)
        act.sem_inc(N["stage_free"], 3)

        def hi(g):
            wait(act, raw_landed[g % 3], landed_count(g))
            wait(act, N["blk_mm"], NT * (g - 1))
            if g < 6:
                a.activation(whi[g % 2][:], raw[g % 3][:], ACT.Copy).then_inc(N["hi_done"], 1)
            else:
                for k in range(KC):
                    last = a.activation(whi[g % 2][:, k * 512:(k + 1) * 512], raw[g % 3][:, k * 512:(k + 1) * 512], ACT.Copy, scale=hnw[:, k:k + 1])
                last.then_inc(N["hi_done"], 1)

        def x_hi(q):
            n, half = divmod(q, 2)
            act.wait_ge(N["xT_mm"], q + 1)
            a.activation(xhi[:, 4 * half:4 * half + 4, n * L:(n + 1) * L], ps[q % 4][:, 0:4 * L].rearrange("p (k t) -> p k t", k=4), ACT.Copy).then_inc(N["x_hi"], 1)

        act.wait_ge(N["params"], 48)
        a.activation(wg_hi[:], wg_raw[:], ACT.Copy).then_inc(N["gate_l"], 1)
        for q in range(2 * NT):
            x_hi(q)
            if q == 3:
                hi(0)
            if q == 9:
                hi(1)

        def evac_pair(i, func):
            for pos in range(2 * NT):
                sub, n = divmod(pos, NT)
                wait(act, N["blk_mm"], i * 18 + (pos + 1))
                wait(act, N["stage_free"], i * 18 + (pos + 1))
                a.activation(stage[pos % 3][0:L, :], ps[pos % 6][0:L, :], func).then_inc(N["bank_free"], 1)
                if n == NT - 1:
                    yield sub

        act.wait_ge(N["gate_l"], 2)
        a.activation(gtmp[0:L], glf[0:L], ACT.Exp, scale=-1.0).then_inc(N["gate_l"], 1)
        act.wait_ge(N["gate_l"], 4)
        a.activation(gtmp[0:L], gtmp[0:L], ACT.Ln).then_inc(N["gate_l"], 1)

        for i in range(2):
            for sub in evac_pair(i, ACT.Copy):
                hi(2 * i + sub + 2)
        for sub in evac_pair(2, ACT.Sigmoid):
            hi(6 + sub)

        act.wait_ge(N["m_rows"], 2)
        a.activation(gexp[0:L], garg[0:L], ACT.Exp)
        a.activation(wprev[:], warg[:], ACT.Exp).then_inc(N["m_rows"], 1)

        def front(c):
            L3 = lambda t: t[:, 0:H * L]
            wait(act, N["t_mm"], c * 3 + 1)
            wait(act, N["s_mm"], c)
            a.activation(L3(qT), ps[0][:, 0:H * L], ACT.Copy, scale=QSCALE).then_inc(N["t_cp"], 1)
            wait(act, N["t_mm"], c * 3 + 2)
            a.activation(L3(kT), ps[2][:, 0:H * L], ACT.Copy).then_inc(N["t_cp"], 1)
            wait(act, N["t_mm"], c * 3 + 3)
            wait(act, N["n_mm"], c * 4)
            a.activation(L3(qsT), ps[1][:, 0:H * L], ACT.Copy).then_inc(N["t_cp"], 1)
            wait(act, N["e_mm"], c + 1)
            wait(act, N["sw_done"], c)
            for h in range(H):
                bias = ga[0:L, c, h:h + 1] if isinstance(c, int) else ga[0:L, bass.ds(c, 1), h:h + 1].rearrange("p n h -> p (n h)")
                last = a.activation(ew[0:L, h * L:(h + 1) * L], ps[3][0:L, h * L:(h + 1) * L], ACT.Exp, bias=bias)
            last.then_inc(N["ew_done"], 1)
            wait(act, N["gt_done"], c)
            for h in range(H):
                wait(act, N["n_mm"], c * 4 + (h + 1))
                a.activation(num[0:L, h, :], ps[5 + h % 2][0:L, 0:DV + 1], ACT.Copy).then_inc(N["num_done"], 1)

        def tail(c):
            for q in range(2):
                wait(act, N["ht_mm"], c * 2 + (q + 1))
                wait(act, N["lg_mm"], c)
                a.activation(h1T[:, 4 * q:4 * q + 4, :], ps[4 + q][:, 0:4 * L].rearrange("p (k t) -> p k t", k=4), ACT.Copy).then_inc(N["ht_cp"], 1)

        def back_split(c):
            for q in range(2):
                wait(act, N["ot_mm"], c * 2 + (q + 1))
                wait(act, N["y_mm"], c * 2)
                a.activation(ohi[:, 4 * q:4 * q + 4, :], ps[q][:, 0:4 * L].rearrange("p (k t) -> p k t", k=4), ACT.Copy).then_inc(N["o_hi"], 1)

        def scale(c):
            wait(act, N["gt_done"], c + 1)
            wait(act, N["ot_mm"], c * 2)
            for h in range(H):
                last = a.activation(gated[0:L, h, :], gt[0:L, h, :], ACT.Copy, scale=ep[0:L, 5, h:h + 1])
            last.then_inc(N["gated_done"], 1)

        front(0)
        scale(0)
        front(1)
        back_split(0)
        scale(1)
        with act.Fori(2, NT) as i:
            front(i)
            tail(i - 2)
            back_split(i - 1)
            scale(i)
        tail(NT - 2)
        back_split(NT - 1)
        tail(NT - 1)

        def hi_expert(j, k):
            slot = (G0 + k) % 3
            wait(act, raw_landed[slot], j * 16 + 16 * ((G0 + k) // 3 + 1))
            used, per = ((N["g_mm"], 1), (N["u2_mm"], 1), (N["y2_mm"], 2))[k]
            wait(act, used, j * per)
            a.activation(whi[k][:], raw[slot][:], ACT.Copy).then_inc(N["hi_done"], 1)

        def xg_hi(j, b):
            for q in range(2):
                wait(act, N["xgT_mm"], j * 2 + (q + 1))
                if q == 0:
                    wait(act, N["u2_mm"], j - 1)
                a.activation(xghi[b][:, 4 * q:4 * q + 4, :].rearrange("p k t -> p (k t)"), ps[q][:], ACT.Copy).then_inc(N["xg_hi"], 1)

        def mid(j):
            wait(act, N["g_mm"], j + 1)
            wait(act, N["gu_done"], j)
            a.activation(sg[:], ps[2][:], ACT.Silu).then_inc(N["silu_done"], 1)
            wait(act, N["guT_mm"], j + 1)
            wait(act, N["y2_mm"], j * 2)
            a.activation(ghi[:].rearrange("p k t -> p (k t)"), ps[4][:], ACT.Copy).then_inc(N["g_hi"], 1)

        def y_out(j, b):
            wait(act, scattered[b], (j - b) * 8)
            for q in range(2):
                wait(act, N["y2_mm"], j * 2 + (q + 1))
                a.activation(yt[b][:, q * 512:(q + 1) * 512], ps[5 + q][:], ACT.Copy).then_inc(N["y_cp"], 1)

        act.wait_ge(N["y_mm"], 2 * NT)
        hi_expert(0, 0)
        hi_expert(0, 1)
        act.wait_ge(N["r_arg"], 2)
        a.activation(r_g4[0:L], r_g4[0:L], ACT.Exp)
        a.activation(r_s[0:L, 6, :], r_s[0:L, 5, :], ACT.Exp).then_inc(N["r_exp"], 1)
        act.wait_ge(N["routed"], 1)
        hi_expert(0, 2)
        xg_hi(0, 0)
        pairs_m1 = act.value_load(npm1[0:1, 0:1], min_val=NE // 2 - 1, max_val=ITEMS // 2 - 1)

        def item(j, b, last=False):
            if not last:
                hi_expert(j + 1, 0)
                xg_hi(j + 1, 1 - b)
            mid(j)
            if not last:
                hi_expert(j + 1, 1)
            y_out(j, b)
            if not last:
                hi_expert(j + 1, 2)

        item(0, 0)
        item(1, 1)
        with act.Fori(1, pairs_m1) as i:
            item(i * 2, 0)
            item(i * 2 + 1, 1)
        item(pairs_m1 * 2, 0)
        item(pairs_m1 * 2 + 1, 1, last=True)

        for n in range(NF):
            b = n % 2
            act.wait_ge(y_landed[b], 32 * (n // 2 + 1))
            wait(act, N["f_out_done"], n - 1)
            a.activation(zz[b][:], hh[b][:], ACT.Copy, scale=ALPHA).then_inc(N["y0_done"], 1)

    @block.vector
    def _(dve):
        v = nc.vector
        tt, ts, stt = v.tensor_tensor, v.tensor_scalar, v.scalar_tensor_tensor

        def rsqrt(y, x, tmp):
            ts(x, x, EPS, None, ALU.add)
            dve.drain()
            ts(y.bitcast(I32), x.bitcast(I32), 1, None, ALU.logical_shift_right)
            dve.drain()
            ts(y.bitcast(I32), y.bitcast(I32), -1.0, float(0x5F3759DF), ALU.mult, ALU.add)
            dve.drain()
            for _ in range(3):
                tt(tmp, y, y, ALU.mult)
                dve.drain()
                stt(tmp, tmp, -0.5, x, ALU.mult, ALU.mult)
                dve.drain()
                stt(y, tmp, 1.5, y, ALU.add, ALU.mult)
                dve.drain()

        def lo(g):
            wait(dve, N["hi_done"], g + 1)
            if g < 6:
                tt(wlo[g % 2][:], raw[g % 3][:], whi[g % 2][:].bitcast(F32), ALU.subtract).then_inc(N["lo_done"], 1)
            else:
                for k in range(KC):
                    c = slice(k * 512, (k + 1) * 512)
                    last = stt(wlo[g % 2][:, c], raw[g % 3][:, c], hnw[:, k:k + 1], whi[g % 2][:, c].bitcast(F32), ALU.mult, ALU.subtract)
                last.then_inc(N["lo_done"], 1)

        dve.wait_ge(N["gate_l"], 1)
        tt(wg_lo[:], wg_raw[:], wg_hi[:].bitcast(F32), ALU.subtract).then_inc(N["gate_mm"], 1)
        for q in range(2 * NT):
            n, half = divmod(q, 2)
            dve.wait_ge(N["x_hi"], q + 1)
            cols = (slice(None), slice(4 * half, 4 * half + 4), slice(n * L, (n + 1) * L))
            tt(xlo[cols], ps[q % 4][:, 0:4 * L].rearrange("p (k t) -> p k t", k=4), xhi[cols].bitcast(F32), ALU.subtract).then_inc(N["x_lo"], 1)
            if q == 3:
                lo(0)
            if q == 9:
                lo(1)

        dve.wait_ge(N["gate_mm"], 2)
        tt(gts[0:L], ps[6][0:L, 0:NT * 2 * H].rearrange("p (n g) -> p n g", n=NT), bg[0:L].unsqueeze(1).to_broadcast([L, NT, 2 * H]), ALU.add)
        dve.drain()
        stt(glf[0:L], gts[0:L, :, H:2 * H], -1.0, gts[0:L, :, H:2 * H], ALU.mult, ALU.max).then_inc(N["gate_l"], 1)
        dve.wait_ge(N["gate_l"], 3)
        ts(gtmp[0:L], gtmp[0:L], 1.0, None, ALU.add).then_inc(N["gate_l"], 1)
        dve.wait_ge(N["gate_l"], 5)
        stt(glf[0:L], gts[0:L, :, H:2 * H], 0.0, gtmp[0:L], ALU.min, ALU.subtract).then_inc(N["a_rows"], 1)

        for g in range(2, 6):
            lo(g)
        dve.wait_ge(N["b_mm"], 1)
        v.tensor_copy(gb[0:L].rearrange("p n h -> p (n h)"), ps[6][0:L, 0:NT * H])
        dve.drain()
        tt(ga[0:L], gts[0:L, :, 0:H], gb[0:L], ALU.subtract).then_inc(N["a_rows"], 1)
        lo(6)
        dve.wait_ge(N["aT_mm"], 1)
        v.tensor_copy(at_[:, 0:4, :].rearrange("p n t -> p (n t)"), ps[6][0:H, 0:4 * L])
        v.tensor_copy(at_[:, 4:8, :].rearrange("p n t -> p (n t)"), ps[7][0:H, 0:4 * L]).then_inc(N["aT_mm"], 1)
        dve.wait_ge(N["aT_mm"], 3)
        v.tensor_copy(at_[:, 8, :], ps[6][0:H, 0:L])
        v.tensor_copy(bl[:], ps[6][0:H, 480:480 + NT])
        v.memset(mcar[:, 0:1], 0.0)
        dve.drain()
        for n in range(NT):
            v.tensor_tensor_scan(cm[:, n, :], at_[:, n, :], at_[:, n, :], mcar[:, n:n + 1], ALU.max, ALU.max)
            dve.drain()
            tt(mcar[:, n + 1:n + 2], bl[:, n:n + 1], cm[:, n, L - 1:L], ALU.add)
            dve.drain()
        v.tensor_copy(mcl[:, 0:NT], mcar[:, 0:NT])
        v.tensor_copy(mcl[:, NT:2 * NT], cm[:, :, L - 1:L].rearrange("p n o -> p (n o)")).then_inc(N["m_rows"], 1)
        lo(7)
        dve.wait_ge(N["mb_mm"], 1)
        v.tensor_copy(gcm[0:L].rearrange("p n h -> p (n h)"), ps[6][0:L, 0:NT * H])
        v.tensor_copy(gmc[:].rearrange("p h n -> p (h n)"), ps[7][:, 0:H * 2 * NT])
        dve.drain()
        mprev = gmc[:, :, 0:NT].rearrange("p h n -> p n h")
        mlast = gmc[:, :, NT:2 * NT].rearrange("p h n -> p n h")
        tt(garg[0:L, 0], mprev[0:L], gcm[0:L], ALU.subtract)
        stt(garg[0:L, 1], gb[0:L], -1.0, gcm[0:L], ALU.mult, ALU.subtract)
        tt(garg[0:L, 2], ga[0:L], mlast[0:L], ALU.subtract)
        tt(warg[:], mprev, mlast, ALU.subtract).then_inc(N["m_rows"], 1)
        dve.wait_ge(N["m_rows"], 3)
        ts(gexp[0:L, 0], gexp[0:L, 0], QSCALE, None, ALU.mult).then_inc(N["gate_exp"], 1)

        v.memset(cst[:], 0.0).then_inc(N["c_done"], 1)

        def front(c):
            cc = slice(c, c + 1) if isinstance(c, int) else bass.ds(c, 1)
            wait(dve, N["s_mm"], c + 1)
            wait(dve, N["ew_done"], c + 1)
            wait(dve, N["n_mm"], c * 4)
            tt(sw[0:L, :], ps[4][0:L, 0:H * L], ew[0:L, :], ALU.mult).then_inc(N["sw_done"], 1)
            dve.drain()
            for h in range(H):
                wait(dve, N["u_mm"], c * 4 + (h + 1))
                stt(cst[:, h, :], cst[:, h, :], wprev[:, cc, h:h + 1].rearrange("p n h -> p (n h)"), ps[7][:, 0:DV + 1], ALU.mult, ALU.add).then_inc(N["c_done"], 1)

        def tail(c):
            wait(dve, N["lg_mm"], c + 1)
            cc = slice(c, c + 1) if isinstance(c, int) else bass.ds(c, 1)
            tt(lg[0:L, cc, :].rearrange("p n g -> p (n g)"), ps[6][0:L, 0:GROUPS + NE], bgr[0:L, :], ALU.add).then_inc(N["lg_done"], 1)

        def back_split(c):
            for q in range(2):
                wait(dve, N["o_hi"], c * 2 + (q + 1))
                s = slice(4 * q, 4 * q + 4)
                tt(olo[:, s, :], ps[q][:, 0:4 * L].rearrange("p (k t) -> p k t", k=4), ohi[:, s, :].bitcast(F32), ALU.subtract).then_inc(N["o_lo"], 1)

        def head_norm(c):
            cc = slice(c, c + 1) if isinstance(c, int) else bass.ds(c, 1)
            wait(dve, N["num_done"], c * 4 + 4)
            for h in range(H):
                v.bn_stats(bst[0:L, h, :], num[0:L, h, 0:DV])
            den = num[0:L, :, DV:DV + 1].rearrange("p h o -> p (h o)")
            stt(ep[0:L, 0, :], den, -1.0, den, ALU.mult, ALU.max)
            dve.drain()
            for h in range(H):
                v.bn_aggr(bmv[0:L, h, :], bst[0:L, h, :])
            tt(ep[0:L, 1, :], ep[0:L, 0, :], gexp[0:L, 1, cc, :].rearrange("p n h -> p (n h)"), ALU.max)
            dve.drain()
            v.reciprocal(ep[0:L, 2, :], ep[0:L, 1, :])
            dve.drain()
            tt(ep[0:L, 3, :], ep[0:L, 2, :], ep[0:L, 2, :], ALU.mult)
            dve.drain()
            tt(ep[0:L, 4, :], ep[0:L, 3, :], bmv[0:L, :, 1:2].rearrange("p h o -> p (h o)"), ALU.mult)
            dve.drain()
            rsqrt(ep[0:L, 6, :], ep[0:L, 4, :], ep[0:L, 7, :])
            wait(dve, N["gated_done"], c)
            tt(ep[0:L, 5, :], ep[0:L, 6, :], ep[0:L, 2, :], ALU.mult)
            wait(dve, N["o_in"], c * 32 + 32)
            for h in range(H):
                last = stt(gt[0:L, h, :], num[0:L, h, 0:DV], bmv[0:L, h, 0:1], osig[0:L, h, :], ALU.subtract, ALU.mult)
            last.then_inc(N["gt_done"], 1)

        def back(c):
            wait(dve, N["h_in"], c * 32 + 32)
            wait(dve, N["h1_done"], c)
            for q in range(2):
                s = slice(q * 512, (q + 1) * 512)
                wait(dve, N["y_mm"], c * 2 + (q + 1))
                stt(z1[0:L, s], hres[0:L, s], ALPHA, ps[2 + q][0:L, :], ALU.mult, ALU.add).then_inc(N["z_done"], 1)
            dve.drain()
            for q in range(2):
                v.bn_stats(lst[0:L, q, :], z1[0:L, q * 512:(q + 1) * 512])
            dve.drain()
            v.bn_aggr(lmv[0:L, 0:2], lst[0:L, :, :].rearrange("p a b -> p (a b)"))
            dve.drain()
            rsqrt(lmv[0:L, 2:3], lmv[0:L, 1:2], lmv[0:L, 3:4])
            ts(z1[0:L, :], z1[0:L, :], lmv[0:L, 0:1], lmv[0:L, 2:3], ALU.subtract, ALU.mult).then_inc(N["ln_done"], 1)

        front(0)
        head_norm(0)
        dve.wait_ge(N["params"], 16 * 9)
        front(1)
        back_split(0)
        head_norm(1)
        back(0)
        with dve.Fori(2, NT) as i:
            front(i)
            tail(i - 2)
            back_split(i - 1)
            head_norm(i)
            back(i - 1)
        tail(NT - 2)
        back_split(NT - 1)
        back(NT - 1)
        tail(NT - 1)

        def lo_expert(j, k):
            slot = (G0 + k) % 3
            wait(dve, N["hi_done"], j * 3 + (G0 + k + 1))
            tt(wlo[k][:], raw[slot][:], whi[k][:].bitcast(F32), ALU.subtract).then_inc(N["lo_done"], 1)

        lo_expert(0, 0)
        lo_expert(0, 1)

        dve.wait_ge(N["r_arg"], 1)
        dve.wait_ge(N["lg_done"], NT)

        def over_last(ap, k):
            return ap.unsqueeze(2).to_broadcast([ap.shape[0], ap.shape[1], k])

        def over_mid(ap, k):
            return ap.unsqueeze(1).to_broadcast([ap.shape[0], k, ap.shape[1]])

        def red(out, in_, op):
            v.tensor_reduce(out, in_, AX, op)

        i4 = over_mid(r_iota[0:L, 0:GROUPS], NT)
        i8 = over_mid(r_iota[0:L, 0:PER_GROUP], NT)
        gl = lg[0:L, :, 0:GROUPS]
        sc = lambda k: r_s[0:L, k, :]
        red(sc(0), gl, ALU.max)
        dve.drain()
        tt(r_eq4[0:L], gl, over_last(sc(0), GROUPS), ALU.is_lt)
        tt(r_g4[0:L], gl, over_last(sc(0), GROUPS), ALU.subtract)
        dve.drain()
        stt(r_eq4[0:L], r_eq4[0:L], 64.0, i4, ALU.mult, ALU.add)
        dve.drain()
        red(sc(1), r_eq4[0:L], ALU.min)
        dve.drain()
        tt(r_oh4[0:L], i4, over_last(sc(1), GROUPS), ALU.is_equal)
        dve.drain()
        tt(r_prod[0:L], lg[0:L, :, GROUPS:].rearrange("p n (g e) -> p n g e", g=GROUPS),
           r_oh4[0:L].unsqueeze(3).to_broadcast([L, NT, GROUPS, PER_GROUP]), ALU.mult)
        dve.drain()
        tt(r_prod[0:L, :, 0:2, :], r_prod[0:L, :, 0:2, :], r_prod[0:L, :, 2:4, :], ALU.add)
        dve.drain()
        tt(r_in[0:L], r_prod[0:L, :, 0, :], r_prod[0:L, :, 1, :], ALU.add)
        dve.drain()
        for k in range(2):
            red(sc(2 + k), r_in[0:L], ALU.max)
            dve.drain()
            tt(r_t8[0:L], r_in[0:L], over_last(sc(2 + k), PER_GROUP), ALU.is_lt)
            dve.drain()
            stt(r_t8[0:L], r_t8[0:L], 64.0, i8, ALU.mult, ALU.add)
            dve.drain()
            red(sc(7 + k), r_t8[0:L], ALU.min)
            dve.drain()
            tt(r_oh8[0:L, k], i8, over_last(sc(7 + k), PER_GROUP), ALU.is_equal)
            dve.drain()
            if k == 0:
                stt(r_in[0:L], r_oh8[0:L, 0], -3e38, r_in[0:L], ALU.mult, ALU.add)
                dve.drain()
        tt(sc(5), sc(3), sc(2), ALU.subtract).then_inc(N["r_arg"], 1)
        oh5 = r_oh[0:L].rearrange("p (k n) (g e) -> p k n g e", k=2, g=GROUPS)
        for k in range(2):
            for gg in range(GROUPS):
                tt(oh5[:, k, :, gg, :], r_oh8[0:L, k], r_oh4[0:L, :, gg:gg + 1].to_broadcast([L, NT, PER_GROUP]), ALU.mult)
        dve.drain()
        tt(r_oh[0:L], r_oh[0:L], over_last(r_kn[0:L, 2, :], NE), ALU.mult)
        dve.drain()
        tt(r_a[0:L, 0:NT, :], r_oh[0:L, 0:NT, :], r_oh[0:L, NT:, :], ALU.add)
        v.memset(r_acum[0:L, 0, :], 0.0)
        dve.drain()
        for n in range(NT):
            last = tt(r_acum[0:L, n + 1, :], r_acum[0:L, n, :], r_a[0:L, n, :], ALU.add)
            if n < NT - 1:
                dve.drain()
        last.then_inc(N["r_hot"], 1)
        dve.wait_ge(N["r_exp"], 1)
        red(sc(9), r_g4[0:L], ALU.add)
        ts(sc(10), sc(6), 1.0, None, ALU.add)
        dve.drain()
        tt(sc(9), sc(9), sc(10), ALU.mult)
        dve.drain()
        v.reciprocal(wts[0:L, :, 0], sc(9))
        dve.drain()
        tt(wts[0:L, :, 1], wts[0:L, :, 0], sc(6), ALU.mult)
        dve.wait_ge(N["rk_mm"], 1)
        v.tensor_copy(r_rk[0:L].rearrange("p n e -> p (n e)"), ps[2][0:L, 0:NT * NE])
        v.tensor_copy(r_cnt[:], ps[3][:, 0:NE])
        dve.drain()
        for k in range(2):
            tt(r_pr[0:L, k * NT:(k + 1) * NT, :], r_oh[0:L, k * NT:(k + 1) * NT, :], r_rk[0:L], ALU.mult)
        tt(r_ex8[:], r_cnt[:].unsqueeze(2).to_broadcast([P, NE, 8]), r_thr[:].unsqueeze(1).to_broadcast([P, NE, 8]), ALU.is_gt)
        dve.drain()
        red(r_kn[0:L, 3, :], r_pr[0:L], ALU.add)
        red(r_ex[:, 0, :], r_ex8[:], ALU.add)
        dve.drain()
        v.tensor_tensor_scan(r_ex[:, 1, :], r_ex[:, 0, :], r_ex[:, 0, :], 0.0, ALU.add, ALU.max)
        tt(r_c8[0:L], over_last(r_kn[0:L, 3, :], 8), r_thr[0:L].unsqueeze(1).to_broadcast([L, KN, 8]), ALU.is_ge)
        dve.drain()
        tt(r_ex[:, 2, :], r_ex[:, 1, :], r_ex[:, 0, :], ALU.subtract)
        red(r_kn[0:L, 4, :], r_c8[0:L], ALU.add)
        dve.drain()
        tt(r_pr[0:L], r_oh[0:L], over_mid(r_ex[0:L, 2, :], KN), ALU.mult)
        stt(r_kn[0:L, 5, :], r_kn[0:L, 4, :], -float(P), r_kn[0:L, 3, :], ALU.mult, ALU.add)
        for k in range(2):
            stt(r_kn[0:L, 6, k * NT:(k + 1) * NT], sc(1), float(PER_GROUP), sc(7 + k), ALU.mult, ALU.add)
        dve.drain()
        red(r_kn[0:L, 7, :], r_pr[0:L], ALU.add)
        ts(r_kn[0:L, 8, :], r_kn[0:L, 4, :], 1.0, None, ALU.min)
        tt(r_ohr[0:L], over_mid(r_iota[0:L, :], KN), over_last(r_kn[0:L, 5, :], P), ALU.is_equal)
        dve.drain()
        tt(r_kn[0:L, 9, :], r_kn[0:L, 4, :], r_kn[0:L, 7, :], ALU.add)
        dve.drain()
        stt(r_kn[0:L, 9, :], r_kn[0:L, 9, :], float(NE - 1), r_kn[0:L, 6, :], ALU.add, ALU.subtract)
        dve.drain()
        tt(r_kn[0:L, 9, :], r_kn[0:L, 9, :], r_kn[0:L, 8, :], ALU.mult)
        tt(r_kn[0:L, 3, :], r_kn[0:L, 1, :], r_kn[0:L, 2, :], ALU.mult)
        dve.drain()
        tt(r_kn[0:L, 9, :], r_kn[0:L, 9, :], r_kn[0:L, 6, :], ALU.add)
        dve.drain()
        tt(r_rhs[0:L], over_mid(r_iota[0:L, 0:ITEMS], KN), over_last(r_kn[0:L, 9, :], ITEMS), ALU.is_equal)
        dve.drain()
        tt(r_rhs[0:L], r_rhs[0:L], over_last(r_kn[0:L, 3, :], ITEMS), ALU.mult).then_inc(N["r_rhs_done"], 1)
        tt(r_cmp[:], r_iota[0:1, 0:EXTRA].unsqueeze(2).to_broadcast([1, EXTRA, NE]), over_mid(r_ex[0:1, 1, :], EXTRA), ALU.is_ge)
        v.tensor_copy(r_e[:, 0, 0:NE], r_iota[0:1, 0:NE])
        ts(r_e[:, 2, 0:1], r_ex[0:1, 1, NE - 1:NE], float(NE - 1), None, ALU.add)
        dve.drain()
        red(r_e[:, 1, 0:EXTRA], r_cmp[:], ALU.add)
        v.tensor_copy(npm1[:, 1:2], r_e[:, 2, 0:1])
        dve.drain()
        ts(r_e[:, 0, NE:], r_e[:, 1, 0:EXTRA], float(NE - 1), None, ALU.min)
        ts(npm1[:, 0:1], npm1[:, 1:2], 1, None, ALU.arith_shift_right)
        dve.drain()
        v.tensor_copy(eidx[:], r_e[:, 0, :])
        dve.wait_ge(N["v_mm"], 1)
        ts(r_v[:, 0, :], ps[2][:, 0:ITEMS], 0.5, 1e6, ALU.is_lt, ALU.mult)
        dve.drain()
        stt(r_v[:, 1, :], ps[2][:, 0:ITEMS], -1.0, r_v[:, 0, :], ALU.add, ALU.add)
        dve.drain()
        v.tensor_copy(dstrow[:], r_v[:, 1, :])
        dve.drain()
        ts(tokrow[:], dstrow[:], 1, None, ALU.arith_shift_right).then_inc(N["routed"], 1)

        def xg_lo(j, b):
            for q in range(2):
                wait(dve, N["xg_hi"], j * 2 + (q + 1))
                s = slice(4 * q, 4 * q + 4)
                tt(xglo[b][:, s, :].rearrange("p k t -> p (k t)"), ps[q][:], xghi[b][:, s, :].rearrange("p k t -> p (k t)").bitcast(F32), ALU.subtract).then_inc(N["xg_lo"], 1)

        def mid(j):
            wait(dve, N["silu_done"], j + 1)
            wait(dve, N["u2_mm"], j + 1)
            tt(gu[:], sg[:], ps[3][:], ALU.mult).then_inc(N["gu_done"], 1)
            wait(dve, N["g_hi"], j + 1)
            tt(glo[:].rearrange("p k t -> p (k t)"), ps[4][:], ghi[:].rearrange("p k t -> p (k t)").bitcast(F32), ALU.subtract).then_inc(N["g_lo"], 1)

        lo_expert(0, 2)
        xg_lo(0, 0)
        pairs_m1 = dve.value_load(npm1[0:1, 0:1], min_val=NE // 2 - 1, max_val=ITEMS // 2 - 1)

        def item(j, b, last=False):
            if not last:
                lo_expert(j + 1, 0)
                xg_lo(j + 1, 1 - b)
            mid(j)
            if not last:
                lo_expert(j + 1, 1)
                lo_expert(j + 1, 2)

        item(0, 0)
        item(1, 1)
        with dve.Fori(1, pairs_m1) as i:
            item(i * 2, 0)
            item(i * 2 + 1, 1)
        item(pairs_m1 * 2, 0)
        item(pairs_m1 * 2 + 1, 1, last=True)

        dve.wait_ge(N["wts_in"], 16)
        for n in range(NF):
            b = n % 2
            dve.wait_ge(N["y0_done"], n + 1)
            stt(zz[b][:], yy[b][:, 0, :], wts2[:, n, 0:1], zz[b][:], ALU.mult, ALU.add)
            dve.drain()
            stt(zz[b][:], yy[b][:, 1, :], wts2[:, n, 1:2], zz[b][:], ALU.mult, ALU.add).then_inc(N["fsum_done"], 1)
            dve.drain()
            for q in range(2):
                v.bn_stats(fst[:, q, :], zz[b][:, q * 512:(q + 1) * 512])
            dve.drain()
            v.bn_aggr(fmv[:, 0:2], fst[:].rearrange("p a b -> p (a b)"))
            dve.drain()
            rsqrt(fmv[:, 2:3], fmv[:, 1:2], fmv[:, 3:4])
            ts(zz[b][:], zz[b][:], fmv[:, 0:1], fmv[:, 2:3], ALU.subtract, ALU.mult).then_inc(N["fnorm_done"], 1)

    @block.tensor
    def _(pe):
        t = nc.tensor

        def mm3(out, lh, ll, rh, rl, first, last):
            t.matmul(out, lh, rh, start=first, stop=False)
            t.matmul(out, lh, rl, start=False, stop=False)
            return t.matmul(out, ll, rh, start=False, stop=last)

        pe.wait_ge(N["consts"], 1)
        for n in range(NT):
            pe.wait_ge(xt_landed[n % 2], 32 * (n // 2 + 1))
            xv = xt[n % 2][:].rearrange("p (m k) -> p k m", k=KC)
            for half in range(2):
                q = 2 * n + half
                wait(pe, N["x_lo"], q - 3)
                for k in range(4):
                    last = t.transpose(ps[q % 4][:, k * L:(k + 1) * L], xv[0:L, 4 * half + k, :], ident[0:L, 0:L])
                last.then_inc(N["xT_mm"], 1)
        pe.wait_ge(N["gate_mm"], 1)
        pe.wait_ge(N["x_lo"], 2 * NT)
        for n in range(NT):
            c = slice(n * L, (n + 1) * L)
            for k in range(KC):
                last = mm3(ps[6][0:L, n * 8:(n + 1) * 8], xhi[:, k, c], xlo[:, k, c], wg_hi[:, k, :], wg_lo[:, k, :], k == 0, k == KC - 1)
        last.then_inc(N["gate_mm"], 1)

        def project(i, sub):
            wait(pe, N["lo_done"], i * 2 + (sub + 1))
            wh = whi[sub][:].rearrange("p (k n) -> p k n", k=KC)
            wl = wlo[sub][:].rearrange("p (k n) -> p k n", k=KC)
            for n in range(NT):
                pos = sub * NT + n
                wait(pe, N["bank_free"], i * 18 + (pos + 1))
                c = slice(n * L, (n + 1) * L)
                for k in range(KC):
                    last = mm3(ps[pos % 6][0:L, :], xhi[:, k, c], xlo[:, k, c], wh[:, k, :], wl[:, k, :], k == 0, k == KC - 1)
                last.then_inc(N["blk_mm"], 1)

        with pe.Fori(0, 2) as i:
            project(i, 0)
            project(i, 1)
        pe.wait_ge(N["a_rows"], 1)
        t.matmul(ps[6][0:L, 0:NT * H], upto[0:L, :], glf[0:L].rearrange("p n h -> p (n h)"), start=True, stop=True).then_inc(N["b_mm"], 1)
        project(2, 0)
        pe.wait_ge(N["a_rows"], 2)
        for n in range(8):
            last = t.transpose(ps[6 + n // 4][0:H, (n % 4) * L:(n % 4 + 1) * L], ga[0:L, n, :], ident[0:L, 0:L])
        last.then_inc(N["aT_mm"], 1)
        pe.wait_ge(N["aT_mm"], 2)
        t.transpose(ps[6][0:H, 0:L], ga[0:L, 8, :], ident[0:L, 0:L])
        for n in range(NT):
            last = t.matmul(ps[6][0:H, 480 + n:481 + n], glf[0:L, n, :], ones[0:L, 0:1], start=True, stop=True)
        last.then_inc(N["aT_mm"], 1)
        project(2, 1)
        pe.wait_ge(N["m_rows"], 1)
        for n in range(NT):
            t.transpose(ps[6][0:L, n * H:(n + 1) * H], cm[:, n, :], ident[0:H, 0:H])
        for h in range(H):
            last = t.matmul(ps[7][:, h * 2 * NT:(h + 1) * 2 * NT], selpos[:, h, :], mcl[:], start=True, stop=True)
        last.then_inc(N["mb_mm"], 1)

        def front(c, i):
            wait(pe, N["qk_in"], c * 32 + 32)
            wait(pe, N["o_lo"], i * 2 - 2)
            wait(pe, N["z_done"], i * 2 - 2)
            for h in range(H):
                last = t.transpose(ps[0][:, h * L:(h + 1) * L], qk[0:L, 0, h, :], ident[0:L, 0:L])
            last.then_inc(N["t_mm"], 1)
            for h in range(H):
                last = t.transpose(ps[2][:, h * L:(h + 1) * L], qk[0:L, 1, h, :], ident[0:L, 0:L])
            last.then_inc(N["t_mm"], 1)
            wait(pe, N["qs_done"], c * 2 + 2)
            for h in range(H):
                last = t.transpose(ps[1][:, h * L:(h + 1) * L], qs[0:L, h, :], ident[0:L, 0:L])
            last.then_inc(N["t_mm"], 1)
            for h in range(H):
                rhs = cm[:, c, :] if isinstance(c, int) else cm[:, bass.ds(c, 1), :].rearrange("p n t -> p (n t)")
                out_h = ps[3][0:L, h * L:(h + 1) * L]
                t.matmul(out_h, identb[0:L, :], maskb[0:L, :], start=True, stop=False)
                last = t.matmul(out_h, selneg[:, h, 0:L], rhs, start=False, stop=True)
            last.then_inc(N["e_mm"], 1)
            wait(pe, N["t_cp"], c * 3 + 2)
            wait(pe, N["ht_cp"], i * 2 - 4)
            wait(pe, N["sw_done"], c)
            for h in range(H):
                last = t.matmul(ps[4][0:L, h * L:(h + 1) * L], kT[:, h * L:(h + 1) * L], qT[:, h * L:(h + 1) * L], start=True, stop=True)
            last.then_inc(N["s_mm"], 1)
            wait(pe, N["sw_done"], c + 1)
            wait(pe, N["t_cp"], c * 3 + 3)
            wait(pe, N["v_in"], c * 32 + 32)
            if isinstance(c, int) and c == 0:
                pe.wait_ge(N["ones_ready"], 1)
            wait(pe, N["lg_done"], i - 2)
            for h in range(H):
                wait(pe, N["num_done"], c * 4 + (h - 1))
                wait(pe, N["c_done"], c * 4 + 1)
                t.matmul(ps[5 + h % 2][0:L, 0:DV + 1], sw[0:L, h * L:(h + 1) * L], vext[0:L, h, :], start=True, stop=False)
                t.matmul(ps[5 + h % 2][0:L, 0:DV + 1], qsT[:, h * L:(h + 1) * L], cst[:, h, :], start=False, stop=True).then_inc(N["n_mm"], 1)
                wait(pe, N["c_done"], c * 4 + (h + 1))
                t.matmul(ps[7][:, 0:DV + 1], ks[0:L, h, :], vext[0:L, h, :], start=True, stop=True).then_inc(N["u_mm"], 1)

        def tail(c, i):
            wait(pe, N["num_done"], i * 4 + 4)
            wait(pe, N["h1_done"], c + 1)
            hv = h1t[:].rearrange("p (m k) -> p k m", k=KC)
            for q in range(2):
                for k in range(4):
                    last = t.transpose(ps[4 + q][:, k * L:(k + 1) * L], hv[0:L, 4 * q + k, :], ident[0:L, 0:L])
                last.then_inc(N["ht_mm"], 1)
            wait(pe, N["ht_cp"], c * 2 + 2)
            for k in range(KC):
                last = t.matmul(ps[6][0:L, 0:GROUPS + NE], h1T[:, k, :], wgr[:, k, :], start=k == 0, stop=k == KC - 1)
            last.then_inc(N["lg_mm"], 1)

        def back(c, i):
            wait(pe, N["gated_done"], c + 1)
            wait(pe, N["t_cp"], i * 3 + 3)
            wait(pe, N["ew_done"], i + 1)
            gv = gated[:].rearrange("p h d -> p (h d)").rearrange("p (m k) -> p k m", k=KC)
            for q in range(2):
                for k in range(4):
                    last = t.transpose(ps[q][:, k * L:(k + 1) * L], gv[0:L, 4 * q + k, :], ident[0:L, 0:L])
                last.then_inc(N["ot_mm"], 1)
            wait(pe, N["o_lo"], c * 2 + 2)
            for q in range(2):
                wh = whi[q][:].rearrange("p (k n) -> p k n", k=KC)
                wl = wlo[q][:].rearrange("p (k n) -> p k n", k=KC)
                for k in range(KC):
                    last = mm3(ps[2 + q][0:L, :], ohi[:, k, :], olo[:, k, :], wh[:, k, :], wl[:, k, :], k == 0, k == KC - 1)
                last.then_inc(N["y_mm"], 1)

        pe.wait_ge(N["bank_free"], 6 + 6 * NT)
        pe.wait_ge(N["gate_exp"], 1)
        pe.wait_ge(N["lo_done"], G0)
        front(0, 0)
        front(1, 1)
        back(0, 1)
        pe.wait_ge(N["params"], 16 * 9)
        with pe.Fori(2, NT) as i:
            front(i, i)
            tail(i - 2, i)
            back(i - 1, i)
        tail(NT - 2, NT - 1)
        back(NT - 1, NT - 1)
        tail(NT - 1, NT - 1)

        pe.wait_ge(N["r_hot"], 1)
        t.matmul(ps[2][0:L, 0:NT * NE], beforeb[0:L, :], r_a[0:L, 0:NT, :].rearrange("p n e -> p (n e)"), start=True, stop=False)
        t.matmul(ps[2][0:L, 0:NT * NE], onesb[0:L, 0:L], r_acum[0:L, 0:NT, :].rearrange("p n e -> p (n e)"), start=False, stop=True)
        t.matmul(ps[3][:, 0:NE], onesb[0:L, :], r_acum[0:L, NT, :], start=True, stop=True).then_inc(N["rk_mm"], 1)
        pe.wait_ge(N["r_rhs_done"], 1)
        for q in range(2 * NT):
            last = t.matmul(ps[2][:, 0:ITEMS], r_ohr[0:L, q, :], r_rhs[0:L, q, :], start=q == 0, stop=q == 2 * NT - 1)
        last.then_inc(N["v_mm"], 1)

        def rows_T(j, b):
            wait(pe, gathered[b], (j - b) * 8 + 16)
            wait(pe, N["xg_lo"], j * 2)
            xv = xg[b][:].rearrange("p (m k) -> p k m", k=KC)
            for q in range(2):
                for k in range(4):
                    last = t.transpose(ps[q][:, k * P:(k + 1) * P], xv[:, 4 * q + k, :], ident[:])
                last.then_inc(N["xgT_mm"], 1)

        def item(j, b, last_item=False):
            def up_or_gate(k, bank):
                wait(pe, N["lo_done"], j * 3 + (G0 + k + 1))
                wh = whi[k][:].rearrange("p (k n) -> p k n", k=KC)
                wl = wlo[k][:].rearrange("p (k n) -> p k n", k=KC)
                for kk in range(KC):
                    last = mm3(ps[bank][:], xghi[b][:, kk, :], xglo[b][:, kk, :], wh[:, kk, :], wl[:, kk, :], kk == 0, kk == KC - 1)
                return last

            wait(pe, N["xg_lo"], j * 2 + 2)
            wait(pe, N["silu_done"], j)
            up_or_gate(0, 2).then_inc(N["g_mm"], 1)
            if not last_item:
                rows_T(j + 1, 1 - b)
            wait(pe, N["gu_done"], j)
            up_or_gate(1, 3).then_inc(N["u2_mm"], 1)
            wait(pe, N["gu_done"], j + 1)
            wait(pe, N["g_lo"], j)
            gv = gu[:].rearrange("p (m k) -> p k m", k=FC)
            for k in range(FC):
                last = t.transpose(ps[4][:, k * P:(k + 1) * P], gv[:, k, :], ident[:])
            last.then_inc(N["guT_mm"], 1)
            wait(pe, N["lo_done"], j * 3 + (G0 + 3))
            wait(pe, N["g_lo"], j + 1)
            wait(pe, N["y_cp"], j * 2)
            wh = whi[2][:].rearrange("p (k n) -> p k n", k=FC)
            wl = wlo[2][:].rearrange("p (k n) -> p k n", k=FC)
            for q in range(2):
                c = slice(q * 512, (q + 1) * 512)
                for k in range(FC):
                    last = mm3(ps[5 + q][:], ghi[:, k, :], glo[:, k, :], wh[:, k, c], wl[:, k, c], k == 0, k == FC - 1)
                last.then_inc(N["y2_mm"], 1)

        pe.wait_ge(N["routed"], 1)
        rows_T(0, 0)
        pairs_m1 = pe.value_load(npm1[0:1, 0:1], min_val=NE // 2 - 1, max_val=ITEMS // 2 - 1)
        item(0, 0)
        item(1, 1)
        with pe.Fori(1, pairs_m1) as i:
            item(i * 2, 0)
            item(i * 2 + 1, 1)
        item(pairs_m1 * 2, 0)
        item(pairs_m1 * 2 + 1, 1, last_item=True)

    block.__exit__(None, None, None)
    dma_ok.__exit__(None, None, None)


_INS = ["w_in", "b_gates", "head_norm_w", "w_out", "ln1_g", "ln1_b", "w_group", "b_group", "w_router",
        "b_router", "w_gate", "w_up", "w_down", "ln2_g", "ln2_b"]


def kernel(x, meta_tokens, **params):
    import numpy as np
    import concourse.bacc as bacc
    from concourse.bass_utils import run_bass_kernel_spmd

    nc = bacc.Bacc("TRN2", target_bir_lowering=False, num_devices=1)
    x = np.asarray(x)
    rows = np.concatenate([np.asarray(meta_tokens), x[0], np.zeros((TP - T, D), x.dtype)])
    arrays = {"hcat": rows}
    args = [nc.dram_tensor("hcat", rows.shape, F32, kind="ExternalInput").ap()]
    for name in _INS:
        arrays["l0_" + name] = np.ascontiguousarray(params["l0_" + name])
        args.append(nc.dram_tensor("l0_" + name, arrays["l0_" + name].shape, F32, kind="ExternalInput").ap())
    out = nc.dram_tensor("out", (OUT_ROWS, D), F32, kind="ExternalOutput").ap()
    build(nc, *args, out)
    r = run_bass_kernel_spmd(nc, [arrays], core_ids=[0])
    return r.results[0]["out"].reshape(1, OUT_ROWS, D)
```

```python
import concourse.bass as bass
from concourse import mybir

F32 = mybir.dt.float32
F32R = mybir.dt.float32r
BF16 = mybir.dt.bfloat16
I32 = mybir.dt.int32
U32 = mybir.dt.uint32
ALU = mybir.AluOpType
ACT = mybir.ActivationFunctionType
AX = mybir.AxisListType.X

P = 128
D = 1024
KC = D // P
NMETA = 16
T = 1040
L = 116
NT = 9
TP = L * NT
H = 4
DQ = 128
DV = 256
QSCALE = DQ ** -0.5
ALPHA = 2.0 ** 0.25
EPS = 1e-5
NEG = -1e30
GROUPS = 4
PER_GROUP = 8
NE = 32
FE = 512
FC = FE // P
PIECE = 4096
EXTRA = 16
ITEMS = NE + EXTRA
OUT_ROWS = T - NMETA
NF = OUT_ROWS // P


def wait(eng, sem, value):
    if isinstance(value, int) and value <= 0:
        return
    eng.wait_ge(sem, value)


def rows_of(eng, c):
    if isinstance(c, int):
        return slice(c * L, c * L + L)
    return bass.ds(eng.snap(c * L), L)


def build(nc, hcat, w_in, b_gates, head_norm_w, w_out, ln1_g, ln1_b, w_group, b_group, w_router,
          b_router, w_gate, w_up, w_down, ln2_g, ln2_b, out):
    dma_ok = nc.allow_non_contiguous_dma(reason="small parameter vectors and gate columns")
    dma_ok.__enter__()

    proj = nc.dram_tensor("proj", (TP, 3072), F32).ap()
    h1_dram = nc.dram_tensor("h1_rows", (TP, D), F32).ap()
    ys = nc.dram_tensor("expert_rows", (2 * T, D), F32).ap()
    wts_dram = nc.dram_tensor("pair_weights", (TP, 2), F32).ap()

    base = (nc.sbuf_base + 63) // 64 * 64
    cursor = [base]

    def at(name, shape, dt=F32):
        n = 1
        for s in shape[1:]:
            n *= s
        t = nc.alloc_sbuf_tensor_at(name, list(shape), dt, offset=cursor[0])
        cursor[0] += (n * (2 if dt == BF16 else 4) + 31) // 32 * 32
        assert cursor[0] <= nc.sbuf_usable_end, (name, cursor[0])
        return t

    stream_base = cursor[0]
    raw = [at(f"raw{s}", [P, PIECE]) for s in range(3)]
    whi = [at(f"whi{s}", [P, PIECE], F32R) for s in range(2)]
    wlo = [at(f"wlo{s}", [P, PIECE], F32R) for s in range(2)]
    stream_end = cursor[0]
    ident = at("ident", [P, P])
    identb = at("identb", [P, L], BF16)
    maskb = at("maskb", [P, L], BF16)
    upto = at("upto", [P, L])
    beforeb = at("beforeb", [P, L], BF16)
    onesb = at("onesb", [P, P], BF16)
    ones = at("ones", [P, 2])
    selneg = at("selneg", [H, H, P])
    selpos = at("selpos", [H, H, P])
    hnw = at("hnw", [P, KC])
    wg_raw = at("wg_raw", [P, KC, 2 * H])
    wg_hi = at("wg_hi", [P, KC, 2 * H], F32R)
    wg_lo = at("wg_lo", [P, KC, 2 * H], F32R)
    bg = at("bg", [P, 2 * H])
    gts = at("gts", [P, NT, 2 * H])
    ga = at("ga", [P, NT, H])
    gb = at("gb", [P, NT, H])
    glf = at("glf", [P, NT, H])
    gtmp = at("gtmp", [P, NT, H])
    gcm = at("gcm", [P, NT, H])
    gmc = at("gmc", [P, H, 2 * NT])
    garg = at("garg", [P, 3, NT, H])
    gexp = at("gexp", [P, 3, NT, H])
    warg = at("warg", [P, NT, H])
    wprev = at("wprev", [P, NT, H])
    bl = at("bl", [H, NT])
    mcar = at("mcar", [H, NT + 1])
    mcl = at("mcl", [H, 2 * NT])
    cm = at("cm", [H, NT, L])
    lg = at("lg", [P, NT, GROUPS + NE])
    tokrow = at("tokrow", [P, ITEMS], I32)
    dstrow = at("dstrow", [P, ITEMS], I32)
    eidx = at("eidx", [1, ITEMS], I32)
    npm1 = at("npm1", [1, 2], I32)
    wts = at("wts", [P, NT, 2])
    wts2 = at("wts2", [P, NF, 2])
    region = cursor[0]

    xhi = at("xhi", [P, KC, TP], F32R)
    xlo = at("xlo", [P, KC, TP], F32R)
    xt_at = cursor[0]
    xt = [at(f"xt{i}", [P, D]) for i in range(2)]
    stage = [at(f"stage{i}", [P, 512]) for i in range(3)]
    cursor[0] = xt_at
    at_ = at("aT", [H, NT, L])

    cursor[0] = region
    qk = at("qk", [P, 2, H, DQ])
    vext = at("vext", [P, H, DV + 1])
    osig = at("osig", [P, H, DV])
    hres = at("hres", [P, D])
    qs = at("qs", [P, H, DQ])
    ks = at("ks", [P, H, DQ])
    qT = at("qT", [P, H * L])
    qsT = at("qsT", [P, H * L])
    kT = at("kT", [P, H * L])
    ew = at("ew", [P, H * L])
    sw = at("sw", [P, H * L])
    num = at("num", [P, H, DV + 1])
    cst = at("cst", [P, H, DV + 1])
    gt = at("gt", [P, H, DV])
    gated = at("gated", [P, H, DV])
    ohi = at("ohi", [P, KC, L], F32R)
    olo = at("olo", [P, KC, L], F32R)
    z1 = at("z1", [P, D])
    h1t = at("h1t", [P, D])
    h1T = at("h1T", [P, KC, L])
    g1 = at("g1", [P, D])
    b1 = at("b1", [P, D])
    wgr = at("wgr", [P, KC, GROUPS + NE])
    bgr = at("bgr", [P, GROUPS + NE])
    bst = at("bst", [P, H, 6])
    bmv = at("bmv", [P, H, 2])
    ep = at("ep", [P, 8, H])
    lst = at("lst", [P, 2, 6])
    lmv = at("lmv", [P, 4])

    cursor[0] = region
    route_base = cursor[0]
    whi.append(at("whi2", [P, PIECE], F32R))
    wlo.append(at("wlo2", [P, PIECE], F32R))
    xg = [at(f"xg{i}", [P, D]) for i in range(2)]
    xghi = [at(f"xghi{i}", [P, KC, P], F32R) for i in range(2)]
    xglo = [at(f"xglo{i}", [P, KC, P], F32R) for i in range(2)]
    sg = at("sg", [P, FE])
    gu = at("gu", [P, FE])
    ghi = at("ghi", [P, FC, P], F32R)
    glo = at("glo", [P, FC, P], F32R)
    yt = [at(f"yt{i}", [P, D]) for i in range(2)]
    tix = [at(f"tix{i}", [P, 1], I32) for i in range(2)]
    dix = [at(f"dix{i}", [P, 1], I32) for i in range(2)]

    cursor[0] = route_base
    KN = 2 * NT
    r_iota = at("r_iota", [P, P])
    r_eq4 = at("r_eq4", [P, NT, GROUPS])
    r_oh4 = at("r_oh4", [P, NT, GROUPS])
    r_g4 = at("r_g4", [P, NT, GROUPS])
    r_prod = at("r_prod", [P, NT, GROUPS, PER_GROUP])
    r_in = at("r_in", [P, NT, PER_GROUP])
    r_t8 = at("r_t8", [P, NT, PER_GROUP])
    r_oh8 = at("r_oh8", [P, 2, NT, PER_GROUP])
    r_s = at("r_s", [P, 16, NT])
    r_kn = at("r_kn", [P, 10, KN])
    r_oh = at("r_oh", [P, KN, NE])
    r_pr = at("r_pr", [P, KN, NE])
    r_rk = at("r_rk", [P, NT, NE])
    r_cnt = at("r_cnt", [P, NE])
    r_ex8 = at("r_ex8", [P, NE, 8])
    r_ex = at("r_ex", [P, 4, NE])
    r_c8 = at("r_c8", [P, KN, 8])
    r_thr = at("r_thr", [P, 8])
    r_a = at("r_a", [P, NT + 1, NE], BF16)
    r_acum = at("r_acum", [P, NT + 1, NE], BF16)
    r_ohr = at("r_ohr", [P, KN, P])
    r_rhs = at("r_rhs", [P, KN, ITEMS])
    r_v = at("r_v", [P, 2, ITEMS])
    r_e = at("r_e", [1, 3, ITEMS])
    r_cmp = at("r_cmp", [1, EXTRA, NE])
    assert cursor[0] <= route_base + 2 * PIECE * 4 + 2 * D * 4

    cursor[0] = stream_base
    yy = [at(f"yy{i}", [P, 2, D]) for i in range(2)]
    hh = [at(f"hh{i}", [P, D]) for i in range(2)]
    zz = [at(f"zz{i}", [P, D]) for i in range(2)]
    zn = [at(f"zn{i}", [P, D]) for i in range(2)]
    g2 = at("g2", [P, D])
    b2 = at("b2", [P, D])
    fst = at("fst", [P, 2, 6])
    fmv = at("fmv", [P, 4])
    assert cursor[0] <= stream_end

    ps = [nc.alloc_psum_tensor(f"bank{i}", [P, 512], F32) for i in range(8)]

    S = {}

    def sem(name):
        if name not in S:
            S[name] = nc.alloc_semaphore(name)
        return S[name]

    first_landed = [sem(f"first_landed{s}") for s in range(2)]
    raw_landed = [sem(f"raw_landed{s}") for s in range(3)]
    xt_landed = [sem(f"xt_landed{s}") for s in range(2)]
    gathered = [sem(f"gathered{s}") for s in range(2)]
    scattered = [sem(f"scattered{s}") for s in range(2)]
    y_landed = [sem(f"y_landed{s}") for s in range(2)]
    out_stored = [sem(f"out_stored{s}") for s in range(2)]

    names = """params consts xT_mm x_hi x_lo gate_mm gate_l b_mm a_rows aT_mm m_rows mb_mm
        gate_exp hi_done lo_done blk_mm bank_free stored stage_free ones_ready sp_passed pool_passed
        qk_in v_in o_in h_in qs_done t_mm t_cp e_mm s_mm ew_done sw_done n_mm num_done u_mm
        c_done gt_done gated_done ot_mm o_hi o_lo y_mm z_done ln_done h1_done h1_stored ht_mm
        ht_cp lg_mm lg_done
        r_exp r_arg r_hot rk_mm r_rhs_done v_mm routed wts_stored wts_in
        index_ready xgT_mm xg_hi xg_lo g_mm silu_done u2_mm gu_done guT_mm g_hi g_lo y2_mm y_cp
        ln2_in y0_done fsum_done fnorm_done f_out_done""".split()
    N = {n: sem(n) for n in names}

    def piece_src(g):
        w, c = (w_in, (4, 0, 1, 2, 3, 5)[g]) if g < 6 else (w_out, g - 6)
        return w[:, c * 512:(c + 1) * 512].rearrange("(p k) n -> p k n", k=KC)

    def landed_count(g):
        return 16 * (g // 3 + (g % 3 > 0))

    gate_w = w_gate.rearrange("e (p k) n -> e p (k n)", k=KC)
    up_w = w_up.rearrange("e (p k) n -> e p (k n)", k=KC)
    down_w = w_down.rearrange("e (p k) n -> e p (k n)", k=FC)
    G0 = 8

    def rows_load(eng, dst, src, s):
        eng.dma_start(dst[0:112], src[0:112]).then_inc(s, 16)
        eng.dma_start(dst[112:L], src[112:L]).then_inc(s, 16)

    block = nc.Block()
    block.__enter__()

    @block.sync
    def _(sp):
        def load_piece(g):
            wait(sp, N["lo_done"], 2 * (g - 2))
            sp.dma_start(raw[g % 3][:].rearrange("p (k n) -> p k n", k=KC), piece_src(g)).then_inc(raw_landed[g % 3], 16)

        def load_expert(j, e, k):
            g_slot = (G0 + k) % 3
            wait(sp, N["lo_done"], j * 6 + 2 * (G0 + k - 2))
            src = (gate_w, up_w, down_w)[k]
            sp.dma_start(raw[g_slot][:], src[e, :, :] if isinstance(e, int) else src[bass.ds(e, 1), :, :].rearrange("e p n -> p (e n)")).then_inc(raw_landed[g_slot], 16)

        def load_x(n):
            wait(sp, N["xT_mm"], 2 * (n - 1))
            sp.dma_start(xt[n % 2][0:112, :], hcat[n * L:n * L + 112, :]).then_inc(xt_landed[n % 2], 16)
            sp.dma_start(xt[n % 2][112:L, :], hcat[n * L + 112:(n + 1) * L, :]).then_inc(xt_landed[n % 2], 16)

        load_x(0)
        load_x(1)
        for part in range(2):
            c = slice(part * 2048, (part + 1) * 2048)
            sp.dma_start(raw[0][:, c].rearrange("p (k n) -> p k n", k=4), piece_src(0)[:, 4 * part:4 * part + 4, :]).then_inc(first_landed[part], 16)
        vec = lambda v, n: v.rearrange("(a n) -> a n", a=1).to_broadcast([n, v.shape[0]])
        sp.dma_start(wg_raw[:], w_in[:, 3072:3072 + 2 * H].rearrange("(p k) n -> p k n", k=KC)).then_inc(N["params"], 16)
        sp.dma_start(bg[:], vec(b_gates, P)).then_inc(N["params"], 16)
        sp.dma_start(hnw[:], head_norm_w.rearrange("(p k) -> p k", k=KC)).then_inc(N["params"], 16)
        for n in range(2, NT):
            load_x(n)
            if n == 4:
                load_piece(1)
        for g in range(2, 8):
            load_piece(g)
        for k in range(3):
            load_expert(0, 0, k)

        sp.wait_ge(N["stored"], 16 * 6 * NT)
        sp.wait_ge(N["gate_exp"], 1)
        sp.dma_start(g1[:], vec(ln1_g, P)).then_inc(N["params"], 16)
        sp.dma_start(b1[:], vec(ln1_b, P)).then_inc(N["params"], 16)
        sp.dma_start(wgr[:, :, 0:GROUPS], w_group.rearrange("(p k) n -> p k n", k=KC)).then_inc(N["params"], 16)
        sp.dma_start(wgr[:, :, GROUPS:], w_router.rearrange("(p k) n -> p k n", k=KC)).then_inc(N["params"], 16)
        sp.dma_start(bgr[:, 0:GROUPS], vec(b_group, P)).then_inc(N["params"], 16)
        sp.dma_start(bgr[:, GROUPS:], vec(b_router, P)).then_inc(N["params"], 16)

        def load_residual(c):
            rows = rows_of(sp, c)
            wait(sp, N["z_done"], c * 2)
            rows_load(sp, hres[0:L, :], hcat[rows, :], N["h_in"])

        def load_tile(c):
            rows = rows_of(sp, c)
            src = proj[rows, :]
            wait(sp, N["t_mm"], c * 3)
            sp.sem_inc(N["sp_passed"], 1)
            wait(sp, N["qs_done"], c * 2)
            rows_load(sp, qk[0:L].rearrange("p a h d -> p (a h d)"), src[:, 0:1024], N["qk_in"])
            wait(sp, N["u_mm"], c * 4)
            for r0, r1 in ((0, 112), (112, L)):
                sp.dma_start(vext[r0:r1, :, 0:DV], src[r0:r1, 1024:2048].rearrange("p (h d) -> p h d", h=H)).then_inc(N["v_in"], 16)
            wait(sp, N["gt_done"], c)
            rows_load(sp, osig[0:L].rearrange("p h d -> p (h d)"), src[:, 2048:3072], N["o_in"])
            if not (isinstance(c, int) and c == 0):
                load_residual(c - 1)

        load_tile(0)
        with sp.Fori(1, NT) as c:
            load_tile(c)
        load_residual(NT - 1)

        sp.wait_ge(N["routed"], 1)
        pairs_m1 = sp.value_load(npm1[0:1, 0:1], min_val=NE // 2 - 1, max_val=ITEMS // 2 - 1)
        with sp.Fori(0, pairs_m1) as i:
            for par in range(2):
                j = i * 2 + (1 + par)
                e = sp.value_load(eidx[0:1, bass.ds(j, 1)], min_val=0, max_val=NE - 1)
                for k in range(3):
                    load_expert(j, e, k)
        j = pairs_m1 * 2 + 1
        e = sp.value_load(eidx[0:1, bass.ds(j, 1)], min_val=0, max_val=NE - 1)
        for k in range(3):
            load_expert(j, e, k)

        sp.wait_ge(N["y2_mm"], pairs_m1 * 4 + 4)
        sp.dma_start(g2[:], vec(ln2_g, P)).then_inc(N["ln2_in"], 16)
        sp.dma_start(b2[:], vec(ln2_b, P)).then_inc(N["ln2_in"], 16)
        for s in range(2):
            sp.wait_ge(scattered[s], pairs_m1 * 16 + 16)
        for n in range(NF):
            b = n % 2
            t0 = NMETA + n * P
            wait(sp, N["fsum_done"], n - 1)
            sp.dma_start(yy[b][:].rearrange("p a d -> p (a d)"), ys[2 * t0:2 * (t0 + P), :].rearrange("(p a) d -> p (a d)", a=2)).then_inc(y_landed[b], 16)
            sp.dma_start(hh[b][:], h1_dram[t0:t0 + P, :]).then_inc(y_landed[b], 16)

    @block.gpsimd
    def _(pool):
        g = nc.gpsimd
        g.memset(ident[:], 0.0)
        g.memset(upto[:], 1.0)
        g.memset(selpos[:], 0.0)
        g.memset(selneg[:], 0.0)
        g.memset(onesb[:], 1.0)
        g.memset(identb[:], 0.0)
        g.memset(beforeb[:], 1.0)
        g.memset(maskb[:], 0.0)
        pool.drain()
        g.affine_select(out=ident[:], in_=ident[:], compare_op=ALU.not_equal, fill=1.0, base=0, pattern=[[-1, P]], channel_multiplier=1)
        g.affine_select(out=identb[:], in_=identb[:], compare_op=ALU.not_equal, fill=1.0, base=0, pattern=[[-1, L]], channel_multiplier=1)
        g.affine_select(out=upto[:], in_=upto[:], compare_op=ALU.is_ge, fill=0.0, base=0, pattern=[[1, L]], channel_multiplier=-1)
        g.affine_select(out=beforeb[:], in_=beforeb[:], compare_op=ALU.is_gt, fill=0.0, base=0, pattern=[[1, L]], channel_multiplier=-1)
        g.affine_select(out=maskb[:], in_=maskb[:], compare_op=ALU.is_ge, fill=NEG, base=0, pattern=[[1, L]], channel_multiplier=-1)
        g.affine_select(out=selpos[:], in_=selpos[:], compare_op=ALU.not_equal, fill=1.0, base=0, pattern=[[-1, H], [0, P]], channel_multiplier=1)
        g.affine_select(out=selneg[:], in_=selneg[:], compare_op=ALU.not_equal, fill=-1.0, base=0, pattern=[[-1, H], [0, P]], channel_multiplier=1)
        pool.drain()
        g.memset(ones[:], 1.0).then_inc(N["consts"], 1)

        def store(u, s, col):
            wait(pool, N["bank_free"], u + 4)
            n = s[1]
            pool.dma_start(proj[n * L:(n + 1) * L, col], stage[s[0]][0:L, :]).then_inc(N["stored"], 16)
            wait(pool, N["stored"], u * 16 + 16)
            pool.sem_inc(N["stage_free"], 1)

        for n in range(NT):
            store(n, (n % 3, n), slice(4 * 512, 5 * 512))
        with pool.Fori(0, 2) as i:
            for pos in range(2 * NT):
                store(i * 18 + (NT + pos), (pos % 3, pos % NT), bass.ds(pool.snap(i * 1024 + 512 * (pos // NT)), 512))
        for n in range(NT):
            store(5 * NT + n, (n % 3, n), slice(5 * 512, 6 * 512))

        pool.wait_ge(N["gate_exp"], 1)
        g.memset(vext[:, :, DV:DV + 1], 1.0).then_inc(N["ones_ready"], 1)

        def front(c):
            wait(pool, N["qk_in"], c * 32 + 32)
            wait(pool, N["t_mm"], c * 3)
            wait(pool, N["u_mm"], c * 4)
            cc = bass.ds(c, 1) if not isinstance(c, int) else slice(c, c + 1)
            wint = gexp[0:L, 0, cc, :].rearrange("p n h -> p (n h)").unsqueeze(2).to_broadcast([L, H, DQ])
            wsc = gexp[0:L, 2, cc, :].rearrange("p n h -> p (n h)").unsqueeze(2).to_broadcast([L, H, DQ])
            g.tensor_tensor(qs[0:L], qk[0:L, 0], wint, ALU.mult).then_inc(N["qs_done"], 1)
            g.tensor_tensor(ks[0:L], qk[0:L, 1], wsc, ALU.mult).then_inc(N["qs_done"], 1)

        def back(c):
            rows = rows_of(pool, c)
            wait(pool, N["ln_done"], c + 1)
            wait(pool, N["h1_stored"], c * 16)
            wait(pool, N["ht_mm"], c * 2)
            g.tensor_tensor(h1t[0:L, :], z1[0:L, :], g1[0:L, :], ALU.mult)
            pool.drain()
            g.tensor_tensor(h1t[0:L, :], h1t[0:L, :], b1[0:L, :], ALU.add).then_inc(N["h1_done"], 1)
            wait(pool, N["h1_done"], c + 1)
            pool.dma_start(h1_dram[rows, :], h1t[0:L, :]).then_inc(N["h1_stored"], 16)

        pool.wait_ge(N["params"], 16 * 9)
        front(0)
        front(1)
        front(2)
        back(0)
        with pool.Fori(2, NT - 1) as i:
            front(i + 1)
            back(i - 1)
        back(NT - 2)
        back(NT - 1)

        pool.wait_ge(N["lg_done"], NT)
        pool.wait_ge(N["h1_stored"], 16 * NT)
        g.iota(r_iota[:].bitcast(I32), [[1, P]], base=0, channel_multiplier=0)
        g.iota(r_thr[:].bitcast(I32), [[P, 8]], base=P, channel_multiplier=0)
        g.iota(r_kn[0:L, 0, :].rearrange("p (k n) -> p k n", k=2).bitcast(I32), [[1, 2], [2 * L, NT]], base=1, channel_multiplier=2)
        pool.drain()
        g.tensor_copy(r_iota[:], r_iota[:].bitcast(I32))
        g.tensor_copy(r_thr[:], r_thr[:].bitcast(I32))
        g.tensor_copy(r_kn[0:L, 1, :], r_kn[0:L, 0, :].bitcast(I32))
        g.memset(r_kn[0:L, 2, :], 1.0)
        pool.drain()
        g.affine_select(out=r_kn[0:L, 2, :].rearrange("p (k n) -> p k n", k=2), in_=r_kn[0:L, 2, :].rearrange("p (k n) -> p k n", k=2),
                        compare_op=ALU.is_gt, fill=0.0, base=T, pattern=[[0, 2], [-L, NT]], channel_multiplier=-1).then_inc(N["r_arg"], 1)

        pool.wait_ge(N["routed"], 1)
        pool.dma_start(wts_dram.rearrange("(n p) k -> p n k", p=L), wts[0:L, :, :]).then_inc(N["wts_stored"], 16)
        pool.wait_ge(N["wts_stored"], 16)
        pool.dma_start(wts2[:], wts_dram[NMETA:T, :].rearrange("(n p) k -> p n k", p=P)).then_inc(N["wts_in"], 16)

        for b in range(2):
            g.memset(xg[b][:], 0.0)
        pool.drain()

        last_token, last_row = pool.to_reg(T - 1), pool.to_reg(2 * T - 1)

        def gather(j, b):
            jj = slice(j, j + 1) if isinstance(j, int) else bass.ds(j, 1)
            wait(pool, gathered[b], (j - b) * 8)
            g.tensor_copy(tix[b][:], tokrow[:, jj])
            pool.drain()
            wait(pool, N["xgT_mm"], (j - 1) * 2 if not isinstance(j, int) or j > 1 else 0)
            pool.sem_inc(N["pool_passed"], 1)
            g.indirect_dma_start(xg[b][:], None, h1_dram[0:T, :], bass.IndirectOffsetOnAxis(tix[b][:].bitcast(U32), 0),
                                 bounds_check=last_token, oob_is_err=False).then_inc(gathered[b], 16)

        def scatter(j, b):
            jj = slice(j, j + 1) if isinstance(j, int) else bass.ds(j, 1)
            wait(pool, scattered[b], (j - b) * 8)
            g.tensor_copy(dix[b][:], dstrow[:, jj])
            pool.drain()
            wait(pool, N["y_cp"], j * 2 + 2)
            pool.sem_inc(N["pool_passed"], 1)
            g.indirect_dma_start(ys[0:2 * T, :], bass.IndirectOffsetOnAxis(dix[b][:].bitcast(U32), 0), yt[b][:], None,
                                 bounds_check=last_row, oob_is_err=False).then_inc(scattered[b], 16)

        pairs_m1 = pool.value_load(npm1[0:1, 0:1], min_val=NE // 2 - 1, max_val=ITEMS // 2 - 1)
        gather(0, 0)
        gather(1, 1)
        gather(2, 0)
        scatter(0, 0)
        gather(3, 1)
        scatter(1, 1)
        with pool.Fori(1, pairs_m1) as i:
            gather(i * 2 + 2, 0)
            scatter(i * 2, 0)
            gather(i * 2 + 3, 1)
            scatter(i * 2 + 1, 1)
        scatter(pairs_m1 * 2, 0)
        scatter(pairs_m1 * 2 + 1, 1)

        pool.wait_ge(N["ln2_in"], 32)
        for n in range(NF):
            b = n % 2
            pool.wait_ge(N["fnorm_done"], n + 1)
            wait(pool, out_stored[b], 16 * (n // 2))
            g.tensor_tensor(zn[b][:], zz[b][:], g2[:], ALU.mult)
            pool.drain()
            g.tensor_tensor(zn[b][:], zn[b][:], b2[:], ALU.add).then_inc(N["f_out_done"], 1)
            pool.wait_ge(N["f_out_done"], n + 1)
            pool.dma_start(out[n * P:(n + 1) * P, :], zn[b][:]).then_inc(out_stored[b], 16)
        for b in range(2):
            pool.wait_ge(out_stored[b], 16 * (NF // 2))

    @block.scalar
    def _(act):
        a = nc.scalar
        act.sem_inc(N["bank_free"], 3)
        act.sem_inc(N["stage_free"], 3)

        def hi(g):
            if g:
                wait(act, raw_landed[g % 3], landed_count(g))
            wait(act, N["blk_mm"], NT * (g - 1))
            for part in range(2):
                if g == 0:
                    act.wait_ge(first_landed[part], 16)
                if g < 6:
                    c = slice(part * 2048, (part + 1) * 2048)
                    last = a.activation(whi[g % 2][:, c], raw[g % 3][:, c], ACT.Copy)
                else:
                    for k in range(4 * part, 4 * part + 4):
                        c = slice(k * 512, (k + 1) * 512)
                        last = a.activation(whi[g % 2][:, c], raw[g % 3][:, c], ACT.Copy, scale=hnw[:, k:k + 1])
                last.then_inc(N["hi_done"], 1)

        def x_hi(n):
            for q in (2 * n, 2 * n + 1):
                half = q % 2
                act.wait_ge(N["xT_mm"], q + 1)
                a.activation(xhi[:, 4 * half:4 * half + 4, n * L:(n + 1) * L], ps[4 + q % 4][:, 0:4 * L].rearrange("p (k t) -> p k t", k=4), ACT.Copy).then_inc(N["x_hi"], 1)

        def evac(u, s, func):
            wait(act, N["blk_mm"], u + 1)
            wait(act, N["stage_free"], u + 1)
            a.activation(stage[s][0:L, :], ps[s][0:L, :], func).then_inc(N["bank_free"], 1)

        x_hi(0)
        hi(0)
        x_hi(1)
        act.wait_ge(N["params"], 48)
        a.activation(wg_hi[:], wg_raw[:], ACT.Copy).then_inc(N["gate_l"], 1)
        for n in range(NT):
            if n + 2 < NT:
                x_hi(n + 2)
            if n == 4:
                hi(1)
            evac(n, n % 3, ACT.Sigmoid)
        act.wait_ge(N["gate_l"], 2)
        a.activation(gtmp[0:L], glf[0:L], ACT.Exp, scale=-1.0).then_inc(N["gate_l"], 1)
        act.wait_ge(N["gate_l"], 4)
        a.activation(gtmp[0:L], gtmp[0:L], ACT.Ln).then_inc(N["gate_l"], 1)
        hi(2)

        for i in range(2):
            for pos in range(2 * NT):
                evac(NT + 18 * i + pos, pos % 3, ACT.Copy)
                if pos % NT == NT - 1:
                    hi(2 * i + 3 + pos // NT)
        for n in range(NT):
            evac(5 * NT + n, n % 3, ACT.Sigmoid)

        act.wait_ge(N["m_rows"], 2)
        a.activation(gexp[0:L], garg[0:L], ACT.Exp)
        a.activation(wprev[:], warg[:], ACT.Exp).then_inc(N["m_rows"], 1)
        hi(7)

        def front(c):
            L3 = lambda t: t[:, 0:H * L]
            wait(act, N["t_mm"], c * 3 + 1)
            wait(act, N["s_mm"], c)
            a.activation(L3(qT), ps[4][:, 0:H * L], ACT.Copy, scale=QSCALE).then_inc(N["t_cp"], 1)
            wait(act, N["t_mm"], c * 3 + 2)
            a.activation(L3(kT), ps[5][:, 0:H * L], ACT.Copy).then_inc(N["t_cp"], 1)
            wait(act, N["t_mm"], c * 3 + 3)
            wait(act, N["n_mm"], c * 4)
            a.activation(L3(qsT), ps[6][:, 0:H * L], ACT.Copy).then_inc(N["t_cp"], 1)
            wait(act, N["e_mm"], c + 1)
            wait(act, N["sw_done"], c)
            for h in range(H):
                bias = ga[0:L, c, h:h + 1] if isinstance(c, int) else ga[0:L, bass.ds(c, 1), h:h + 1].rearrange("p n h -> p (n h)")
                last = a.activation(ew[0:L, h * L:(h + 1) * L], ps[7][0:L, h * L:(h + 1) * L], ACT.Exp, bias=bias)
            last.then_inc(N["ew_done"], 1)

        def copy_num(c):
            wait(act, N["gt_done"], c)
            for h in range(H):
                wait(act, N["n_mm"], c * 4 + (h + 1))
                a.activation(num[0:L, h, :], ps[5 + h % 2][0:L, 0:DV + 1], ACT.Copy).then_inc(N["num_done"], 1)

        def tail(c):
            for q in range(2):
                wait(act, N["ht_mm"], c * 2 + (q + 1))
                wait(act, N["lg_mm"], c)
                a.activation(h1T[:, 4 * q:4 * q + 4, :], ps[2 + q][:, 0:4 * L].rearrange("p (k t) -> p k t", k=4), ACT.Copy).then_inc(N["ht_cp"], 1)

        def back_split(c):
            for q in range(2):
                wait(act, N["ot_mm"], c * 2 + (q + 1))
                wait(act, N["y_mm"], c * 2)
                a.activation(ohi[:, 4 * q:4 * q + 4, :], ps[q][:, 0:4 * L].rearrange("p (k t) -> p k t", k=4), ACT.Copy).then_inc(N["o_hi"], 1)

        def scale(c):
            wait(act, N["gt_done"], c + 1)
            wait(act, N["ot_mm"], c * 2)
            for h in range(H):
                last = a.activation(gated[0:L, h, :], gt[0:L, h, :], ACT.Copy, scale=ep[0:L, 5, h:h + 1])
            last.then_inc(N["gated_done"], 1)

        front(0)
        copy_num(0)
        scale(0)
        front(1)
        back_split(0)
        copy_num(1)
        scale(1)
        with act.Fori(2, NT) as i:
            front(i)
            back_split(i - 1)
            tail(i - 2)
            copy_num(i)
            scale(i)
        back_split(NT - 1)
        tail(NT - 2)
        tail(NT - 1)

        def hi_expert(j, k):
            slot = (G0 + k) % 3
            wait(act, raw_landed[slot], j * 16 + landed_count(G0 + k))
            used, per = ((N["g_mm"], 1), (N["u2_mm"], 1), (N["y2_mm"], 2))[k]
            wait(act, used, j * per)
            for part in range(2):
                c = slice(part * 2048, (part + 1) * 2048)
                a.activation(whi[k][:, c], raw[slot][:, c], ACT.Copy).then_inc(N["hi_done"], 1)

        def xg_hi(j, b):
            for q in range(2):
                wait(act, N["xgT_mm"], j * 2 + (q + 1))
                if q == 0:
                    wait(act, N["u2_mm"], j - 1)
                a.activation(xghi[b][:, 4 * q:4 * q + 4, :].rearrange("p k t -> p (k t)"), ps[q][:], ACT.Copy).then_inc(N["xg_hi"], 1)

        def mid(j):
            wait(act, N["g_mm"], j + 1)
            wait(act, N["gu_done"], j)
            a.activation(sg[:], ps[2][:], ACT.Silu).then_inc(N["silu_done"], 1)
            wait(act, N["guT_mm"], j + 1)
            wait(act, N["y2_mm"], j * 2)
            a.activation(ghi[:].rearrange("p k t -> p (k t)"), ps[4][:], ACT.Copy).then_inc(N["g_hi"], 1)

        def y_out(j, b):
            wait(act, scattered[b], (j - b) * 8)
            for q in range(2):
                wait(act, N["y2_mm"], j * 2 + (q + 1))
                a.activation(yt[b][:, q * 512:(q + 1) * 512], ps[5 + q][:], ACT.Copy).then_inc(N["y_cp"], 1)

        act.wait_ge(N["y_mm"], 2 * NT)
        hi_expert(0, 0)
        hi_expert(0, 1)
        act.wait_ge(N["r_arg"], 2)
        a.activation(r_g4[0:L], r_g4[0:L], ACT.Exp)
        a.activation(r_s[0:L, 6, :], r_s[0:L, 5, :], ACT.Exp).then_inc(N["r_exp"], 1)
        act.wait_ge(N["routed"], 1)
        hi_expert(0, 2)
        xg_hi(0, 0)
        pairs_m1 = act.value_load(npm1[0:1, 0:1], min_val=NE // 2 - 1, max_val=ITEMS // 2 - 1)

        def item(j, b, last=False):
            if not last:
                hi_expert(j + 1, 0)
                xg_hi(j + 1, 1 - b)
            mid(j)
            if not last:
                hi_expert(j + 1, 1)
            y_out(j, b)
            if not last:
                hi_expert(j + 1, 2)

        item(0, 0)
        item(1, 1)
        with act.Fori(1, pairs_m1) as i:
            item(i * 2, 0)
            item(i * 2 + 1, 1)
        item(pairs_m1 * 2, 0)
        item(pairs_m1 * 2 + 1, 1, last=True)

        for n in range(NF):
            b = n % 2
            act.wait_ge(y_landed[b], 32 * (n // 2 + 1))
            wait(act, N["f_out_done"], n - 1)
            a.activation(zz[b][:], hh[b][:], ACT.Copy, scale=ALPHA).then_inc(N["y0_done"], 1)

    @block.vector
    def _(dve):
        v = nc.vector
        tt, ts, stt = v.tensor_tensor, v.tensor_scalar, v.scalar_tensor_tensor

        def rsqrt(y, x, tmp):
            ts(x, x, EPS, None, ALU.add)
            dve.drain()
            ts(y.bitcast(I32), x.bitcast(I32), 1, None, ALU.logical_shift_right)
            dve.drain()
            ts(y.bitcast(I32), y.bitcast(I32), -1.0, float(0x5F3759DF), ALU.mult, ALU.add)
            dve.drain()
            for _ in range(3):
                tt(tmp, y, y, ALU.mult)
                dve.drain()
                stt(tmp, tmp, -0.5, x, ALU.mult, ALU.mult)
                dve.drain()
                stt(y, tmp, 1.5, y, ALU.add, ALU.mult)
                dve.drain()

        def lo(g):
            for part in range(2):
                wait(dve, N["hi_done"], 2 * g + part + 1)
                if g < 6:
                    c = slice(part * 2048, (part + 1) * 2048)
                    last = tt(wlo[g % 2][:, c], raw[g % 3][:, c], whi[g % 2][:, c].bitcast(F32), ALU.subtract)
                else:
                    for k in range(4 * part, 4 * part + 4):
                        c = slice(k * 512, (k + 1) * 512)
                        last = stt(wlo[g % 2][:, c], raw[g % 3][:, c], hnw[:, k:k + 1], whi[g % 2][:, c].bitcast(F32), ALU.mult, ALU.subtract)
                last.then_inc(N["lo_done"], 1)

        def x_lo(n):
            for q in (2 * n, 2 * n + 1):
                half = q % 2
                dve.wait_ge(N["x_hi"], q + 1)
                cols = (slice(None), slice(4 * half, 4 * half + 4), slice(n * L, (n + 1) * L))
                tt(xlo[cols], ps[4 + q % 4][:, 0:4 * L].rearrange("p (k t) -> p k t", k=4), xhi[cols].bitcast(F32), ALU.subtract).then_inc(N["x_lo"], 1)

        x_lo(0)
        lo(0)
        x_lo(1)
        dve.wait_ge(N["gate_l"], 1)
        tt(wg_lo[:], wg_raw[:], wg_hi[:].bitcast(F32), ALU.subtract).then_inc(N["gate_mm"], 1)
        for n in range(2, NT):
            x_lo(n)
            if n == 6:
                lo(1)

        dve.wait_ge(N["gate_mm"], 2)
        tt(gts[0:L], ps[3][0:L, 0:NT * 2 * H].rearrange("p (n g) -> p n g", n=NT), bg[0:L].unsqueeze(1).to_broadcast([L, NT, 2 * H]), ALU.add)
        dve.drain()
        stt(glf[0:L], gts[0:L, :, H:2 * H], -1.0, gts[0:L, :, H:2 * H], ALU.mult, ALU.max).then_inc(N["gate_l"], 1)
        dve.wait_ge(N["gate_l"], 3)
        ts(gtmp[0:L], gtmp[0:L], 1.0, None, ALU.add).then_inc(N["gate_l"], 1)
        dve.wait_ge(N["gate_l"], 5)
        stt(glf[0:L], gts[0:L, :, H:2 * H], 0.0, gtmp[0:L], ALU.min, ALU.subtract).then_inc(N["a_rows"], 1)

        for g in range(2, 6):
            lo(g)
        dve.wait_ge(N["b_mm"], 1)
        v.tensor_copy(gb[0:L].rearrange("p n h -> p (n h)"), ps[6][0:L, 0:NT * H])
        dve.drain()
        tt(ga[0:L], gts[0:L, :, 0:H], gb[0:L], ALU.subtract).then_inc(N["a_rows"], 1)
        dve.wait_ge(N["aT_mm"], 1)
        v.tensor_copy(at_[:, 0:4, :].rearrange("p n t -> p (n t)"), ps[6][0:H, 0:4 * L])
        v.tensor_copy(at_[:, 4:8, :].rearrange("p n t -> p (n t)"), ps[7][0:H, 0:4 * L]).then_inc(N["aT_mm"], 1)
        dve.wait_ge(N["aT_mm"], 3)
        v.tensor_copy(at_[:, 8, :], ps[6][0:H, 0:L])
        v.tensor_copy(bl[:], ps[6][0:H, 480:480 + NT])
        v.memset(mcar[:, 0:1], 0.0)
        dve.drain()
        for n in range(NT):
            v.tensor_tensor_scan(cm[:, n, :], at_[:, n, :], at_[:, n, :], mcar[:, n:n + 1], ALU.max, ALU.max)
            dve.drain()
            tt(mcar[:, n + 1:n + 2], bl[:, n:n + 1], cm[:, n, L - 1:L], ALU.add)
            dve.drain()
        v.tensor_copy(mcl[:, 0:NT], mcar[:, 0:NT])
        v.tensor_copy(mcl[:, NT:2 * NT], cm[:, :, L - 1:L].rearrange("p n o -> p (n o)")).then_inc(N["m_rows"], 1)
        lo(6)
        dve.wait_ge(N["mb_mm"], 1)
        v.tensor_copy(gcm[0:L].rearrange("p n h -> p (n h)"), ps[6][0:L, 0:NT * H])
        v.tensor_copy(gmc[:].rearrange("p h n -> p (h n)"), ps[7][:, 0:H * 2 * NT])
        dve.drain()
        mprev = gmc[:, :, 0:NT].rearrange("p h n -> p n h")
        mlast = gmc[:, :, NT:2 * NT].rearrange("p h n -> p n h")
        tt(garg[0:L, 0], mprev[0:L], gcm[0:L], ALU.subtract)
        stt(garg[0:L, 1], gb[0:L], -1.0, gcm[0:L], ALU.mult, ALU.subtract)
        tt(garg[0:L, 2], ga[0:L], mlast[0:L], ALU.subtract)
        tt(warg[:], mprev, mlast, ALU.subtract).then_inc(N["m_rows"], 1)
        dve.wait_ge(N["m_rows"], 3)
        ts(gexp[0:L, 0], gexp[0:L, 0], QSCALE, None, ALU.mult).then_inc(N["gate_exp"], 1)
        lo(7)

        v.memset(cst[:], 0.0).then_inc(N["c_done"], 1)

        def front(c):
            wait(dve, N["s_mm"], c + 1)
            wait(dve, N["ew_done"], c + 1)
            wait(dve, N["n_mm"], c * 4)
            tt(sw[0:L, :], ps[4][0:L, 0:H * L], ew[0:L, :], ALU.mult).then_inc(N["sw_done"], 1)

        def state(c):
            cc = slice(c, c + 1) if isinstance(c, int) else bass.ds(c, 1)
            dve.drain()
            for h in range(H):
                wait(dve, N["u_mm"], c * 4 + (h + 1))
                stt(cst[:, h, :], cst[:, h, :], wprev[:, cc, h:h + 1].rearrange("p n h -> p (n h)"), ps[(7, 0)[h % 2]][:, 0:DV + 1], ALU.mult, ALU.add).then_inc(N["c_done"], 1)

        def tail(c):
            wait(dve, N["lg_mm"], c + 1)
            cc = slice(c, c + 1) if isinstance(c, int) else bass.ds(c, 1)
            tt(lg[0:L, cc, :].rearrange("p n g -> p (n g)"), ps[5][0:L, 0:GROUPS + NE], bgr[0:L, :], ALU.add).then_inc(N["lg_done"], 1)

        def back_split(c):
            for q in range(2):
                wait(dve, N["o_hi"], c * 2 + (q + 1))
                s = slice(4 * q, 4 * q + 4)
                tt(olo[:, s, :], ps[q][:, 0:4 * L].rearrange("p (k t) -> p k t", k=4), ohi[:, s, :].bitcast(F32), ALU.subtract).then_inc(N["o_lo"], 1)

        def head_norm(c):
            cc = slice(c, c + 1) if isinstance(c, int) else bass.ds(c, 1)
            wait(dve, N["num_done"], c * 4 + 4)
            for h in range(H):
                v.bn_stats(bst[0:L, h, :], num[0:L, h, 0:DV])
            den = num[0:L, :, DV:DV + 1].rearrange("p h o -> p (h o)")
            stt(ep[0:L, 0, :], den, -1.0, den, ALU.mult, ALU.max)
            dve.drain()
            for h in range(H):
                v.bn_aggr(bmv[0:L, h, :], bst[0:L, h, :])
            tt(ep[0:L, 1, :], ep[0:L, 0, :], gexp[0:L, 1, cc, :].rearrange("p n h -> p (n h)"), ALU.max)
            dve.drain()
            v.reciprocal(ep[0:L, 2, :], ep[0:L, 1, :])
            dve.drain()
            tt(ep[0:L, 3, :], ep[0:L, 2, :], ep[0:L, 2, :], ALU.mult)
            dve.drain()
            tt(ep[0:L, 4, :], ep[0:L, 3, :], bmv[0:L, :, 1:2].rearrange("p h o -> p (h o)"), ALU.mult)
            dve.drain()
            rsqrt(ep[0:L, 6, :], ep[0:L, 4, :], ep[0:L, 7, :])
            wait(dve, N["gated_done"], c)
            tt(ep[0:L, 5, :], ep[0:L, 6, :], ep[0:L, 2, :], ALU.mult)
            wait(dve, N["o_in"], c * 32 + 32)
            for h in range(H):
                last = stt(gt[0:L, h, :], num[0:L, h, 0:DV], bmv[0:L, h, 0:1], osig[0:L, h, :], ALU.subtract, ALU.mult)
            last.then_inc(N["gt_done"], 1)

        def residual(c, q):
            s = slice(q * 512, (q + 1) * 512)
            if q == 0:
                wait(dve, N["h_in"], c * 32 + 32)
                wait(dve, N["h1_done"], c)
            wait(dve, N["y_mm"], c * 2 + (q + 1))
            stt(z1[0:L, s], hres[0:L, s], ALPHA, ps[2 + q][0:L, :], ALU.mult, ALU.add).then_inc(N["z_done"], 1)

        def norm(c):
            dve.drain()
            for q in range(2):
                v.bn_stats(lst[0:L, q, :], z1[0:L, q * 512:(q + 1) * 512])
            dve.drain()
            v.bn_aggr(lmv[0:L, 0:2], lst[0:L, :, :].rearrange("p a b -> p (a b)"))
            dve.drain()
            rsqrt(lmv[0:L, 2:3], lmv[0:L, 1:2], lmv[0:L, 3:4])
            ts(z1[0:L, :], z1[0:L, :], lmv[0:L, 0:1], lmv[0:L, 2:3], ALU.subtract, ALU.mult).then_inc(N["ln_done"], 1)

        front(0)
        state(0)
        head_norm(0)
        dve.wait_ge(N["params"], 16 * 9)
        front(1)
        back_split(0)
        residual(0, 0)
        state(1)
        head_norm(1)
        residual(0, 1)
        norm(0)
        with dve.Fori(2, NT) as i:
            front(i)
            back_split(i - 1)
            tail(i - 2)
            residual(i - 1, 0)
            state(i)
            head_norm(i)
            residual(i - 1, 1)
            norm(i - 1)
        back_split(NT - 1)
        tail(NT - 2)
        residual(NT - 1, 0)
        residual(NT - 1, 1)
        norm(NT - 1)
        tail(NT - 1)

        def lo_expert(j, k):
            slot = (G0 + k) % 3
            for part in range(2):
                c = slice(part * 2048, (part + 1) * 2048)
                wait(dve, N["hi_done"], j * 6 + (2 * (G0 + k) + part + 1))
                tt(wlo[k][:, c], raw[slot][:, c], whi[k][:, c].bitcast(F32), ALU.subtract).then_inc(N["lo_done"], 1)

        lo_expert(0, 0)
        lo_expert(0, 1)

        dve.wait_ge(N["r_arg"], 1)
        dve.wait_ge(N["lg_done"], NT)

        def over_last(ap, k):
            return ap.unsqueeze(2).to_broadcast([ap.shape[0], ap.shape[1], k])

        def over_mid(ap, k):
            return ap.unsqueeze(1).to_broadcast([ap.shape[0], k, ap.shape[1]])

        def red(out, in_, op):
            v.tensor_reduce(out, in_, AX, op)

        i4 = over_mid(r_iota[0:L, 0:GROUPS], NT)
        i8 = over_mid(r_iota[0:L, 0:PER_GROUP], NT)
        gl = lg[0:L, :, 0:GROUPS]
        sc = lambda k: r_s[0:L, k, :]
        red(sc(0), gl, ALU.max)
        dve.drain()
        tt(r_eq4[0:L], gl, over_last(sc(0), GROUPS), ALU.is_lt)
        tt(r_g4[0:L], gl, over_last(sc(0), GROUPS), ALU.subtract)
        dve.drain()
        stt(r_eq4[0:L], r_eq4[0:L], 64.0, i4, ALU.mult, ALU.add)
        dve.drain()
        red(sc(1), r_eq4[0:L], ALU.min)
        dve.drain()
        tt(r_oh4[0:L], i4, over_last(sc(1), GROUPS), ALU.is_equal)
        dve.drain()
        tt(r_prod[0:L], lg[0:L, :, GROUPS:].rearrange("p n (g e) -> p n g e", g=GROUPS),
           r_oh4[0:L].unsqueeze(3).to_broadcast([L, NT, GROUPS, PER_GROUP]), ALU.mult)
        dve.drain()
        tt(r_prod[0:L, :, 0:2, :], r_prod[0:L, :, 0:2, :], r_prod[0:L, :, 2:4, :], ALU.add)
        dve.drain()
        tt(r_in[0:L], r_prod[0:L, :, 0, :], r_prod[0:L, :, 1, :], ALU.add)
        dve.drain()
        for k in range(2):
            red(sc(2 + k), r_in[0:L], ALU.max)
            dve.drain()
            tt(r_t8[0:L], r_in[0:L], over_last(sc(2 + k), PER_GROUP), ALU.is_lt)
            dve.drain()
            stt(r_t8[0:L], r_t8[0:L], 64.0, i8, ALU.mult, ALU.add)
            dve.drain()
            red(sc(7 + k), r_t8[0:L], ALU.min)
            dve.drain()
            tt(r_oh8[0:L, k], i8, over_last(sc(7 + k), PER_GROUP), ALU.is_equal)
            dve.drain()
            if k == 0:
                stt(r_in[0:L], r_oh8[0:L, 0], -3e38, r_in[0:L], ALU.mult, ALU.add)
                dve.drain()
        tt(sc(5), sc(3), sc(2), ALU.subtract).then_inc(N["r_arg"], 1)
        oh5 = r_oh[0:L].rearrange("p (k n) (g e) -> p k n g e", k=2, g=GROUPS)
        for k in range(2):
            for gg in range(GROUPS):
                tt(oh5[:, k, :, gg, :], r_oh8[0:L, k], r_oh4[0:L, :, gg:gg + 1].to_broadcast([L, NT, PER_GROUP]), ALU.mult)
        dve.drain()
        tt(r_oh[0:L], r_oh[0:L], over_last(r_kn[0:L, 2, :], NE), ALU.mult)
        dve.drain()
        tt(r_a[0:L, 0:NT, :], r_oh[0:L, 0:NT, :], r_oh[0:L, NT:, :], ALU.add)
        v.memset(r_acum[0:L, 0, :], 0.0)
        dve.drain()
        for n in range(NT):
            last = tt(r_acum[0:L, n + 1, :], r_acum[0:L, n, :], r_a[0:L, n, :], ALU.add)
            if n < NT - 1:
                dve.drain()
        last.then_inc(N["r_hot"], 1)
        dve.wait_ge(N["r_exp"], 1)
        red(sc(9), r_g4[0:L], ALU.add)
        ts(sc(10), sc(6), 1.0, None, ALU.add)
        dve.drain()
        tt(sc(9), sc(9), sc(10), ALU.mult)
        dve.drain()
        v.reciprocal(wts[0:L, :, 0], sc(9))
        dve.drain()
        tt(wts[0:L, :, 1], wts[0:L, :, 0], sc(6), ALU.mult)
        dve.wait_ge(N["rk_mm"], 1)
        v.tensor_copy(r_rk[0:L].rearrange("p n e -> p (n e)"), ps[2][0:L, 0:NT * NE])
        v.tensor_copy(r_cnt[:], ps[3][:, 0:NE])
        dve.drain()
        for k in range(2):
            tt(r_pr[0:L, k * NT:(k + 1) * NT, :], r_oh[0:L, k * NT:(k + 1) * NT, :], r_rk[0:L], ALU.mult)
        tt(r_ex8[:], r_cnt[:].unsqueeze(2).to_broadcast([P, NE, 8]), r_thr[:].unsqueeze(1).to_broadcast([P, NE, 8]), ALU.is_gt)
        dve.drain()
        red(r_kn[0:L, 3, :], r_pr[0:L], ALU.add)
        red(r_ex[:, 0, :], r_ex8[:], ALU.add)
        dve.drain()
        v.tensor_tensor_scan(r_ex[:, 1, :], r_ex[:, 0, :], r_ex[:, 0, :], 0.0, ALU.add, ALU.max)
        tt(r_c8[0:L], over_last(r_kn[0:L, 3, :], 8), r_thr[0:L].unsqueeze(1).to_broadcast([L, KN, 8]), ALU.is_ge)
        dve.drain()
        tt(r_ex[:, 2, :], r_ex[:, 1, :], r_ex[:, 0, :], ALU.subtract)
        red(r_kn[0:L, 4, :], r_c8[0:L], ALU.add)
        dve.drain()
        tt(r_pr[0:L], r_oh[0:L], over_mid(r_ex[0:L, 2, :], KN), ALU.mult)
        stt(r_kn[0:L, 5, :], r_kn[0:L, 4, :], -float(P), r_kn[0:L, 3, :], ALU.mult, ALU.add)
        for k in range(2):
            stt(r_kn[0:L, 6, k * NT:(k + 1) * NT], sc(1), float(PER_GROUP), sc(7 + k), ALU.mult, ALU.add)
        dve.drain()
        red(r_kn[0:L, 7, :], r_pr[0:L], ALU.add)
        ts(r_kn[0:L, 8, :], r_kn[0:L, 4, :], 1.0, None, ALU.min)
        tt(r_ohr[0:L], over_mid(r_iota[0:L, :], KN), over_last(r_kn[0:L, 5, :], P), ALU.is_equal)
        dve.drain()
        tt(r_kn[0:L, 9, :], r_kn[0:L, 4, :], r_kn[0:L, 7, :], ALU.add)
        dve.drain()
        stt(r_kn[0:L, 9, :], r_kn[0:L, 9, :], float(NE - 1), r_kn[0:L, 6, :], ALU.add, ALU.subtract)
        dve.drain()
        tt(r_kn[0:L, 9, :], r_kn[0:L, 9, :], r_kn[0:L, 8, :], ALU.mult)
        tt(r_kn[0:L, 3, :], r_kn[0:L, 1, :], r_kn[0:L, 2, :], ALU.mult)
        dve.drain()
        tt(r_kn[0:L, 9, :], r_kn[0:L, 9, :], r_kn[0:L, 6, :], ALU.add)
        dve.drain()
        tt(r_rhs[0:L], over_mid(r_iota[0:L, 0:ITEMS], KN), over_last(r_kn[0:L, 9, :], ITEMS), ALU.is_equal)
        dve.drain()
        tt(r_rhs[0:L], r_rhs[0:L], over_last(r_kn[0:L, 3, :], ITEMS), ALU.mult).then_inc(N["r_rhs_done"], 1)
        tt(r_cmp[:], r_iota[0:1, 0:EXTRA].unsqueeze(2).to_broadcast([1, EXTRA, NE]), over_mid(r_ex[0:1, 1, :], EXTRA), ALU.is_ge)
        v.tensor_copy(r_e[:, 0, 0:NE], r_iota[0:1, 0:NE])
        ts(r_e[:, 2, 0:1], r_ex[0:1, 1, NE - 1:NE], float(NE - 1), None, ALU.add)
        dve.drain()
        red(r_e[:, 1, 0:EXTRA], r_cmp[:], ALU.add)
        v.tensor_copy(npm1[:, 1:2], r_e[:, 2, 0:1])
        dve.drain()
        ts(r_e[:, 0, NE:], r_e[:, 1, 0:EXTRA], float(NE - 1), None, ALU.min)
        ts(npm1[:, 0:1], npm1[:, 1:2], 1, None, ALU.arith_shift_right)
        dve.drain()
        v.tensor_copy(eidx[:], r_e[:, 0, :])
        dve.wait_ge(N["v_mm"], 1)
        ts(r_v[:, 0, :], ps[2][:, 0:ITEMS], 0.5, 1e6, ALU.is_lt, ALU.mult)
        dve.drain()
        stt(r_v[:, 1, :], ps[2][:, 0:ITEMS], -1.0, r_v[:, 0, :], ALU.add, ALU.add)
        dve.drain()
        v.tensor_copy(dstrow[:], r_v[:, 1, :])
        dve.drain()
        ts(tokrow[:], dstrow[:], 1, None, ALU.arith_shift_right).then_inc(N["routed"], 1)

        def xg_lo(j, b):
            for q in range(2):
                wait(dve, N["xg_hi"], j * 2 + (q + 1))
                s = slice(4 * q, 4 * q + 4)
                tt(xglo[b][:, s, :].rearrange("p k t -> p (k t)"), ps[q][:], xghi[b][:, s, :].rearrange("p k t -> p (k t)").bitcast(F32), ALU.subtract).then_inc(N["xg_lo"], 1)

        def times_up(j):
            wait(dve, N["silu_done"], j + 1)
            wait(dve, N["u2_mm"], j + 1)
            tt(gu[:], sg[:], ps[3][:], ALU.mult).then_inc(N["gu_done"], 1)

        def hidden_lo(j):
            wait(dve, N["g_hi"], j + 1)
            tt(glo[:].rearrange("p k t -> p (k t)"), ps[4][:], ghi[:].rearrange("p k t -> p (k t)").bitcast(F32), ALU.subtract).then_inc(N["g_lo"], 1)

        lo_expert(0, 2)
        xg_lo(0, 0)
        pairs_m1 = dve.value_load(npm1[0:1, 0:1], min_val=NE // 2 - 1, max_val=ITEMS // 2 - 1)

        def item(j, b, last=False):
            if not last:
                lo_expert(j + 1, 0)
            times_up(j)
            if not last:
                xg_lo(j + 1, 1 - b)
            hidden_lo(j)
            if not last:
                lo_expert(j + 1, 1)
                lo_expert(j + 1, 2)

        item(0, 0)
        item(1, 1)
        with dve.Fori(1, pairs_m1) as i:
            item(i * 2, 0)
            item(i * 2 + 1, 1)
        item(pairs_m1 * 2, 0)
        item(pairs_m1 * 2 + 1, 1, last=True)

        dve.wait_ge(N["wts_in"], 16)
        for n in range(NF):
            b = n % 2
            dve.wait_ge(N["y0_done"], n + 1)
            stt(zz[b][:], yy[b][:, 0, :], wts2[:, n, 0:1], zz[b][:], ALU.mult, ALU.add)
            dve.drain()
            stt(zz[b][:], yy[b][:, 1, :], wts2[:, n, 1:2], zz[b][:], ALU.mult, ALU.add).then_inc(N["fsum_done"], 1)
            dve.drain()
            for q in range(2):
                v.bn_stats(fst[:, q, :], zz[b][:, q * 512:(q + 1) * 512])
            dve.drain()
            v.bn_aggr(fmv[:, 0:2], fst[:].rearrange("p a b -> p (a b)"))
            dve.drain()
            rsqrt(fmv[:, 2:3], fmv[:, 1:2], fmv[:, 3:4])
            ts(zz[b][:], zz[b][:], fmv[:, 0:1], fmv[:, 2:3], ALU.subtract, ALU.mult).then_inc(N["fnorm_done"], 1)

    @block.tensor
    def _(pe):
        t = nc.tensor

        def mm3(out, lh, ll, rh, rl, first, last):
            t.matmul(out, lh, rh, start=first, stop=False)
            t.matmul(out, lh, rl, start=False, stop=False)
            return t.matmul(out, ll, rh, start=False, stop=last)

        pe.wait_ge(N["consts"], 1)
        def x_T(n):
            pe.wait_ge(xt_landed[n % 2], 32 * (n // 2 + 1))
            xv = xt[n % 2][:].rearrange("p (m k) -> p k m", k=KC)
            for half in range(2):
                q = 2 * n + half
                wait(pe, N["x_lo"], q - 3)
                for k in range(4):
                    last = t.transpose(ps[4 + q % 4][:, k * L:(k + 1) * L], xv[0:L, 4 * half + k, :], ident[0:L, 0:L])
                last.then_inc(N["xT_mm"], 1)

        def project(u, n, s, slot):
            wh = whi[slot][:].rearrange("p (k n) -> p k n", k=KC)
            wl = wlo[slot][:].rearrange("p (k n) -> p k n", k=KC)
            wait(pe, N["bank_free"], u + 1)
            c = slice(n * L, (n + 1) * L)
            for k in range(KC):
                last = mm3(ps[s][0:L, :], xhi[:, k, c], xlo[:, k, c], wh[:, k, :], wl[:, k, :], k == 0, k == KC - 1)
            last.then_inc(N["blk_mm"], 1)

        def gates(n):
            c = slice(n * L, (n + 1) * L)
            for k in range(KC):
                last = mm3(ps[3][0:L, n * 8:(n + 1) * 8], xhi[:, k, c], xlo[:, k, c], wg_hi[:, k, :], wg_lo[:, k, :], k == 0, k == KC - 1)
            if n == NT - 1:
                last.then_inc(N["gate_mm"], 1)

        x_T(0)
        x_T(1)
        for n in range(NT):
            pe.wait_ge(N["x_lo"], 2 * n + 2)
            if n == 0:
                pe.wait_ge(N["lo_done"], 2)
            project(n, n, n % 3, 0)
            if n == 0:
                pe.wait_ge(N["gate_mm"], 1)
            gates(n)
            if n + 2 < NT:
                x_T(n + 2)
        with pe.Fori(0, 2) as i:
            for pos in range(2 * NT):
                if pos % NT == 0:
                    wait(pe, N["lo_done"], i * 4 + 2 * (2 + pos // NT))
                project(i * 18 + (NT + pos), pos % NT, pos % 3, 1 - pos // NT)

        def sums_of_log_f():
            pe.wait_ge(N["a_rows"], 1)
            t.matmul(ps[6][0:L, 0:NT * H], upto[0:L, :], glf[0:L].rearrange("p n h -> p (n h)"), start=True, stop=True).then_inc(N["b_mm"], 1)

        def a_by_head_0():
            pe.wait_ge(N["a_rows"], 2)
            for n in range(8):
                last = t.transpose(ps[6 + n // 4][0:H, (n % 4) * L:(n % 4 + 1) * L], ga[0:L, n, :], ident[0:L, 0:L])
            last.then_inc(N["aT_mm"], 1)

        def a_by_head_1():
            pe.wait_ge(N["aT_mm"], 2)
            t.transpose(ps[6][0:H, 0:L], ga[0:L, 8, :], ident[0:L, 0:L])
            for n in range(NT):
                last = t.matmul(ps[6][0:H, 480 + n:481 + n], glf[0:L, n, :], ones[0:L, 0:1], start=True, stop=True)
            last.then_inc(N["aT_mm"], 1)

        def maxima():
            pe.wait_ge(N["m_rows"], 1)
            for n in range(NT):
                t.transpose(ps[6][0:L, n * H:(n + 1) * H], cm[:, n, :], ident[0:H, 0:H])
            for h in range(H):
                last = t.matmul(ps[7][:, h * 2 * NT:(h + 1) * 2 * NT], selpos[:, h, :], mcl[:], start=True, stop=True)
            last.then_inc(N["mb_mm"], 1)

        pe.wait_ge(N["lo_done"], 12)
        between = {0: sums_of_log_f, 1: a_by_head_0, 2: a_by_head_1, 6: maxima}
        for n in range(NT):
            if n in between:
                between[n]()
            project(5 * NT + n, n, n % 3, 1)

        def transposes(c):
            wait(pe, N["qk_in"], c * 32 + 32)
            wait(pe, N["sw_done"], c)
            wait(pe, N["num_done"], c * 4)
            for h in range(H):
                last = t.transpose(ps[4][:, h * L:(h + 1) * L], qk[0:L, 0, h, :], ident[0:L, 0:L])
            last.then_inc(N["t_mm"], 1)
            for h in range(H):
                last = t.transpose(ps[5][:, h * L:(h + 1) * L], qk[0:L, 1, h, :], ident[0:L, 0:L])
            last.then_inc(N["t_mm"], 1)
            wait(pe, N["qs_done"], c * 2 + 2)
            for h in range(H):
                last = t.transpose(ps[6][:, h * L:(h + 1) * L], qs[0:L, h, :], ident[0:L, 0:L])
            last.then_inc(N["t_mm"], 1)

        def scores(c):
            wait(pe, N["c_done"], c * 4 + 1)
            for h in range(H):
                rhs = cm[:, c, :] if isinstance(c, int) else cm[:, bass.ds(c, 1), :].rearrange("p n t -> p (n t)")
                out_h = ps[7][0:L, h * L:(h + 1) * L]
                t.matmul(out_h, identb[0:L, :], maskb[0:L, :], start=True, stop=False)
                last = t.matmul(out_h, selneg[:, h, 0:L], rhs, start=False, stop=True)
            last.then_inc(N["e_mm"], 1)
            wait(pe, N["t_cp"], c * 3 + 2)
            for h in range(H):
                last = t.matmul(ps[4][0:L, h * L:(h + 1) * L], kT[:, h * L:(h + 1) * L], qT[:, h * L:(h + 1) * L], start=True, stop=True)
            last.then_inc(N["s_mm"], 1)

        def attend(c):
            wait(pe, N["sw_done"], c + 1)
            wait(pe, N["t_cp"], c * 3 + 3)
            wait(pe, N["v_in"], c * 32 + 32)
            wait(pe, N["lg_done"], c - 1)
            wait(pe, N["o_lo"], c * 2)
            if isinstance(c, int) and c == 0:
                pe.wait_ge(N["ones_ready"], 1)
            for h in range(H):
                wait(pe, N["num_done"], c * 4 + (h - 1))
                t.matmul(ps[5 + h % 2][0:L, 0:DV + 1], sw[0:L, h * L:(h + 1) * L], vext[0:L, h, :], start=True, stop=False)
                t.matmul(ps[5 + h % 2][0:L, 0:DV + 1], qsT[:, h * L:(h + 1) * L], cst[:, h, :], start=False, stop=True).then_inc(N["n_mm"], 1)
                wait(pe, N["c_done"], c * 4 + h)
                t.matmul(ps[(7, 0)[h % 2]][:, 0:DV + 1], ks[0:L, h, :], vext[0:L, h, :], start=True, stop=True).then_inc(N["u_mm"], 1)

        def gated_T(c):
            wait(pe, N["gated_done"], c + 1)
            wait(pe, N["c_done"], c * 4 + 5)
            gv = gated[:].rearrange("p h d -> p (h d)").rearrange("p (m k) -> p k m", k=KC)
            for q in range(2):
                for k in range(4):
                    last = t.transpose(ps[q][:, k * L:(k + 1) * L], gv[0:L, 4 * q + k, :], ident[0:L, 0:L])
                last.then_inc(N["ot_mm"], 1)

        def tail(c, i):
            wait(pe, N["h1_done"], c + 1)
            hv = h1t[:].rearrange("p (m k) -> p k m", k=KC)
            for q in range(2):
                for k in range(4):
                    last = t.transpose(ps[2 + q][:, k * L:(k + 1) * L], hv[0:L, 4 * q + k, :], ident[0:L, 0:L])
                last.then_inc(N["ht_mm"], 1)
            wait(pe, N["ht_cp"], c * 2 + 2)
            wait(pe, N["t_cp"], i * 3 + 3)
            if isinstance(i, int):
                wait(pe, N["num_done"], 4 * NT)
            for k in range(KC):
                last = t.matmul(ps[5][0:L, 0:GROUPS + NE], h1T[:, k, :], wgr[:, k, :], start=k == 0, stop=k == KC - 1)
            last.then_inc(N["lg_mm"], 1)

        def out_half(c, q):
            wait(pe, N["o_lo"], c * 2 + 2)
            wait(pe, N["z_done"], c * 2 + q - 1)
            wh = whi[q][:].rearrange("p (k n) -> p k n", k=KC)
            wl = wlo[q][:].rearrange("p (k n) -> p k n", k=KC)
            for k in range(KC):
                last = mm3(ps[2 + q][0:L, :], ohi[:, k, :], olo[:, k, :], wh[:, k, :], wl[:, k, :], k == 0, k == KC - 1)
            last.then_inc(N["y_mm"], 1)

        pe.wait_ge(N["bank_free"], 3 + 6 * NT)
        pe.wait_ge(N["gate_exp"], 1)
        transposes(0)
        scores(0)
        attend(0)
        transposes(1)
        scores(1)
        gated_T(0)
        pe.wait_ge(N["lo_done"], 2 * G0)
        out_half(0, 0)
        attend(1)
        out_half(0, 1)
        pe.wait_ge(N["params"], 16 * 9)
        with pe.Fori(2, NT) as i:
            transposes(i)
            scores(i)
            gated_T(i - 1)
            tail(i - 2, i)
            out_half(i - 1, 0)
            attend(i)
            out_half(i - 1, 1)
        gated_T(NT - 1)
        tail(NT - 2, NT - 1)
        out_half(NT - 1, 0)
        out_half(NT - 1, 1)
        tail(NT - 1, NT - 1)

        pe.wait_ge(N["r_hot"], 1)
        t.matmul(ps[2][0:L, 0:NT * NE], beforeb[0:L, :], r_a[0:L, 0:NT, :].rearrange("p n e -> p (n e)"), start=True, stop=False)
        t.matmul(ps[2][0:L, 0:NT * NE], onesb[0:L, 0:L], r_acum[0:L, 0:NT, :].rearrange("p n e -> p (n e)"), start=False, stop=True)
        t.matmul(ps[3][:, 0:NE], onesb[0:L, :], r_acum[0:L, NT, :], start=True, stop=True).then_inc(N["rk_mm"], 1)
        pe.wait_ge(N["r_rhs_done"], 1)
        for q in range(2 * NT):
            last = t.matmul(ps[2][:, 0:ITEMS], r_ohr[0:L, q, :], r_rhs[0:L, q, :], start=q == 0, stop=q == 2 * NT - 1)
        last.then_inc(N["v_mm"], 1)

        def rows_T(j, b):
            wait(pe, gathered[b], (j - b) * 8 + 16)
            wait(pe, N["xg_lo"], j * 2)
            xv = xg[b][:].rearrange("p (m k) -> p k m", k=KC)
            for q in range(2):
                for k in range(4):
                    last = t.transpose(ps[q][:, k * P:(k + 1) * P], xv[:, 4 * q + k, :], ident[:])
                last.then_inc(N["xgT_mm"], 1)

        def item(j, b, last_item=False):
            def up_or_gate(k, bank):
                wait(pe, N["lo_done"], j * 6 + 2 * (G0 + k + 1))
                wh = whi[k][:].rearrange("p (k n) -> p k n", k=KC)
                wl = wlo[k][:].rearrange("p (k n) -> p k n", k=KC)
                for kk in range(KC):
                    last = mm3(ps[bank][:], xghi[b][:, kk, :], xglo[b][:, kk, :], wh[:, kk, :], wl[:, kk, :], kk == 0, kk == KC - 1)
                return last

            wait(pe, N["xg_lo"], j * 2 + 2)
            wait(pe, N["silu_done"], j)
            up_or_gate(0, 2).then_inc(N["g_mm"], 1)
            if not last_item:
                rows_T(j + 1, 1 - b)
            wait(pe, N["gu_done"], j)
            up_or_gate(1, 3).then_inc(N["u2_mm"], 1)
            wait(pe, N["gu_done"], j + 1)
            wait(pe, N["g_lo"], j)
            gv = gu[:].rearrange("p (m k) -> p k m", k=FC)
            for k in range(FC):
                last = t.transpose(ps[4][:, k * P:(k + 1) * P], gv[:, k, :], ident[:])
            last.then_inc(N["guT_mm"], 1)
            wait(pe, N["lo_done"], j * 6 + 2 * (G0 + 3))
            wait(pe, N["g_lo"], j + 1)
            wait(pe, N["y_cp"], j * 2)
            wh = whi[2][:].rearrange("p (k n) -> p k n", k=FC)
            wl = wlo[2][:].rearrange("p (k n) -> p k n", k=FC)
            for q in range(2):
                c = slice(q * 512, (q + 1) * 512)
                for k in range(FC):
                    last = mm3(ps[5 + q][:], ghi[:, k, :], glo[:, k, :], wh[:, k, c], wl[:, k, c], k == 0, k == FC - 1)
                last.then_inc(N["y2_mm"], 1)

        pe.wait_ge(N["routed"], 1)
        rows_T(0, 0)
        pairs_m1 = pe.value_load(npm1[0:1, 0:1], min_val=NE // 2 - 1, max_val=ITEMS // 2 - 1)
        item(0, 0)
        item(1, 1)
        with pe.Fori(1, pairs_m1) as i:
            item(i * 2, 0)
            item(i * 2 + 1, 1)
        item(pairs_m1 * 2, 0)
        item(pairs_m1 * 2 + 1, 1, last_item=True)

    block.__exit__(None, None, None)
    dma_ok.__exit__(None, None, None)


_INS = ["w_in", "b_gates", "head_norm_w", "w_out", "ln1_g", "ln1_b", "w_group", "b_group", "w_router",
        "b_router", "w_gate", "w_up", "w_down", "ln2_g", "ln2_b"]


def kernel(x, meta_tokens, **params):
    import numpy as np
    import concourse.bacc as bacc
    from concourse.bass_utils import run_bass_kernel_spmd

    nc = bacc.Bacc("TRN2", target_bir_lowering=False, num_devices=1)
    x = np.asarray(x)
    rows = np.concatenate([np.asarray(meta_tokens), x[0], np.zeros((TP - T, D), x.dtype)])
    arrays = {"hcat": rows}
    args = [nc.dram_tensor("hcat", rows.shape, F32, kind="ExternalInput").ap()]
    for name in _INS:
        arrays["l0_" + name] = np.ascontiguousarray(params["l0_" + name])
        args.append(nc.dram_tensor("l0_" + name, arrays["l0_" + name].shape, F32, kind="ExternalInput").ap())
    out = nc.dram_tensor("out", (OUT_ROWS, D), F32, kind="ExternalOutput").ap()
    build(nc, *args, out)
    r = run_bass_kernel_spmd(nc, [arrays], core_ids=[0])
    return r.results[0]["out"].reshape(1, OUT_ROWS, D)
```

```python
import concourse.bass as bass
from concourse import mybir

F32 = mybir.dt.float32
F32R = mybir.dt.float32r
BF16 = mybir.dt.bfloat16
I32 = mybir.dt.int32
U32 = mybir.dt.uint32
ALU = mybir.AluOpType
ACT = mybir.ActivationFunctionType
AX = mybir.AxisListType.X

P = 128
D = 1024
KC = D // P
NMETA = 16
T = 1040
L = 116
NT = 9
TP = L * NT
H = 4
DQ = 128
DV = 256
QSCALE = DQ ** -0.5
ALPHA = 2.0 ** 0.25
EPS = 1e-5
NEG = -1e30
GROUPS = 4
PER_GROUP = 8
NE = 32
FE = 512
FC = FE // P
PIECE = 4096
EXTRA = 16
ITEMS = NE + EXTRA
OUT_ROWS = T - NMETA
NF = OUT_ROWS // P


def wait(eng, sem, value):
    if isinstance(value, int) and value <= 0:
        return
    eng.wait_ge(sem, value)


def is_tile(c):
    return not isinstance(c, int) or 0 <= c < NT


def rows_of(eng, c):
    if isinstance(c, int):
        return slice(c * L, c * L + L)
    return bass.ds(eng.snap(c * L), L)


def build(nc, hcat, w_in, b_gates, head_norm_w, w_out, ln1_g, ln1_b, w_group, b_group, w_router,
          b_router, w_gate, w_up, w_down, ln2_g, ln2_b, out):
    dma_ok = nc.allow_non_contiguous_dma(reason="small parameter vectors and gate columns")
    dma_ok.__enter__()

    proj = nc.dram_tensor("proj", (TP, 3072), F32).ap()
    h1_dram = nc.dram_tensor("h1_rows", (TP, D), F32).ap()
    ys = nc.dram_tensor("expert_rows", (2 * T, D), F32).ap()
    wts_dram = nc.dram_tensor("pair_weights", (TP, 2), F32).ap()

    base = (nc.sbuf_base + 63) // 64 * 64
    cursor = [base]

    def at(name, shape, dt=F32):
        n = 1
        for s in shape[1:]:
            n *= s
        t = nc.alloc_sbuf_tensor_at(name, list(shape), dt, offset=cursor[0])
        cursor[0] += (n * (2 if dt == BF16 else 4) + 31) // 32 * 32
        assert cursor[0] <= nc.sbuf_usable_end, (name, cursor[0])
        return t

    stream_base = cursor[0]
    raw = [at(f"raw{s}", [P, PIECE]) for s in range(3)]
    whi = [at(f"whi{s}", [P, PIECE], F32R) for s in range(2)]
    wlo = [at(f"wlo{s}", [P, PIECE], F32R) for s in range(2)]
    stream_end = cursor[0]
    ident = at("ident", [P, P])
    identb = at("identb", [P, L], BF16)
    maskb = at("maskb", [P, L], BF16)
    upto = at("upto", [P, L])
    beforeb = at("beforeb", [P, L], BF16)
    onesb = at("onesb", [P, P], BF16)
    ones = at("ones", [P, 2])
    selneg = at("selneg", [H, H, P])
    selpos = at("selpos", [H, H, P])
    hnw = at("hnw", [P, KC])
    wg_raw = at("wg_raw", [P, KC, 2 * H])
    wg_hi = at("wg_hi", [P, KC, 2 * H], F32R)
    wg_lo = at("wg_lo", [P, KC, 2 * H], F32R)
    bg = at("bg", [P, 2 * H])
    gts = at("gts", [P, NT, 2 * H])
    ga = at("ga", [P, NT, H])
    gb = at("gb", [P, NT, H])
    glf = at("glf", [P, NT, H])
    gtmp = at("gtmp", [P, NT, H])
    gcm = at("gcm", [P, NT, H])
    gmc = at("gmc", [P, H, 2 * NT])
    garg = at("garg", [P, 3, NT, H])
    gexp = at("gexp", [P, 3, NT, H])
    warg = at("warg", [P, NT, H])
    wprev = at("wprev", [P, NT, H])
    bl = at("bl", [H, NT])
    mcar = at("mcar", [H, NT + 1])
    mcl = at("mcl", [H, 2 * NT])
    cm = at("cm", [H, NT, L])
    lg = at("lg", [P, NT, GROUPS + NE])
    tokrow = at("tokrow", [P, ITEMS], I32)
    dstrow = at("dstrow", [P, ITEMS], I32)
    eidx = at("eidx", [1, ITEMS], I32)
    npm1 = at("npm1", [1, 4], I32)
    wts = at("wts", [P, NT, 2])
    wts2 = at("wts2", [P, NF, 2])
    region = cursor[0]

    xhi = at("xhi", [P, KC, TP], F32R)
    xlo = at("xlo", [P, KC, TP], F32R)
    xt_at = cursor[0]
    xt = [at(f"xt{i}", [P, D]) for i in range(2)]
    stage = [at(f"stage{i}", [P, 512]) for i in range(3)]
    cursor[0] = xt_at
    at_ = at("aT", [H, NT, L])

    cursor[0] = region
    qk = at("qk", [P, 2, H, DQ])
    vext = at("vext", [P, H, DV + 1])
    osig = at("osig", [P, H, DV])
    hres = at("hres", [P, D])
    qs = at("qs", [P, H, DQ])
    ks = at("ks", [P, H, DQ])
    qT = at("qT", [P, H * L])
    qsT = at("qsT", [P, H * L])
    kT = at("kT", [P, H * L])
    ew = at("ew", [P, H * L])
    sw = at("sw", [P, H * L])
    num = at("num", [P, H, DV + 1])
    cst = at("cst", [P, H, DV + 1])
    gt = at("gt", [P, H, DV])
    gated = at("gated", [P, H, DV])
    ohi = at("ohi", [P, KC, L], F32R)
    olo = at("olo", [P, KC, L], F32R)
    z1 = at("z1", [P, D])
    z1n = at("z1n", [P, D])
    h1t = at("h1t", [P, D])
    h1T = at("h1T", [P, KC, L])
    g1 = at("g1", [P, D])
    b1 = at("b1", [P, D])
    wgr = at("wgr", [P, KC, GROUPS + NE])
    bgr = at("bgr", [P, GROUPS + NE])
    bst = at("bst", [P, H, 6])
    bmv = at("bmv", [P, H, 2])
    ep = at("ep", [P, 8, H])
    lst = at("lst", [P, 2, 6])
    lmv = at("lmv", [P, 4])

    cursor[0] = region
    route_base = cursor[0]
    whi.append(at("whi2", [P, PIECE], F32R))
    wlo.append(at("wlo2", [P, PIECE], F32R))
    xg = [at(f"xg{i}", [P, D]) for i in range(2)]
    xghi = [at(f"xghi{i}", [P, KC, P], F32R) for i in range(2)]
    xglo = [at(f"xglo{i}", [P, KC, P], F32R) for i in range(2)]
    sg = at("sg", [P, FE])
    gu = at("gu", [P, FE])
    ghi = at("ghi", [P, FC, P], F32R)
    glo = at("glo", [P, FC, P], F32R)
    yt = [at(f"yt{i}", [P, D]) for i in range(2)]
    tix = [at(f"tix{i}", [P, 1], I32) for i in range(2)]
    dix = [at(f"dix{i}", [P, 1], I32) for i in range(2)]

    cursor[0] = route_base
    KN = 2 * NT
    r_iota = at("r_iota", [P, P])
    r_eq4 = at("r_eq4", [P, NT, GROUPS])
    r_oh4 = at("r_oh4", [P, NT, GROUPS])
    r_g4 = at("r_g4", [P, NT, GROUPS])
    r_prod = at("r_prod", [P, NT, GROUPS, PER_GROUP])
    r_in = at("r_in", [P, NT, PER_GROUP])
    r_t8 = at("r_t8", [P, NT, PER_GROUP])
    r_oh8 = at("r_oh8", [P, 2, NT, PER_GROUP])
    r_s = at("r_s", [P, 16, NT])
    r_kn = at("r_kn", [P, 10, KN])
    r_oh = at("r_oh", [P, KN, NE])
    r_pr = at("r_pr", [P, KN, NE])
    r_rk = at("r_rk", [P, NT, NE])
    r_cnt = at("r_cnt", [P, NE])
    r_ex8 = at("r_ex8", [P, NE, 8])
    r_ex = at("r_ex", [P, 4, NE])
    r_c8 = at("r_c8", [P, KN, 8])
    r_thr = at("r_thr", [P, 8])
    r_a = at("r_a", [P, NT + 1, NE], BF16)
    r_acum = at("r_acum", [P, NT + 1, NE], BF16)
    r_ohr = at("r_ohr", [P, KN, P], BF16)
    r_eq = at("r_eq", [P, KN, ITEMS], BF16)
    r_rhs = at("r_rhs", [P, 2, KN, ITEMS], BF16)
    r_val = at("r_val", [P, 2, KN])
    r_v = at("r_v", [P, 2, ITEMS])
    r_e = at("r_e", [1, 3, ITEMS])
    r_cmp = at("r_cmp", [1, EXTRA, NE])
    assert cursor[0] <= route_base + 2 * PIECE * 4

    cursor[0] = stream_base
    FB = 3
    yy = [at(f"yy{i}", [P, 2, D]) for i in range(FB)]
    hh = [at(f"hh{i}", [P, D]) for i in range(FB)]
    zz = [at(f"zz{i}", [P, D]) for i in range(FB)]
    zn = [at(f"zn{i}", [P, D]) for i in range(FB)]
    g2 = at("g2", [P, D])
    b2 = at("b2", [P, D])
    fst = at("fst", [P, 2, 6])
    fmv = [at(f"fmv{i}", [P, 4]) for i in range(FB)]
    assert cursor[0] <= stream_end

    ps = [nc.alloc_psum_tensor(f"bank{i}", [P, 512], F32) for i in range(8)]

    S = {}

    def sem(name):
        if name not in S:
            S[name] = nc.alloc_semaphore(name)
        return S[name]

    first_landed = [sem(f"first_landed{s}") for s in range(2)]
    raw_landed = [sem(f"raw_landed{s}") for s in range(3)]
    xt_landed = [sem(f"xt_landed{s}") for s in range(2)]
    gathered = [sem(f"gathered{s}") for s in range(2)]
    scattered = [sem(f"scattered{s}") for s in range(2)]
    y_landed = [sem(f"y_landed{s}") for s in range(3)]
    h_landed = [sem(f"h_landed{s}") for s in range(3)]
    out_stored = [sem(f"out_stored{s}") for s in range(3)]

    names = """params consts xT_mm x_hi x_lo gate_mm gate_l b_mm a_rows aT_mm m_rows mb_mm
        gate_exp hi_done lo_done blk_mm bank_free stored stage_free ones_ready sp_passed pool_passed
        qk_in v_in o_in h_in qs_done t_mm t_cp e_mm s_mm ew_done sw_done n_mm num_done u_mm
        c_done gt_done gated_done ot_mm o_hi o_lo y_mm z_done ln_done h1_done h1_stored ht_mm
        ht_cp lg_mm lg_done
        r_exp r_arg r_hot r_item rk_mm r_rhs_done v_mm routed wts_stored wts_in
        index_ready xgT_mm xg_hi xg_lo g_mm silu_done u2_mm gu_done guT_mm g_hi g_lo y2_mm y_cp
        ln2_in y0_done fsum_done fstat_done fnorm_done f_out_done""".split()
    N = {n: sem(n) for n in names}

    def piece_src(g):
        w, c = (w_in, (4, 0, 1, 2, 3, 5)[g]) if g < 6 else (w_out, g - 6)
        return w[:, c * 512:(c + 1) * 512].rearrange("(p k) n -> p k n", k=KC)

    def landed_count(g):
        return 16 * (g // 3 + (g % 3 > 0))

    gate_w = w_gate.rearrange("e (p k) n -> e p (k n)", k=KC)
    up_w = w_up.rearrange("e (p k) n -> e p (k n)", k=KC)
    down_w = w_down.rearrange("e (p k) n -> e p (k n)", k=FC)
    G0 = 8

    def split_count(j, k, final=False):
        if isinstance(j, int) and j == 0 and k == 0:
            return 2 * G0 + 2
        return j * 6 + (2 * G0 + 4 * k - 2 * final)

    def rows_load(eng, dst, src, s):
        eng.dma_start(dst[0:112], src[0:112]).then_inc(s, 16)
        eng.dma_start(dst[112:L], src[112:L]).then_inc(s, 16)

    block = nc.Block()
    block.__enter__()

    @block.sync
    def _(sp):
        def load_piece(g):
            wait(sp, N["lo_done"], 2 * (g - 2))
            sp.dma_start(raw[g % 3][:].rearrange("p (k n) -> p k n", k=KC), piece_src(g)).then_inc(raw_landed[g % 3], 16)

        def load_expert(j, e, k):
            g_slot = (G0 + k) % 3
            if isinstance(j, int) and j == 0:
                sp.wait_ge(N["lo_done"], 2 * (G0 + k - 2))
            else:
                sp.wait_ge(N["lo_done"], split_count(j - 1, k))
            src = (gate_w, up_w, down_w)[k]
            sp.dma_start(raw[g_slot][:], src[e, :, :] if isinstance(e, int) else src[bass.ds(e, 1), :, :].rearrange("e p n -> p (e n)")).then_inc(raw_landed[g_slot], 16)

        def load_x(n):
            wait(sp, N["xT_mm"], 2 * (n - 1))
            sp.dma_start(xt[n % 2][0:112, :], hcat[n * L:n * L + 112, :]).then_inc(xt_landed[n % 2], 16)
            sp.dma_start(xt[n % 2][112:L, :], hcat[n * L + 112:(n + 1) * L, :]).then_inc(xt_landed[n % 2], 16)

        load_x(0)
        load_x(1)
        for part in range(2):
            c = slice(part * 2048, (part + 1) * 2048)
            sp.dma_start(raw[0][:, c].rearrange("p (k n) -> p k n", k=4), piece_src(0)[:, 4 * part:4 * part + 4, :]).then_inc(first_landed[part], 16)
        vec = lambda v, n: v.rearrange("(a n) -> a n", a=1).to_broadcast([n, v.shape[0]])
        sp.dma_start(wg_raw[:], w_in[:, 3072:3072 + 2 * H].rearrange("(p k) n -> p k n", k=KC)).then_inc(N["params"], 16)
        sp.dma_start(bg[:], vec(b_gates, P)).then_inc(N["params"], 16)
        sp.dma_start(hnw[:], head_norm_w.rearrange("(p k) -> p k", k=KC)).then_inc(N["params"], 16)
        for n in range(2, NT):
            load_x(n)
            if n == 4:
                load_piece(1)
        for g in range(2, 8):
            load_piece(g)
        load_expert(0, 0, 0)

        def load_qk(c):
            rows = rows_of(sp, c)
            wait(sp, N["t_mm"], c * 3)
            sp.sem_inc(N["sp_passed"], 1)
            wait(sp, N["qs_done"], c * 2)
            rows_load(sp, qk[0:L].rearrange("p a h d -> p (a h d)"), proj[rows, 0:1024], N["qk_in"])

        def load_v(c):
            rows = rows_of(sp, c)
            wait(sp, N["u_mm"], c * 4)
            src = proj[rows, 1024:2048]
            for r0, r1 in ((0, 112), (112, L)):
                sp.dma_start(vext[r0:r1, :, 0:DV], src[r0:r1, :].rearrange("p (h d) -> p h d", h=H)).then_inc(N["v_in"], 16)

        def load_o(c):
            rows = rows_of(sp, c)
            wait(sp, N["gt_done"], c)
            rows_load(sp, osig[0:L].rearrange("p h d -> p (h d)"), proj[rows, 2048:3072], N["o_in"])

        def load_residual(c):
            rows = rows_of(sp, c)
            wait(sp, N["z_done"], c * 2)
            rows_load(sp, hres[0:L, :], hcat[rows, :], N["h_in"])

        sp.wait_ge(N["blk_mm"], 6 * NT)
        sp.wait_ge(N["stored"], 16 * 5 * NT)
        load_qk(0)
        load_v(0)
        sp.wait_ge(N["stored"], 16 * 6 * NT)
        load_o(0)
        load_qk(1)
        load_residual(0)
        sp.dma_start(g1[:], vec(ln1_g, P)).then_inc(N["params"], 16)
        sp.dma_start(b1[:], vec(ln1_b, P)).then_inc(N["params"], 16)
        sp.dma_start(wgr[:, :, 0:GROUPS], w_group.rearrange("(p k) n -> p k n", k=KC)).then_inc(N["params"], 16)
        sp.dma_start(wgr[:, :, GROUPS:], w_router.rearrange("(p k) n -> p k n", k=KC)).then_inc(N["params"], 16)
        sp.dma_start(bgr[:, 0:GROUPS], vec(b_group, P)).then_inc(N["params"], 16)
        sp.dma_start(bgr[:, GROUPS:], vec(b_router, P)).then_inc(N["params"], 16)
        load_v(1)
        load_expert(0, 0, 1)
        load_expert(0, 0, 2)
        load_qk(2)
        load_o(1)

        def body(i):
            load_v(i)
            if is_tile(i + 1):
                load_qk(i + 1)
            load_o(i)
            load_residual(i - 1)

        with sp.Fori(2, NT - 1) as i:
            body(i)
        body(NT - 1)
        load_residual(NT - 1)
        load_expert(1, 1, 0)

        sp.wait_ge(N["routed"], 1)
        pairs_m1 = sp.value_load(npm1[0:1, 0:1], min_val=NE // 2 - 1, max_val=ITEMS // 2 - 1)
        def expert_of(j):
            return sp.value_load(eidx[0:1, bass.ds(j, 1)], min_val=0, max_val=NE - 1)

        with sp.Fori(0, pairs_m1) as i:
            for par in range(2):
                j = i * 2 + (1 + par)
                e = expert_of(j)
                load_expert(j, e, 1)
                load_expert(i * 2 + (2 + par), expert_of(i * 2 + (2 + par)), 0)
                load_expert(j, e, 2)
        j = pairs_m1 * 2 + 1
        e = expert_of(j)
        load_expert(j, e, 1)
        load_expert(j, e, 2)

        sp.wait_ge(N["y2_mm"], pairs_m1 * 4 + 4)
        sp.dma_start(g2[:], vec(ln2_g, P)).then_inc(N["ln2_in"], 16)
        sp.dma_start(b2[:], vec(ln2_b, P)).then_inc(N["ln2_in"], 16)

        def load_h(n):
            t0 = NMETA + n * P
            wait(sp, N["fsum_done"], n - FB + 1)
            sp.dma_start(hh[n % FB][:], h1_dram[t0:t0 + P, :]).then_inc(h_landed[n % FB], 16)

        def load_y(n):
            t0 = NMETA + n * P
            sp.dma_start(yy[n % FB][:].rearrange("p a d -> p (a d)"), ys[2 * t0:2 * (t0 + P), :].rearrange("(p a) d -> p (a d)", a=2)).then_inc(y_landed[n % FB], 16)

        def store_out(n):
            sp.wait_ge(N["f_out_done"], n + 1)
            sp.dma_start(out[n * P:(n + 1) * P, :], zn[n % FB][:]).then_inc(out_stored[n % FB], 16)

        for n in range(FB):
            load_h(n)
        for s in range(2):
            sp.wait_ge(scattered[s], pairs_m1 * 16 + 16)
        for n in range(FB):
            load_y(n)
        for n in range(FB, NF):
            load_h(n)
            load_y(n)
            store_out(n - FB)
        for n in range(NF - FB, NF):
            store_out(n)
        for s in range(FB):
            sp.wait_ge(out_stored[s], 16 * len(range(s, NF, FB)))

    @block.gpsimd
    def _(pool):
        g = nc.gpsimd
        g.memset(ident[:], 0.0)
        g.memset(upto[:], 1.0)
        g.memset(selpos[:], 0.0)
        g.memset(selneg[:], 0.0)
        g.memset(onesb[:], 1.0)
        g.memset(identb[:], 0.0)
        g.memset(beforeb[:], 1.0)
        g.memset(maskb[:], 0.0)
        pool.drain()
        g.affine_select(out=ident[:], in_=ident[:], compare_op=ALU.not_equal, fill=1.0, base=0, pattern=[[-1, P]], channel_multiplier=1)
        g.affine_select(out=identb[:], in_=identb[:], compare_op=ALU.not_equal, fill=1.0, base=0, pattern=[[-1, L]], channel_multiplier=1)
        g.affine_select(out=upto[:], in_=upto[:], compare_op=ALU.is_ge, fill=0.0, base=0, pattern=[[1, L]], channel_multiplier=-1)
        g.affine_select(out=beforeb[:], in_=beforeb[:], compare_op=ALU.is_gt, fill=0.0, base=0, pattern=[[1, L]], channel_multiplier=-1)
        g.affine_select(out=maskb[:], in_=maskb[:], compare_op=ALU.is_ge, fill=NEG, base=0, pattern=[[1, L]], channel_multiplier=-1)
        g.affine_select(out=selpos[:], in_=selpos[:], compare_op=ALU.not_equal, fill=1.0, base=0, pattern=[[-1, H], [0, P]], channel_multiplier=1)
        g.affine_select(out=selneg[:], in_=selneg[:], compare_op=ALU.not_equal, fill=-1.0, base=0, pattern=[[-1, H], [0, P]], channel_multiplier=1)
        pool.drain()
        g.memset(ones[:], 1.0).then_inc(N["consts"], 1)

        def store(u, s, col):
            wait(pool, N["bank_free"], u + 4)
            n = s[1]
            pool.dma_start(proj[n * L:(n + 1) * L, col], stage[s[0]][0:L, :]).then_inc(N["stored"], 16)
            wait(pool, N["stored"], u * 16 + 16)
            pool.sem_inc(N["stage_free"], 1)

        for n in range(NT):
            store(n, (n % 3, n), slice(4 * 512, 5 * 512))
        with pool.Fori(0, 2) as i:
            for pos in range(2 * NT):
                store(i * 18 + (NT + pos), (pos % 3, pos % NT), bass.ds(pool.snap(i * 1024 + 512 * (pos // NT)), 512))
        for n in range(NT):
            store(5 * NT + n, (n % 3, n), slice(5 * 512, 6 * 512))

        pool.wait_ge(N["gate_exp"], 1)
        pool.wait_ge(N["blk_mm"], 6 * NT)
        g.memset(vext[:, :, DV:DV + 1], 1.0).then_inc(N["ones_ready"], 1)

        def by_tokens(c, which):
            cc = slice(c, c + 1) if isinstance(c, int) else bass.ds(c, 1)
            return gexp[0:L, which, cc, :].rearrange("p n h -> p (n h)").unsqueeze(2).to_broadcast([L, H, DQ])

        def scale_q(c):
            wait(pool, N["qk_in"], c * 32 + 32)
            wait(pool, N["t_mm"], c * 3)
            g.tensor_tensor(qs[0:L], qk[0:L, 0], by_tokens(c, 0), ALU.mult).then_inc(N["qs_done"], 1)

        def scale_k(c):
            wait(pool, N["u_mm"], c * 4)
            g.tensor_tensor(ks[0:L], qk[0:L, 1], by_tokens(c, 2), ALU.mult).then_inc(N["qs_done"], 1)

        def back(c):
            rows = rows_of(pool, c)
            wait(pool, N["ln_done"], c + 1)
            wait(pool, N["h1_stored"], c * 16)
            wait(pool, N["ht_mm"], c * 2)
            g.tensor_tensor(h1t[0:L, :], z1n[0:L, :], g1[0:L, :], ALU.mult)
            pool.drain()
            g.tensor_tensor(h1t[0:L, :], h1t[0:L, :], b1[0:L, :], ALU.add).then_inc(N["h1_done"], 1)
            wait(pool, N["h1_done"], c + 1)
            pool.dma_start(h1_dram[rows, :], h1t[0:L, :]).then_inc(N["h1_stored"], 16)

        def body(i):
            if is_tile(i + 1):
                scale_q(i + 1)
            if is_tile(i - 3):
                back(i - 3)
            if is_tile(i + 1):
                scale_k(i + 1)

        scale_q(0)
        scale_k(0)
        for i in range(3):
            body(i)
        pool.wait_ge(N["params"], 16 * 9)
        body(3)
        with pool.Fori(4, NT - 1) as i:
            body(i)
        for i in range(NT - 1, NT + 3):
            body(i)

        pool.wait_ge(N["lg_done"], NT)
        pool.wait_ge(N["h1_stored"], 16 * NT)
        g.iota(r_iota[:].bitcast(I32), [[1, P]], base=0, channel_multiplier=0)
        g.iota(r_thr[:].bitcast(I32), [[P, 8]], base=P, channel_multiplier=0)
        by_kn = lambda ap: ap.rearrange("p (k n) -> p k n", k=2)
        g.iota(by_kn(r_kn[0:L, 0, :]).bitcast(I32), [[1, 2], [0, NT]], base=1, channel_multiplier=2)
        g.iota(by_kn(r_kn[0:L, 1, :]).bitcast(I32), [[0, 2], [2 * L, NT]], base=0, channel_multiplier=0)
        pool.drain()
        g.tensor_copy(r_iota[:], r_iota[:].bitcast(I32))
        g.tensor_copy(r_thr[:], r_thr[:].bitcast(I32))
        g.tensor_copy(r_val[0:L, 0, :], r_kn[0:L, 0, :].bitcast(I32))
        g.tensor_copy(r_val[0:L, 1, :], r_kn[0:L, 1, :].bitcast(I32))
        g.memset(r_kn[0:L, 2, :], 1.0)
        pool.drain()
        for ap in (r_val[0:L, 0, :], r_val[0:L, 1, :], r_kn[0:L, 2, :]):
            last = g.affine_select(out=by_kn(ap), in_=by_kn(ap), compare_op=ALU.is_gt, fill=0.0, base=T,
                                   pattern=[[0, 2], [-L, NT]], channel_multiplier=-1)
        last.then_inc(N["r_arg"], 1)
        for b in range(2):
            g.memset(xg[b][:], 0.0)
        pool.wait_ge(N["r_item"], 1)
        g.tensor_tensor(r_rhs[0:L, 0], r_eq[0:L], r_val[0:L, 0, :].unsqueeze(2).to_broadcast([L, KN, ITEMS]), ALU.mult).then_inc(N["r_rhs_done"], 1)

        pool.wait_ge(N["routed"], 1)

        last_token, last_row = pool.to_reg(T - 1), pool.to_reg(2 * T - 1)

        def gather(j, b):
            jj = slice(j, j + 1) if isinstance(j, int) else bass.ds(j, 1)
            wait(pool, gathered[b], (j - b) * 8)
            g.tensor_copy(tix[b][:], tokrow[:, jj])
            pool.drain()
            wait(pool, N["xgT_mm"], (j - 1) * 2 if not isinstance(j, int) or j > 1 else 0)
            pool.sem_inc(N["pool_passed"], 1)
            g.indirect_dma_start(xg[b][:], None, h1_dram[0:T, :], bass.IndirectOffsetOnAxis(tix[b][:].bitcast(U32), 0),
                                 bounds_check=last_token, oob_is_err=False).then_inc(gathered[b], 16)

        def scatter(j, b):
            jj = slice(j, j + 1) if isinstance(j, int) else bass.ds(j, 1)
            wait(pool, scattered[b], (j - b) * 8)
            g.tensor_copy(dix[b][:], dstrow[:, jj])
            pool.drain()
            wait(pool, N["y_cp"], j * 2 + 2)
            pool.sem_inc(N["pool_passed"], 1)
            g.indirect_dma_start(ys[0:2 * T, :], bass.IndirectOffsetOnAxis(dix[b][:].bitcast(U32), 0), yt[b][:], None,
                                 bounds_check=last_row, oob_is_err=False).then_inc(scattered[b], 16)

        for j in range(4):
            gather(j, j % 2)
        pool.dma_start(wts_dram.rearrange("(n p) k -> p n k", p=L), wts[0:L, :, :]).then_inc(N["wts_stored"], 16)
        pool.wait_ge(N["wts_stored"], 16)
        pool.dma_start(wts2[:], wts_dram[NMETA:T, :].rearrange("(n p) k -> p n k", p=P)).then_inc(N["wts_in"], 16)
        for b in range(2):
            scatter(b, b)
            gather(4 + b, b)
        pairs_m2 = pool.value_load(npm1[0:1, 2:3], min_val=NE // 2 - 2, max_val=ITEMS // 2 - 2)
        with pool.Fori(1, pairs_m2) as i:
            for b in range(2):
                scatter(i * 2 + b, b)
                gather(i * 2 + (4 + b), b)
        for j in range(4):
            scatter(pairs_m2 * 2 + j, j % 2)

        pool.wait_ge(N["ln2_in"], 32)
        for n in range(NF):
            b = n % FB
            pool.wait_ge(N["fnorm_done"], n + 1)
            wait(pool, out_stored[b], 16 * (n // FB))
            g.tensor_tensor(zn[b][:], zn[b][:], g2[:], ALU.mult)
            pool.drain()
            g.tensor_tensor(zn[b][:], zn[b][:], b2[:], ALU.add).then_inc(N["f_out_done"], 1)

    @block.scalar
    def _(act):
        a = nc.scalar
        act.sem_inc(N["bank_free"], 3)
        act.sem_inc(N["stage_free"], 3)

        def hi(g):
            if g:
                wait(act, raw_landed[g % 3], landed_count(g))
            wait(act, N["blk_mm"], NT * (g - 1))
            for part in range(2):
                if g == 0:
                    act.wait_ge(first_landed[part], 16)
                if g < 6:
                    c = slice(part * 2048, (part + 1) * 2048)
                    last = a.activation(whi[g % 2][:, c], raw[g % 3][:, c], ACT.Copy)
                else:
                    for k in range(4 * part, 4 * part + 4):
                        c = slice(k * 512, (k + 1) * 512)
                        last = a.activation(whi[g % 2][:, c], raw[g % 3][:, c], ACT.Copy, scale=hnw[:, k:k + 1])
                last.then_inc(N["hi_done"], 1)

        def x_hi(n):
            for q in (2 * n, 2 * n + 1):
                half = q % 2
                act.wait_ge(N["xT_mm"], q + 1)
                a.activation(xhi[:, 4 * half:4 * half + 4, n * L:(n + 1) * L], ps[4 + q % 4][:, 0:4 * L].rearrange("p (k t) -> p k t", k=4), ACT.Copy).then_inc(N["x_hi"], 1)

        def evac(u, s, func):
            wait(act, N["blk_mm"], u + 1)
            wait(act, N["stage_free"], u + 1)
            a.activation(stage[s][0:L, :], ps[s][0:L, :], func).then_inc(N["bank_free"], 1)

        x_hi(0)
        hi(0)
        x_hi(1)
        act.wait_ge(N["params"], 48)
        a.activation(wg_hi[:], wg_raw[:], ACT.Copy).then_inc(N["gate_l"], 1)
        for n in range(NT):
            if n + 2 < NT:
                x_hi(n + 2)
            if n == 4:
                hi(1)
            evac(n, n % 3, ACT.Sigmoid)
        act.wait_ge(N["gate_l"], 2)
        a.activation(gtmp[0:L], glf[0:L], ACT.Exp, scale=-1.0).then_inc(N["gate_l"], 1)
        act.wait_ge(N["gate_l"], 4)
        a.activation(gtmp[0:L], gtmp[0:L], ACT.Ln).then_inc(N["gate_l"], 1)
        hi(2)

        for i in range(2):
            for pos in range(2 * NT):
                evac(NT + 18 * i + pos, pos % 3, ACT.Copy)
                if pos % NT == NT - 1:
                    hi(2 * i + 3 + pos // NT)
        for n in range(NT):
            evac(5 * NT + n, n % 3, ACT.Sigmoid)

        act.wait_ge(N["m_rows"], 2)
        a.activation(gexp[0:L], garg[0:L], ACT.Exp)
        a.activation(wprev[:], warg[:], ACT.Exp).then_inc(N["m_rows"], 1)

        def front(c):
            L3 = lambda t: t[:, 0:H * L]
            wait(act, N["t_mm"], c * 3 + 1)
            wait(act, N["s_mm"], c)
            a.activation(L3(qT), ps[4][:, 0:H * L], ACT.Copy, scale=QSCALE).then_inc(N["t_cp"], 1)
            wait(act, N["t_mm"], c * 3 + 2)
            a.activation(L3(kT), ps[5][:, 0:H * L], ACT.Copy).then_inc(N["t_cp"], 1)
            wait(act, N["t_mm"], c * 3 + 3)
            wait(act, N["n_mm"], c * 4)
            a.activation(L3(qsT), ps[6][:, 0:H * L], ACT.Copy).then_inc(N["t_cp"], 1)
            wait(act, N["e_mm"], c + 1)
            wait(act, N["sw_done"], c)
            for h in range(H):
                bias = ga[0:L, c, h:h + 1] if isinstance(c, int) else ga[0:L, bass.ds(c, 1), h:h + 1].rearrange("p n h -> p (n h)")
                last = a.activation(ew[0:L, h * L:(h + 1) * L], ps[7][0:L, h * L:(h + 1) * L], ACT.Exp, bias=bias)
            last.then_inc(N["ew_done"], 1)

        def copy_num(c):
            wait(act, N["gt_done"], c)
            for h in range(H):
                wait(act, N["n_mm"], c * 4 + (h + 1))
                a.activation(num[0:L, h, :], ps[5 + h % 2][0:L, 0:DV + 1], ACT.Copy).then_inc(N["num_done"], 1)

        def h1_T(c):
            for q in range(2):
                wait(act, N["ht_mm"], c * 2 + (q + 1))
                wait(act, N["lg_mm"], c)
                a.activation(h1T[:, 4 * q:4 * q + 4, :], ps[5 + q][:, 0:4 * L].rearrange("p (k t) -> p k t", k=4), ACT.Copy).then_inc(N["ht_cp"], 1)

        def back_split(c):
            for q in range(2):
                wait(act, N["ot_mm"], c * 2 + (q + 1))
                wait(act, N["y_mm"], c * 2)
                a.activation(ohi[:, 4 * q:4 * q + 4, :], ps[q][:, 0:4 * L].rearrange("p (k t) -> p k t", k=4), ACT.Copy).then_inc(N["o_hi"], 1)

        def scale(c):
            wait(act, N["gt_done"], c + 1)
            wait(act, N["ot_mm"], c * 2)
            for h in range(H):
                last = a.activation(gated[0:L, h, :], gt[0:L, h, :], ACT.Copy, scale=ep[0:L, 5, h:h + 1])
            last.then_inc(N["gated_done"], 1)

        def body(i):
            if is_tile(i):
                front(i)
            if isinstance(i, int) and i == 1:
                hi(7)
            if is_tile(i - 4):
                h1_T(i - 4)
            if is_tile(i - 1):
                scale(i - 1)
                back_split(i - 1)
            if is_tile(i):
                copy_num(i)

        for i in range(5):
            body(i)
        with act.Fori(5, NT) as i:
            body(i)
        for i in range(NT, NT + 3):
            body(i)

        def hi_expert(j, k):
            slot = (G0 + k) % 3
            wait(act, raw_landed[slot], j * 16 + landed_count(G0 + k))
            used, per = ((N["g_mm"], 1), (N["u2_mm"], 1), (N["y2_mm"], 2))[k]
            wait(act, used, j * per)
            for part in range(2):
                c = slice(part * 2048, (part + 1) * 2048)
                a.activation(whi[k][:, c], raw[slot][:, c], ACT.Copy).then_inc(N["hi_done"], 1)

        def xg_hi(j, b):
            for q in range(2):
                wait(act, N["xgT_mm"], j * 2 + (q + 1))
                if q == 0:
                    wait(act, N["u2_mm"], j - 1)
                a.activation(xghi[b][:, 4 * q:4 * q + 4, :].rearrange("p k t -> p (k t)"), ps[q][:], ACT.Copy).then_inc(N["xg_hi"], 1)

        def silu(j):
            wait(act, N["g_mm"], j + 1)
            wait(act, N["gu_done"], j)
            a.activation(sg[:], ps[2][:], ACT.Silu).then_inc(N["silu_done"], 1)

        def hidden_hi(j):
            wait(act, N["guT_mm"], j + 1)
            wait(act, N["y2_mm"], j * 2)
            a.activation(ghi[:].rearrange("p k t -> p (k t)"), ps[4][:], ACT.Copy).then_inc(N["g_hi"], 1)

        def y_out(j, b):
            wait(act, scattered[b], (j - b) * 8)
            for q in range(2):
                wait(act, N["y2_mm"], j * 2 + (q + 1))
                a.activation(yt[b][:, q * 512:(q + 1) * 512], ps[5 + q][:], ACT.Copy).then_inc(N["y_cp"], 1)

        act.wait_ge(N["y_mm"], 2 * NT)
        hi_expert(0, 0)
        hi_expert(0, 1)
        h1_T(NT - 1)
        act.wait_ge(N["r_arg"], 2)
        a.activation(r_g4[0:L], r_g4[0:L], ACT.Exp)
        a.activation(r_s[0:L, 6, :], r_s[0:L, 5, :], ACT.Exp).then_inc(N["r_exp"], 1)
        act.wait_ge(N["routed"], 1)
        xg_hi(0, 0)
        xg_hi(1, 1)
        silu(0)
        hi_expert(1, 0)
        hi_expert(0, 2)
        pairs_m1 = act.value_load(npm1[0:1, 0:1], min_val=NE // 2 - 1, max_val=ITEMS // 2 - 1)

        def item(j, b, ahead=2):
            if ahead:
                hi_expert(j + 1, 1)
            hidden_hi(j)
            if ahead == 2:
                xg_hi(j + 2, b)
            if ahead:
                silu(j + 1)
            if ahead == 2:
                hi_expert(j + 2, 0)
            y_out(j, b)
            if ahead:
                hi_expert(j + 1, 2)

        item(0, 0)
        item(1, 1)
        with act.Fori(1, pairs_m1) as i:
            item(i * 2, 0)
            item(i * 2 + 1, 1)
        item(pairs_m1 * 2, 0, ahead=1)
        item(pairs_m1 * 2 + 1, 1, ahead=0)

        def residual2(n):
            b = n % FB
            act.wait_ge(h_landed[b], 16 * (n // FB + 1))
            wait(act, N["fnorm_done"], n - FB + 1)
            a.activation(zz[b][:], hh[b][:], ACT.Copy, scale=ALPHA).then_inc(N["y0_done"], 1)

        for n in range(FB):
            residual2(n)
        for n in range(NF):
            b = n % FB
            act.wait_ge(N["fstat_done"], n + 1)
            wait(act, out_stored[b], 16 * (n // FB))
            a.activation(zn[b][:], zz[b][:], ACT.Identity, bias=fmv[b][:, 3:4], scale=fmv[b][:, 2:3]).then_inc(N["fnorm_done"], 1)
            if n + FB < NF:
                residual2(n + FB)

    @block.vector
    def _(dve):
        v = nc.vector
        tt, ts, stt = v.tensor_tensor, v.tensor_scalar, v.scalar_tensor_tensor

        def rsqrt(y, x, tmp):
            ts(x, x, EPS, None, ALU.add)
            dve.drain()
            ts(y.bitcast(I32), x.bitcast(I32), 1, None, ALU.logical_shift_right)
            dve.drain()
            ts(y.bitcast(I32), y.bitcast(I32), -1.0, float(0x5F3759DF), ALU.mult, ALU.add)
            dve.drain()
            for _ in range(3):
                tt(tmp, y, y, ALU.mult)
                dve.drain()
                stt(tmp, tmp, -0.5, x, ALU.mult, ALU.mult)
                dve.drain()
                stt(y, tmp, 1.5, y, ALU.add, ALU.mult)
                dve.drain()

        def rsqrt_column(y, x, tmp):
            ts(x, x, EPS, None, ALU.add)
            dve.drain()
            ts(y.bitcast(I32), x.bitcast(I32), 1, None, ALU.logical_shift_right)
            ts(x, x, -0.5, None, ALU.mult)
            dve.drain()
            ts(y.bitcast(I32), y.bitcast(I32), -1.0, float(0x5F3759DF), ALU.mult, ALU.add)
            dve.drain()
            for _ in range(3):
                stt(tmp, y, y, x, ALU.mult, ALU.mult)
                dve.drain()
                stt(y, tmp, 1.5, y, ALU.add, ALU.mult)
                dve.drain()

        def lo(g):
            for part in range(2):
                wait(dve, N["hi_done"], 2 * g + part + 1)
                if g < 6:
                    c = slice(part * 2048, (part + 1) * 2048)
                    last = tt(wlo[g % 2][:, c], raw[g % 3][:, c], whi[g % 2][:, c].bitcast(F32), ALU.subtract)
                else:
                    for k in range(4 * part, 4 * part + 4):
                        c = slice(k * 512, (k + 1) * 512)
                        last = stt(wlo[g % 2][:, c], raw[g % 3][:, c], hnw[:, k:k + 1], whi[g % 2][:, c].bitcast(F32), ALU.mult, ALU.subtract)
                last.then_inc(N["lo_done"], 1)

        def x_lo(n):
            for q in (2 * n, 2 * n + 1):
                half = q % 2
                dve.wait_ge(N["x_hi"], q + 1)
                cols = (slice(None), slice(4 * half, 4 * half + 4), slice(n * L, (n + 1) * L))
                tt(xlo[cols], ps[4 + q % 4][:, 0:4 * L].rearrange("p (k t) -> p k t", k=4), xhi[cols].bitcast(F32), ALU.subtract).then_inc(N["x_lo"], 1)

        x_lo(0)
        lo(0)
        x_lo(1)
        dve.wait_ge(N["gate_l"], 1)
        tt(wg_lo[:], wg_raw[:], wg_hi[:].bitcast(F32), ALU.subtract).then_inc(N["gate_mm"], 1)
        for n in range(2, NT):
            x_lo(n)
            if n == 6:
                lo(1)

        dve.wait_ge(N["gate_mm"], 2)
        tt(gts[0:L], ps[3][0:L, 0:NT * 2 * H].rearrange("p (n g) -> p n g", n=NT), bg[0:L].unsqueeze(1).to_broadcast([L, NT, 2 * H]), ALU.add)
        dve.drain()
        stt(glf[0:L], gts[0:L, :, H:2 * H], -1.0, gts[0:L, :, H:2 * H], ALU.mult, ALU.max).then_inc(N["gate_l"], 1)
        dve.wait_ge(N["gate_l"], 3)
        ts(gtmp[0:L], gtmp[0:L], 1.0, None, ALU.add).then_inc(N["gate_l"], 1)
        dve.wait_ge(N["gate_l"], 5)
        stt(glf[0:L], gts[0:L, :, H:2 * H], 0.0, gtmp[0:L], ALU.min, ALU.subtract).then_inc(N["a_rows"], 1)

        for g in range(2, 6):
            lo(g)
        dve.wait_ge(N["b_mm"], 1)
        v.tensor_copy(gb[0:L].rearrange("p n h -> p (n h)"), ps[6][0:L, 0:NT * H])
        dve.drain()
        tt(ga[0:L], gts[0:L, :, 0:H], gb[0:L], ALU.subtract).then_inc(N["a_rows"], 1)
        dve.wait_ge(N["aT_mm"], 1)
        v.tensor_copy(at_[:, 0:4, :].rearrange("p n t -> p (n t)"), ps[6][0:H, 0:4 * L])
        v.tensor_copy(at_[:, 4:8, :].rearrange("p n t -> p (n t)"), ps[7][0:H, 0:4 * L]).then_inc(N["aT_mm"], 1)
        dve.wait_ge(N["aT_mm"], 3)
        v.tensor_copy(at_[:, 8, :], ps[6][0:H, 0:L])
        v.tensor_copy(bl[:], ps[6][0:H, 480:480 + NT])
        v.memset(mcar[:, 0:1], 0.0)
        dve.drain()
        for n in range(NT):
            v.tensor_tensor_scan(cm[:, n, :], at_[:, n, :], at_[:, n, :], mcar[:, n:n + 1], ALU.max, ALU.max)
            dve.drain()
            tt(mcar[:, n + 1:n + 2], bl[:, n:n + 1], cm[:, n, L - 1:L], ALU.add)
            dve.drain()
        v.tensor_copy(mcl[:, 0:NT], mcar[:, 0:NT])
        v.tensor_copy(mcl[:, NT:2 * NT], cm[:, :, L - 1:L].rearrange("p n o -> p (n o)")).then_inc(N["m_rows"], 1)
        lo(6)
        dve.wait_ge(N["mb_mm"], 1)
        v.tensor_copy(gcm[0:L].rearrange("p n h -> p (n h)"), ps[6][0:L, 0:NT * H])
        v.tensor_copy(gmc[:].rearrange("p h n -> p (h n)"), ps[7][:, 0:H * 2 * NT])
        dve.drain()
        mprev = gmc[:, :, 0:NT].rearrange("p h n -> p n h")
        mlast = gmc[:, :, NT:2 * NT].rearrange("p h n -> p n h")
        tt(garg[0:L, 0], mprev[0:L], gcm[0:L], ALU.subtract)
        stt(garg[0:L, 1], gb[0:L], -1.0, gcm[0:L], ALU.mult, ALU.subtract)
        tt(garg[0:L, 2], ga[0:L], mlast[0:L], ALU.subtract)
        tt(warg[:], mprev, mlast, ALU.subtract).then_inc(N["m_rows"], 1)
        dve.wait_ge(N["m_rows"], 3)
        ts(gexp[0:L, 0], gexp[0:L, 0], QSCALE, None, ALU.mult).then_inc(N["gate_exp"], 1)

        dve.wait_ge(N["blk_mm"], 6 * NT)
        v.memset(cst[:], 0.0).then_inc(N["c_done"], 1)

        def front(c):
            wait(dve, N["s_mm"], c + 1)
            wait(dve, N["ew_done"], c + 1)
            wait(dve, N["n_mm"], c * 4)
            tt(sw[0:L, :], ps[4][0:L, 0:H * L], ew[0:L, :], ALU.mult).then_inc(N["sw_done"], 1)

        def state(c):
            cc = slice(c, c + 1) if isinstance(c, int) else bass.ds(c, 1)
            dve.drain()
            for h in range(H):
                wait(dve, N["u_mm"], c * 4 + (h + 1))
                stt(cst[:, h, :], cst[:, h, :], wprev[:, cc, h:h + 1].rearrange("p n h -> p (n h)"), ps[(7, 0)[h % 2]][:, 0:DV + 1], ALU.mult, ALU.add).then_inc(N["c_done"], 1)

        def logits(c):
            wait(dve, N["lg_mm"], c + 1)
            cc = slice(c, c + 1) if isinstance(c, int) else bass.ds(c, 1)
            tt(lg[0:L, cc, :].rearrange("p n g -> p (n g)"), ps[1][0:L, 0:GROUPS + NE], bgr[0:L, :], ALU.add).then_inc(N["lg_done"], 1)

        def back_split(c):
            for q in range(2):
                wait(dve, N["o_hi"], c * 2 + (q + 1))
                s = slice(4 * q, 4 * q + 4)
                tt(olo[:, s, :], ps[q][:, 0:4 * L].rearrange("p (k t) -> p k t", k=4), ohi[:, s, :].bitcast(F32), ALU.subtract).then_inc(N["o_lo"], 1)

        def head_norm(c):
            cc = slice(c, c + 1) if isinstance(c, int) else bass.ds(c, 1)
            wait(dve, N["num_done"], c * 4 + 4)
            for h in range(H):
                v.bn_stats(bst[0:L, h, :], num[0:L, h, 0:DV])
            den = num[0:L, :, DV:DV + 1].rearrange("p h o -> p (h o)")
            stt(ep[0:L, 0, :], den, -1.0, den, ALU.mult, ALU.max)
            dve.drain()
            for h in range(H):
                v.bn_aggr(bmv[0:L, h, :], bst[0:L, h, :])
            tt(ep[0:L, 1, :], ep[0:L, 0, :], gexp[0:L, 1, cc, :].rearrange("p n h -> p (n h)"), ALU.max)
            dve.drain()
            v.reciprocal(ep[0:L, 2, :], ep[0:L, 1, :])
            dve.drain()
            tt(ep[0:L, 3, :], ep[0:L, 2, :], ep[0:L, 2, :], ALU.mult)
            dve.drain()
            tt(ep[0:L, 4, :], ep[0:L, 3, :], bmv[0:L, :, 1:2].rearrange("p h o -> p (h o)"), ALU.mult)
            dve.drain()
            rsqrt(ep[0:L, 6, :], ep[0:L, 4, :], ep[0:L, 7, :])
            wait(dve, N["gated_done"], c)
            tt(ep[0:L, 5, :], ep[0:L, 6, :], ep[0:L, 2, :], ALU.mult)
            wait(dve, N["o_in"], c * 32 + 32)
            for h in range(H):
                last = stt(gt[0:L, h, :], num[0:L, h, 0:DV], bmv[0:L, h, 0:1], osig[0:L, h, :], ALU.subtract, ALU.mult)
            last.then_inc(N["gt_done"], 1)

        def residual(c, q):
            s = slice(q * 512, (q + 1) * 512)
            if q == 0:
                wait(dve, N["ln_done"], c)
                wait(dve, N["h_in"], c * 32 + 32)
            wait(dve, N["y_mm"], c * 2 + (q + 1))
            stt(z1[0:L, s], hres[0:L, s], ALPHA, ps[2 + q][0:L, :], ALU.mult, ALU.add).then_inc(N["z_done"], 1)

        def row_stats(c):
            dve.drain()
            for q in range(2):
                v.bn_stats(lst[0:L, q, :], z1[0:L, q * 512:(q + 1) * 512])

        def norm(c):
            v.bn_aggr(lmv[0:L, 0:2], lst[0:L, :, :].rearrange("p a b -> p (a b)"))
            dve.drain()
            rsqrt_column(lmv[0:L, 2:3], lmv[0:L, 1:2], lmv[0:L, 3:4])
            wait(dve, N["h1_done"], c)
            ts(z1n[0:L, :], z1[0:L, :], lmv[0:L, 0:1], lmv[0:L, 2:3], ALU.subtract, ALU.mult).then_inc(N["ln_done"], 1)

        def body(i):
            if is_tile(i - 1):
                head_norm(i - 1)
            if is_tile(i):
                front(i)
            if isinstance(i, int) and i == 1:
                lo(7)
            if is_tile(i - 3):
                dve.drain()
                norm(i - 3)
            if is_tile(i - 2):
                residual(i - 2, 0)
            if is_tile(i - 4):
                logits(i - 4)
            if is_tile(i - 2):
                residual(i - 2, 1)
            if is_tile(i - 1):
                back_split(i - 1)
            if is_tile(i - 2):
                row_stats(i - 2)
            if is_tile(i):
                state(i)

        for i in range(5):
            body(i)
            if i == 1:
                dve.wait_ge(N["params"], 16 * 9)
        with dve.Fori(5, NT) as i:
            body(i)
        for i in range(NT, NT + 3):
            body(i)

        def lo_expert(j, k, final=False):
            slot = (G0 + k) % 3
            for part in range(2):
                c = slice(part * 2048, (part + 1) * 2048)
                wait(dve, N["hi_done"], split_count(j, k, final) + (part - 1))
                tt(wlo[k][:, c], raw[slot][:, c], whi[k][:, c].bitcast(F32), ALU.subtract).then_inc(N["lo_done"], 1)

        lo_expert(0, 0)
        lo_expert(0, 1)
        logits(NT - 1)

        dve.wait_ge(N["r_arg"], 1)
        dve.wait_ge(N["lg_done"], NT)

        def over_last(ap, k):
            return ap.unsqueeze(2).to_broadcast([ap.shape[0], ap.shape[1], k])

        def over_mid(ap, k):
            return ap.unsqueeze(1).to_broadcast([ap.shape[0], k, ap.shape[1]])

        def red(out, in_, op):
            v.tensor_reduce(out, in_, AX, op)

        i4 = over_mid(r_iota[0:L, 0:GROUPS], NT)
        i8 = over_mid(r_iota[0:L, 0:PER_GROUP], NT)
        gl = lg[0:L, :, 0:GROUPS]
        sc = lambda k: r_s[0:L, k, :]
        red(sc(0), gl, ALU.max)
        dve.drain()
        tt(r_eq4[0:L], gl, over_last(sc(0), GROUPS), ALU.is_lt)
        tt(r_g4[0:L], gl, over_last(sc(0), GROUPS), ALU.subtract)
        dve.drain()
        stt(r_eq4[0:L], r_eq4[0:L], 64.0, i4, ALU.mult, ALU.add)
        dve.drain()
        red(sc(1), r_eq4[0:L], ALU.min)
        dve.drain()
        tt(r_oh4[0:L], i4, over_last(sc(1), GROUPS), ALU.is_equal)
        dve.drain()
        tt(r_prod[0:L], lg[0:L, :, GROUPS:].rearrange("p n (g e) -> p n g e", g=GROUPS),
           r_oh4[0:L].unsqueeze(3).to_broadcast([L, NT, GROUPS, PER_GROUP]), ALU.mult)
        dve.drain()
        tt(r_prod[0:L, :, 0:2, :], r_prod[0:L, :, 0:2, :], r_prod[0:L, :, 2:4, :], ALU.add)
        dve.drain()
        tt(r_in[0:L], r_prod[0:L, :, 0, :], r_prod[0:L, :, 1, :], ALU.add)
        dve.drain()
        for k in range(2):
            red(sc(2 + k), r_in[0:L], ALU.max)
            dve.drain()
            tt(r_t8[0:L], r_in[0:L], over_last(sc(2 + k), PER_GROUP), ALU.is_lt)
            dve.drain()
            stt(r_t8[0:L], r_t8[0:L], 64.0, i8, ALU.mult, ALU.add)
            dve.drain()
            red(sc(7 + k), r_t8[0:L], ALU.min)
            dve.drain()
            tt(r_oh8[0:L, k], i8, over_last(sc(7 + k), PER_GROUP), ALU.is_equal)
            dve.drain()
            if k == 0:
                stt(r_in[0:L], r_oh8[0:L, 0], -3e38, r_in[0:L], ALU.mult, ALU.add)
                dve.drain()
        tt(sc(5), sc(3), sc(2), ALU.subtract).then_inc(N["r_arg"], 1)
        oh5 = r_oh[0:L].rearrange("p (k n) (g e) -> p k n g e", k=2, g=GROUPS)
        for k in range(2):
            for gg in range(GROUPS):
                tt(oh5[:, k, :, gg, :], r_oh8[0:L, k], r_oh4[0:L, :, gg:gg + 1].to_broadcast([L, NT, PER_GROUP]), ALU.mult)
        dve.drain()
        tt(r_oh[0:L], r_oh[0:L], over_last(r_kn[0:L, 2, :], NE), ALU.mult)
        dve.drain()
        tt(r_a[0:L, 0:NT, :], r_oh[0:L, 0:NT, :], r_oh[0:L, NT:, :], ALU.add)
        v.memset(r_acum[0:L, 0, :], 0.0)
        dve.drain()
        for n in range(NT):
            last = tt(r_acum[0:L, n + 1, :], r_acum[0:L, n, :], r_a[0:L, n, :], ALU.add)
            if n < NT - 1:
                dve.drain()
        last.then_inc(N["r_hot"], 1)
        dve.wait_ge(N["r_exp"], 1)
        red(sc(9), r_g4[0:L], ALU.add)
        ts(sc(10), sc(6), 1.0, None, ALU.add)
        dve.drain()
        tt(sc(9), sc(9), sc(10), ALU.mult)
        dve.drain()
        v.reciprocal(wts[0:L, :, 0], sc(9))
        dve.drain()
        tt(wts[0:L, :, 1], wts[0:L, :, 0], sc(6), ALU.mult)
        dve.wait_ge(N["rk_mm"], 1)
        v.tensor_copy(r_rk[0:L].rearrange("p n e -> p (n e)"), ps[2][0:L, 0:NT * NE])
        v.tensor_copy(r_cnt[:], ps[3][:, 0:NE])
        dve.drain()
        for k in range(2):
            tt(r_pr[0:L, k * NT:(k + 1) * NT, :], r_oh[0:L, k * NT:(k + 1) * NT, :], r_rk[0:L], ALU.mult)
        tt(r_ex8[:], r_cnt[:].unsqueeze(2).to_broadcast([P, NE, 8]), r_thr[:].unsqueeze(1).to_broadcast([P, NE, 8]), ALU.is_gt)
        dve.drain()
        red(r_kn[0:L, 3, :], r_pr[0:L], ALU.add)
        red(r_ex[:, 0, :], r_ex8[:], ALU.add)
        dve.drain()
        v.tensor_tensor_scan(r_ex[:, 1, :], r_ex[:, 0, :], r_ex[:, 0, :], 0.0, ALU.add, ALU.max)
        tt(r_c8[0:L], over_last(r_kn[0:L, 3, :], 8), r_thr[0:L].unsqueeze(1).to_broadcast([L, KN, 8]), ALU.is_ge)
        dve.drain()
        tt(r_ex[:, 2, :], r_ex[:, 1, :], r_ex[:, 0, :], ALU.subtract)
        red(r_kn[0:L, 4, :], r_c8[0:L], ALU.add)
        dve.drain()
        tt(r_pr[0:L], r_oh[0:L], over_mid(r_ex[0:L, 2, :], KN), ALU.mult)
        stt(r_kn[0:L, 5, :], r_kn[0:L, 4, :], -float(P), r_kn[0:L, 3, :], ALU.mult, ALU.add)
        for k in range(2):
            stt(r_kn[0:L, 6, k * NT:(k + 1) * NT], sc(1), float(PER_GROUP), sc(7 + k), ALU.mult, ALU.add)
        dve.drain()
        red(r_kn[0:L, 7, :], r_pr[0:L], ALU.add)
        ts(r_kn[0:L, 8, :], r_kn[0:L, 4, :], 1.0, None, ALU.min)
        dve.drain()
        tt(r_kn[0:L, 9, :], r_kn[0:L, 4, :], r_kn[0:L, 7, :], ALU.add)
        dve.drain()
        stt(r_kn[0:L, 9, :], r_kn[0:L, 9, :], float(NE - 1), r_kn[0:L, 6, :], ALU.add, ALU.subtract)
        dve.drain()
        tt(r_kn[0:L, 9, :], r_kn[0:L, 9, :], r_kn[0:L, 8, :], ALU.mult)
        dve.drain()
        tt(r_kn[0:L, 9, :], r_kn[0:L, 9, :], r_kn[0:L, 6, :], ALU.add)
        dve.drain()
        tt(r_eq[0:L], over_mid(r_iota[0:L, 0:ITEMS], KN), over_last(r_kn[0:L, 9, :], ITEMS), ALU.is_equal).then_inc(N["r_item"], 1)
        tt(r_ohr[0:L], over_mid(r_iota[0:L, :], KN), over_last(r_kn[0:L, 5, :], P), ALU.is_equal)
        dve.wait_ge(N["r_item"], 1)
        tt(r_rhs[0:L, 1], r_eq[0:L], over_last(r_val[0:L, 1, :], ITEMS), ALU.mult).then_inc(N["r_rhs_done"], 1)
        tt(r_cmp[:], r_iota[0:1, 0:EXTRA].unsqueeze(2).to_broadcast([1, EXTRA, NE]), over_mid(r_ex[0:1, 1, :], EXTRA), ALU.is_ge)
        v.tensor_copy(r_e[:, 0, 0:NE], r_iota[0:1, 0:NE])
        ts(r_e[:, 2, 0:1], r_ex[0:1, 1, NE - 1:NE], float(NE - 1), None, ALU.add)
        dve.drain()
        red(r_e[:, 1, 0:EXTRA], r_cmp[:], ALU.add)
        v.tensor_copy(npm1[:, 1:2], r_e[:, 2, 0:1])
        dve.drain()
        ts(r_e[:, 0, NE:], r_e[:, 1, 0:EXTRA], float(NE - 1), None, ALU.min)
        ts(npm1[:, 0:1], npm1[:, 1:2], 1, None, ALU.arith_shift_right)
        dve.drain()
        v.tensor_copy(eidx[:], r_e[:, 0, :])
        ts(npm1[:, 2:3], npm1[:, 0:1], -1.0, None, ALU.add)
        dve.wait_ge(N["v_mm"], 1)
        ts(r_v[:, 0, :], ps[2][:, 0:ITEMS], 0.5, 1e6, ALU.is_lt, ALU.mult)
        dve.drain()
        stt(r_v[:, 1, :], ps[2][:, 0:ITEMS], -1.0, r_v[:, 0, :], ALU.add, ALU.add)
        dve.drain()
        v.tensor_copy(dstrow[:], r_v[:, 1, :])
        dve.drain()
        ts(tokrow[:], dstrow[:], 1, None, ALU.arith_shift_right).then_inc(N["routed"], 1)

        def xg_lo(j, b):
            for q in range(2):
                wait(dve, N["xg_hi"], j * 2 + (q + 1))
                s = slice(4 * q, 4 * q + 4)
                tt(xglo[b][:, s, :].rearrange("p k t -> p (k t)"), ps[q][:], xghi[b][:, s, :].rearrange("p k t -> p (k t)").bitcast(F32), ALU.subtract).then_inc(N["xg_lo"], 1)

        def times_up(j):
            wait(dve, N["silu_done"], j + 1)
            wait(dve, N["u2_mm"], j + 1)
            tt(gu[:], sg[:], ps[3][:], ALU.mult).then_inc(N["gu_done"], 1)

        def hidden_lo(j):
            wait(dve, N["g_hi"], j + 1)
            tt(glo[:].rearrange("p k t -> p (k t)"), ps[4][:], ghi[:].rearrange("p k t -> p (k t)").bitcast(F32), ALU.subtract).then_inc(N["g_lo"], 1)

        xg_lo(0, 0)
        xg_lo(1, 1)
        lo_expert(1, 0)
        lo_expert(0, 2)
        pairs_m1 = dve.value_load(npm1[0:1, 0:1], min_val=NE // 2 - 1, max_val=ITEMS // 2 - 1)

        def item(j, b, ahead=2):
            times_up(j)
            if ahead:
                lo_expert(j + 1, 1)
            hidden_lo(j)
            if ahead == 2:
                xg_lo(j + 2, b)
                lo_expert(j + 2, 0)
            if ahead:
                lo_expert(j + 1, 2, final=ahead == 1)

        item(0, 0)
        item(1, 1)
        with dve.Fori(1, pairs_m1) as i:
            item(i * 2, 0)
            item(i * 2 + 1, 1)
        item(pairs_m1 * 2, 0, ahead=1)
        item(pairs_m1 * 2 + 1, 1, ahead=0)

        dve.wait_ge(N["wts_in"], 16)
        for n in range(NF):
            b = n % FB
            f = fmv[b]
            dve.wait_ge(N["y0_done"], n + 1)
            dve.wait_ge(y_landed[b], 16 * (n // FB + 1))
            stt(zz[b][:], yy[b][:, 0, :], wts2[:, n, 0:1], zz[b][:], ALU.mult, ALU.add)
            dve.drain()
            stt(zz[b][:], yy[b][:, 1, :], wts2[:, n, 1:2], zz[b][:], ALU.mult, ALU.add).then_inc(N["fsum_done"], 1)
            dve.drain()
            for q in range(2):
                v.bn_stats(fst[:, q, :], zz[b][:, q * 512:(q + 1) * 512])
            dve.drain()
            wait(dve, N["fnorm_done"], n - FB + 1)
            v.bn_aggr(f[:, 0:2], fst[:].rearrange("p a b -> p (a b)"))
            dve.drain()
            rsqrt_column(f[:, 2:3], f[:, 1:2], f[:, 3:4])
            stt(f[:, 3:4], f[:, 0:1], -1.0, f[:, 2:3], ALU.mult, ALU.mult).then_inc(N["fstat_done"], 1)

    @block.tensor
    def _(pe):
        t = nc.tensor

        def mm3(out, lh, ll, rh, rl, first, last):
            t.matmul(out, lh, rh, start=first, stop=False)
            t.matmul(out, lh, rl, start=False, stop=False)
            return t.matmul(out, ll, rh, start=False, stop=last)

        pe.wait_ge(N["consts"], 1)
        def x_T(n):
            pe.wait_ge(xt_landed[n % 2], 32 * (n // 2 + 1))
            xv = xt[n % 2][:].rearrange("p (m k) -> p k m", k=KC)
            for half in range(2):
                q = 2 * n + half
                wait(pe, N["x_lo"], q - 3)
                for k in range(4):
                    last = t.transpose(ps[4 + q % 4][:, k * L:(k + 1) * L], xv[0:L, 4 * half + k, :], ident[0:L, 0:L])
                last.then_inc(N["xT_mm"], 1)

        def project(u, n, s, slot):
            wh = whi[slot][:].rearrange("p (k n) -> p k n", k=KC)
            wl = wlo[slot][:].rearrange("p (k n) -> p k n", k=KC)
            wait(pe, N["bank_free"], u + 1)
            c = slice(n * L, (n + 1) * L)
            for k in range(KC):
                last = mm3(ps[s][0:L, :], xhi[:, k, c], xlo[:, k, c], wh[:, k, :], wl[:, k, :], k == 0, k == KC - 1)
            last.then_inc(N["blk_mm"], 1)

        def gates(n):
            c = slice(n * L, (n + 1) * L)
            for k in range(KC):
                last = mm3(ps[3][0:L, n * 8:(n + 1) * 8], xhi[:, k, c], xlo[:, k, c], wg_hi[:, k, :], wg_lo[:, k, :], k == 0, k == KC - 1)
            if n == NT - 1:
                last.then_inc(N["gate_mm"], 1)

        x_T(0)
        x_T(1)
        for n in range(NT):
            pe.wait_ge(N["x_lo"], 2 * n + 2)
            if n == 0:
                pe.wait_ge(N["lo_done"], 2)
            project(n, n, n % 3, 0)
            if n == 0:
                pe.wait_ge(N["gate_mm"], 1)
            gates(n)
            if n + 2 < NT:
                x_T(n + 2)
        with pe.Fori(0, 2) as i:
            for pos in range(2 * NT):
                if pos % NT == 0:
                    wait(pe, N["lo_done"], i * 4 + 2 * (2 + pos // NT))
                project(i * 18 + (NT + pos), pos % NT, pos % 3, 1 - pos // NT)

        def sums_of_log_f():
            pe.wait_ge(N["a_rows"], 1)
            t.matmul(ps[6][0:L, 0:NT * H], upto[0:L, :], glf[0:L].rearrange("p n h -> p (n h)"), start=True, stop=True).then_inc(N["b_mm"], 1)

        def a_by_head_0():
            pe.wait_ge(N["a_rows"], 2)
            for n in range(8):
                last = t.transpose(ps[6 + n // 4][0:H, (n % 4) * L:(n % 4 + 1) * L], ga[0:L, n, :], ident[0:L, 0:L])
            last.then_inc(N["aT_mm"], 1)

        def a_by_head_1():
            pe.wait_ge(N["aT_mm"], 2)
            t.transpose(ps[6][0:H, 0:L], ga[0:L, 8, :], ident[0:L, 0:L])
            for n in range(NT):
                last = t.matmul(ps[6][0:H, 480 + n:481 + n], glf[0:L, n, :], ones[0:L, 0:1], start=True, stop=True)
            last.then_inc(N["aT_mm"], 1)

        def maxima():
            pe.wait_ge(N["m_rows"], 1)
            for n in range(NT):
                t.transpose(ps[6][0:L, n * H:(n + 1) * H], cm[:, n, :], ident[0:H, 0:H])
            for h in range(H):
                last = t.matmul(ps[7][:, h * 2 * NT:(h + 1) * 2 * NT], selpos[:, h, :], mcl[:], start=True, stop=True)
            last.then_inc(N["mb_mm"], 1)

        pe.wait_ge(N["lo_done"], 12)
        between = {0: sums_of_log_f, 1: a_by_head_0, 2: a_by_head_1, 6: maxima}
        for n in range(NT):
            if n in between:
                between[n]()
            project(5 * NT + n, n, n % 3, 1)

        def transposes(c):
            wait(pe, N["qk_in"], c * 32 + 32)
            wait(pe, N["sw_done"], c)
            wait(pe, N["num_done"], c * 4)
            for h in range(H):
                last = t.transpose(ps[4][:, h * L:(h + 1) * L], qk[0:L, 0, h, :], ident[0:L, 0:L])
            last.then_inc(N["t_mm"], 1)
            for h in range(H):
                last = t.transpose(ps[5][:, h * L:(h + 1) * L], qk[0:L, 1, h, :], ident[0:L, 0:L])
            last.then_inc(N["t_mm"], 1)
            wait(pe, N["qs_done"], c * 2 + 1)
            for h in range(H):
                last = t.transpose(ps[6][:, h * L:(h + 1) * L], qs[0:L, h, :], ident[0:L, 0:L])
            last.then_inc(N["t_mm"], 1)

        def scores(c):
            wait(pe, N["c_done"], c * 4 + 1)
            for h in range(H):
                rhs = cm[:, c, :] if isinstance(c, int) else cm[:, bass.ds(c, 1), :].rearrange("p n t -> p (n t)")
                out_h = ps[7][0:L, h * L:(h + 1) * L]
                t.matmul(out_h, identb[0:L, :], maskb[0:L, :], start=True, stop=False)
                last = t.matmul(out_h, selneg[:, h, 0:L], rhs, start=False, stop=True)
            last.then_inc(N["e_mm"], 1)
            wait(pe, N["t_cp"], c * 3 + 2)
            for h in range(H):
                last = t.matmul(ps[4][0:L, h * L:(h + 1) * L], kT[:, h * L:(h + 1) * L], qT[:, h * L:(h + 1) * L], start=True, stop=True)
            last.then_inc(N["s_mm"], 1)

        def attend(c):
            wait(pe, N["sw_done"], c + 1)
            wait(pe, N["t_cp"], c * 3 + 3)
            wait(pe, N["v_in"], c * 32 + 32)
            wait(pe, N["qs_done"], c * 2 + 2)
            wait(pe, N["o_lo"], c * 2)
            if isinstance(c, int) and c == 0:
                pe.wait_ge(N["ones_ready"], 1)
            for h in range(H):
                wait(pe, N["num_done"], c * 4 + (h - 1))
                t.matmul(ps[5 + h % 2][0:L, 0:DV + 1], sw[0:L, h * L:(h + 1) * L], vext[0:L, h, :], start=True, stop=False)
                t.matmul(ps[5 + h % 2][0:L, 0:DV + 1], qsT[:, h * L:(h + 1) * L], cst[:, h, :], start=False, stop=True).then_inc(N["n_mm"], 1)
                wait(pe, N["c_done"], c * 4 + h)
                t.matmul(ps[(7, 0)[h % 2]][:, 0:DV + 1], ks[0:L, h, :], vext[0:L, h, :], start=True, stop=True).then_inc(N["u_mm"], 1)

        def gated_T(c):
            wait(pe, N["gated_done"], c + 1)
            wait(pe, N["c_done"], c * 4 + 5)
            wait(pe, N["lg_done"], c - 2)
            gv = gated[:].rearrange("p h d -> p (h d)").rearrange("p (m k) -> p k m", k=KC)
            for q in range(2):
                for k in range(4):
                    last = t.transpose(ps[q][:, k * L:(k + 1) * L], gv[0:L, 4 * q + k, :], ident[0:L, 0:L])
                last.then_inc(N["ot_mm"], 1)

        def h1_T(c, i):
            if is_tile(i):
                wait(pe, N["t_cp"], i * 3 + 3)
            else:
                wait(pe, N["num_done"], 4 * NT)
                wait(pe, N["ht_cp"], c * 2)
            wait(pe, N["h1_done"], c + 1)
            hv = h1t[:].rearrange("p (m k) -> p k m", k=KC)
            for q in range(2):
                for k in range(4):
                    last = t.transpose(ps[5 + q][:, k * L:(k + 1) * L], hv[0:L, 4 * q + k, :], ident[0:L, 0:L])
                last.then_inc(N["ht_mm"], 1)

        def logits(c):
            wait(pe, N["ht_cp"], c * 2 + 2)
            wait(pe, N["lg_done"], c)
            for k in range(KC):
                last = t.matmul(ps[1][0:L, 0:GROUPS + NE], h1T[:, k, :], wgr[:, k, :], start=k == 0, stop=k == KC - 1)
            last.then_inc(N["lg_mm"], 1)

        def out_half(c, q):
            wait(pe, N["o_lo"], c * 2 + 2)
            wait(pe, N["z_done"], c * 2 + q - 1)
            wh = whi[q][:].rearrange("p (k n) -> p k n", k=KC)
            wl = wlo[q][:].rearrange("p (k n) -> p k n", k=KC)
            for k in range(KC):
                last = mm3(ps[2 + q][0:L, :], ohi[:, k, :], olo[:, k, :], wh[:, k, :], wl[:, k, :], k == 0, k == KC - 1)
            last.then_inc(N["y_mm"], 1)

        pe.wait_ge(N["bank_free"], 3 + 6 * NT)
        pe.wait_ge(N["gate_exp"], 1)
        def body(i):
            if is_tile(i):
                transposes(i)
                scores(i)
            if is_tile(i - 4):
                h1_T(i - 4, i)
            if is_tile(i - 2):
                out_half(i - 2, 0)
            if is_tile(i - 4):
                logits(i - 4)
            if is_tile(i - 2):
                out_half(i - 2, 1)
            if is_tile(i - 1):
                gated_T(i - 1)
            if is_tile(i):
                attend(i)

        body(0)
        body(1)
        pe.wait_ge(N["lo_done"], 2 * G0)
        pe.wait_ge(N["params"], 16 * 9)
        for i in range(2, 5):
            body(i)
        with pe.Fori(5, NT) as i:
            body(i)
        for i in range(NT, NT + 4):
            body(i)

        pe.wait_ge(N["r_hot"], 1)
        t.matmul(ps[2][0:L, 0:NT * NE], beforeb[0:L, :], r_a[0:L, 0:NT, :].rearrange("p n e -> p (n e)"), start=True, stop=False)
        t.matmul(ps[2][0:L, 0:NT * NE], onesb[0:L, 0:L], r_acum[0:L, 0:NT, :].rearrange("p n e -> p (n e)"), start=False, stop=True)
        t.matmul(ps[3][:, 0:NE], onesb[0:L, :], r_acum[0:L, NT, :], start=True, stop=True).then_inc(N["rk_mm"], 1)
        pe.wait_ge(N["r_rhs_done"], 2)
        for part in range(2):
            for q in range(2 * NT):
                last = t.matmul(ps[2][:, 0:ITEMS], r_ohr[0:L, q, :], r_rhs[0:L, part, q, :],
                                start=part == 0 and q == 0, stop=part == 1 and q == 2 * NT - 1)
        last.then_inc(N["v_mm"], 1)

        def rows_T(j, b):
            wait(pe, gathered[b], (j - b) * 8 + 16)
            wait(pe, N["xg_lo"], j * 2)
            xv = xg[b][:].rearrange("p (m k) -> p k m", k=KC)
            for q in range(2):
                for k in range(4):
                    last = t.transpose(ps[q][:, k * P:(k + 1) * P], xv[:, 4 * q + k, :], ident[:])
                last.then_inc(N["xgT_mm"], 1)

        def up_or_gate(j, b, k, bank):
            wait(pe, N["lo_done"], split_count(j, k))
            wh = whi[k][:].rearrange("p (k n) -> p k n", k=KC)
            wl = wlo[k][:].rearrange("p (k n) -> p k n", k=KC)
            for kk in range(KC):
                last = mm3(ps[bank][:], xghi[b][:, kk, :], xglo[b][:, kk, :], wh[:, kk, :], wl[:, kk, :], kk == 0, kk == KC - 1)
            return last

        def gate(j, b):
            wait(pe, N["xg_lo"], j * 2 + 2)
            wait(pe, N["silu_done"], j)
            up_or_gate(j, b, 0, 2).then_inc(N["g_mm"], 1)

        def up(j, b):
            wait(pe, N["gu_done"], j)
            up_or_gate(j, b, 1, 3).then_inc(N["u2_mm"], 1)

        def hidden_T(j):
            wait(pe, N["gu_done"], j + 1)
            wait(pe, N["g_lo"], j)
            gv = gu[:].rearrange("p (m k) -> p k m", k=FC)
            for k in range(FC):
                last = t.transpose(ps[4][:, k * P:(k + 1) * P], gv[:, k, :], ident[:])
            last.then_inc(N["guT_mm"], 1)

        def down(j, final):
            wait(pe, N["lo_done"], split_count(j, 2, final))
            wait(pe, N["g_lo"], j + 1)
            wait(pe, N["y_cp"], j * 2)
            wh = whi[2][:].rearrange("p (k n) -> p k n", k=FC)
            wl = wlo[2][:].rearrange("p (k n) -> p k n", k=FC)
            for q in range(2):
                c = slice(q * 512, (q + 1) * 512)
                for k in range(FC):
                    last = mm3(ps[5 + q][:], ghi[:, k, :], glo[:, k, :], wh[:, k, c], wl[:, k, c], k == 0, k == FC - 1)
                last.then_inc(N["y2_mm"], 1)

        def item(j, b, ahead=2):
            up(j, b)
            if ahead:
                gate(j + 1, 1 - b)
            hidden_T(j)
            if ahead == 2:
                rows_T(j + 2, b)
            down(j, final=not ahead)

        pe.wait_ge(N["routed"], 1)
        rows_T(0, 0)
        pairs_m1 = pe.value_load(npm1[0:1, 0:1], min_val=NE // 2 - 1, max_val=ITEMS // 2 - 1)
        gate(0, 0)
        rows_T(1, 1)
        item(0, 0)
        item(1, 1)
        with pe.Fori(1, pairs_m1) as i:
            item(i * 2, 0)
            item(i * 2 + 1, 1)
        item(pairs_m1 * 2, 0, ahead=1)
        item(pairs_m1 * 2 + 1, 1, ahead=0)

    block.__exit__(None, None, None)
    dma_ok.__exit__(None, None, None)


_INS = ["w_in", "b_gates", "head_norm_w", "w_out", "ln1_g", "ln1_b", "w_group", "b_group", "w_router",
        "b_router", "w_gate", "w_up", "w_down", "ln2_g", "ln2_b"]


def kernel(x, meta_tokens, **params):
    import numpy as np
    import concourse.bacc as bacc
    from concourse.bass_utils import run_bass_kernel_spmd

    nc = bacc.Bacc("TRN2", target_bir_lowering=False, num_devices=1)
    x = np.asarray(x)
    rows = np.concatenate([np.asarray(meta_tokens), x[0], np.zeros((TP - T, D), x.dtype)])
    arrays = {"hcat": rows}
    args = [nc.dram_tensor("hcat", rows.shape, F32, kind="ExternalInput").ap()]
    for name in _INS:
        arrays["l0_" + name] = np.ascontiguousarray(params["l0_" + name])
        args.append(nc.dram_tensor("l0_" + name, arrays["l0_" + name].shape, F32, kind="ExternalInput").ap())
    out = nc.dram_tensor("out", (OUT_ROWS, D), F32, kind="ExternalOutput").ap()
    build(nc, *args, out)
    r = run_bass_kernel_spmd(nc, [arrays], core_ids=[0])
    return r.results[0]["out"].reshape(1, OUT_ROWS, D)
```
